# Optimizing a Trainium2 kernel written in Bass

```python
import jax, jax.numpy as jnp
from jax import lax
import numpy as np

D_MODEL = 1024
BATCH = 1
SEQ = 256
DEPTH = 1
DEC_BATCH = 8
DEC_SEQ = 1
PAST_LEN = 2048
PAGE_SIZE = 128

N_MEM = 256
SB_HEADS = 8
SB_HEAD_DIM = 64
SB_WIDTH = SB_HEADS * SB_HEAD_DIM
SB_BLOCK = 128
SB_SCALE = SB_HEAD_DIM ** -0.5
SB_BIAS_INIT = -6.0
MEM_HEADS = 4
MEM_HEAD_DIM = 128
MEM_WIDTH = MEM_HEADS * MEM_HEAD_DIM
MEM_SCALE = MEM_HEAD_DIM ** -0.5
RW_HEADS = 8
RW_HEAD_DIM = 64
RW_WIDTH = RW_HEADS * RW_HEAD_DIM
DECAY_LORA = 64
AAA_LORA = 64
GATE_LORA = 128
RW_SPLITS = (RW_WIDTH, RW_WIDTH, RW_WIDTH, DECAY_LORA, AAA_LORA, GATE_LORA)
RW_SHIFT_WIDTH = sum(RW_SPLITS)
RW_GN_EPS = 64e-5
N_EXPERTS = 32
TOP_K = 4
D_FF = D_MODEL
SWIGLU_ALPHA = 1.702
SWIGLU_LIMIT = 7.0
MOE_BLOCK = 128
DN_ALPHA = (2 * DEPTH) ** 0.25
DN_BETA = (8 * DEPTH) ** -0.25
LN_EPS = 1e-5
IN_SPLITS = (SB_WIDTH, SB_WIDTH, SB_WIDTH, MEM_WIDTH, RW_SHIFT_WIDTH, D_MODEL, D_MODEL, D_MODEL)
IN_WIDTH = sum(IN_SPLITS)

kernel_name = 'stickbreak_rwkv7_memxattn_moe_deepnorm_step'

def _split(x, sizes):
    return jnp.split(x, np.cumsum(sizes)[:-1].tolist(), axis=-1)

def _layer_norm(x, g, b):
    xf = x.astype(jnp.float32)
    mu = xf.mean(-1, keepdims=True)
    var = jnp.square(xf - mu).mean(-1, keepdims=True)
    return ((xf - mu) * lax.rsqrt(var + LN_EPS) * g + b).astype(x.dtype)

def _sb_logits(q, k, bias):
    z = jnp.einsum('bqhd,bkhd->bhqk', q, k, preferred_element_type=jnp.float32) * SB_SCALE
    return z + bias.astype(jnp.float32)[None, :, None, None]

def _sb_weights(z, causal):
    log_keep = jnp.where(causal, jax.nn.log_sigmoid(-z), 0.0)
    log_survive = lax.cumsum(log_keep, axis=z.ndim - 1, reverse=True) - log_keep
    return jnp.where(causal, jnp.exp(jax.nn.log_sigmoid(z) + log_survive), 0.0)

def _sb_prompt(q, k, v, bias):
    b, s = q.shape[:2]
    n_blk = s // SB_BLOCK
    q_blocks = jnp.moveaxis(q.reshape(b, n_blk, SB_BLOCK, SB_HEADS, SB_HEAD_DIM), 1, 0)
    k_pos = jnp.arange(s)

    def one_block(args):
        q_blk, blk = args
        q_pos = blk * SB_BLOCK + jnp.arange(SB_BLOCK)
        w = _sb_weights(_sb_logits(q_blk, k, bias), k_pos[None, :] < q_pos[:, None])
        return jnp.einsum('bhqk,bkhd->bqhd', w.astype(v.dtype), v)

    o = lax.map(one_block, (q_blocks, jnp.arange(n_blk)))
    return jnp.moveaxis(o, 0, 1).reshape(b, s, SB_WIDTH)

def _sb_sample(q, k_new, v_new, bias, k_pool, v_pool, layer, page_table):
    b, s = q.shape[:2]
    past = page_table.shape[1] * PAGE_SIZE
    k_past = k_pool[layer][page_table].reshape(b, past, SB_HEADS, SB_HEAD_DIM)
    v_past = v_pool[layer][page_table].reshape(b, past, SB_HEADS, SB_HEAD_DIM)
    z = jnp.concatenate([_sb_logits(q, k_past, bias), _sb_logits(q, k_new, bias)], axis=-1)
    q_pos = past + jnp.arange(s)
    k_pos = jnp.arange(past + s)
    w = _sb_weights(z, k_pos[None, :] < q_pos[:, None])
    o = (jnp.einsum('bhqk,bkhd->bqhd', w[..., :past].astype(v_past.dtype), v_past)
         + jnp.einsum('bhqk,bkhd->bqhd', w[..., past:].astype(v_new.dtype), v_new))
    return o.reshape(b, s, SB_WIDTH).astype(q.dtype)

def _mem_attend(q, mem_k, mem_v):
    s = jnp.einsum('bshd,bmhd->bhsm', q, mem_k, preferred_element_type=jnp.float32) * MEM_SCALE
    p = jax.nn.softmax(s, axis=-1)
    return jnp.einsum('bhsm,bmhd->bshd', p.astype(mem_v.dtype), mem_v)

def _rwkv7(p_rw, shift0, wkv0, mu_rw, w_decay0, w_decay2, w_aaa0, w_aaa2, w_gate2,
           rw_k_k, rw_k_a, rw_r_k, rw_gn_g, rw_gn_b):
    f32 = jnp.float32
    b, s, _ = p_rw.shape
    prev = jnp.concatenate([shift0[:, None, :].astype(p_rw.dtype), p_rw[:, :-1]], axis=1)
    xs = p_rw + mu_rw * (prev - p_rw)
    r, k, v, w_lo, a_lo, g_lo = _split(xs, RW_SPLITS)
    w_raw = (w_decay0 + jnp.tanh(w_lo) @ w_decay2).astype(f32)
    decay = jnp.exp(-jnp.exp(-jax.nn.softplus(-w_raw) - 0.5))
    a = jax.nn.sigmoid((w_aaa0 + a_lo @ w_aaa2).astype(f32))
    g = jax.nn.sigmoid(g_lo) @ w_gate2
    heads = lambda t: t.reshape(b, s, RW_HEADS, RW_HEAD_DIM)
    kk = heads(k.astype(f32) * rw_k_k)
    kk = kk / jnp.maximum(jnp.sqrt(jnp.sum(kk * kk, axis=-1, keepdims=True)), 1e-12)
    k_mod = k.astype(f32) * (1.0 + (a - 1.0) * rw_k_a)
    rh, kh, vh, ah, dh = heads(r.astype(f32)), heads(k_mod), heads(v.astype(f32)), heads(a), heads(decay)

    def step(state, inp):
        r_t, d_t, k_t, v_t, kk_t, a_t = inp
        s_a = jnp.einsum('bhvk,bhk->bhv', state, -kk_t)
        state = (state * d_t[:, :, None, :] + s_a[..., None] * (kk_t * a_t)[:, :, None, :]
                 + v_t[..., None] * k_t[:, :, None, :])
        return state, jnp.einsum('bhvk,bhk->bhv', state, r_t)

    seq_first = lambda t: jnp.moveaxis(t, 1, 0)
    wkv, y = lax.scan(step, wkv0.astype(f32), (seq_first(rh), seq_first(dh), seq_first(kh),
                                               seq_first(vh), seq_first(kk), seq_first(ah)))
    y = jnp.moveaxis(y, 0, 1)
    mu = y.mean(-1, keepdims=True)
    var = jnp.square(y - mu).mean(-1, keepdims=True)
    y = ((y - mu) * lax.rsqrt(var + RW_GN_EPS)).reshape(b, s, RW_WIDTH) * rw_gn_g + rw_gn_b
    bonus = jnp.sum(rh * kh * rw_r_k, axis=-1, keepdims=True) * vh
    y = (y + bonus.reshape(b, s, RW_WIDTH)) * g
    return y.astype(p_rw.dtype), p_rw[:, -1], wkv

def _moe(x, w_router, b_router, w_gate_up, b_gate_up, w_down, b_down):
    lead = x.shape[:-1]
    xf = x.reshape(-1, D_MODEL)
    t = xf.shape[0]
    logits = jnp.dot(xf, w_router, preferred_element_type=jnp.float32) + b_router
    top_logit, top_e = lax.top_k(logits, TOP_K)
    top_p = jax.nn.softmax(top_logit, axis=-1)
    n_pairs = t * TOP_K
    n_blocks = -(-n_pairs // MOE_BLOCK) + N_EXPERTS
    pair_e = top_e.reshape(-1)
    order = jnp.argsort(pair_e)
    sorted_e = pair_e[order]
    sorted_tok = order // TOP_K
    counts = jnp.bincount(pair_e, length=N_EXPERTS)
    padded = (counts + MOE_BLOCK - 1) // MOE_BLOCK * MOE_BLOCK
    pad_end = jnp.cumsum(padded)
    rank = jnp.arange(n_pairs) - (jnp.cumsum(counts) - counts)[sorted_e]
    dest = (pad_end - padded)[sorted_e] + rank
    row_tok = jnp.zeros((n_blocks * MOE_BLOCK,), jnp.int32).at[dest].set(sorted_tok)
    row_w = jnp.zeros((n_blocks * MOE_BLOCK,), jnp.float32).at[dest].set(top_p.reshape(-1)[order])
    block_e = jnp.minimum(jnp.searchsorted(pad_end, jnp.arange(n_blocks) * MOE_BLOCK, side='right'),
                          N_EXPERTS - 1)
    xb = xf[row_tok].reshape(n_blocks, MOE_BLOCK, D_MODEL)

    def expert_block(args):
        xe, e = args
        gu = xe @ w_gate_up[e] + b_gate_up[e]
        glu = jnp.minimum(gu[:, ::2], SWIGLU_LIMIT)
        lin = jnp.clip(gu[:, 1::2], -SWIGLU_LIMIT, SWIGLU_LIMIT)
        h = glu * jax.nn.sigmoid(SWIGLU_ALPHA * glu) * (lin + 1.0)
        return h @ w_down[e] + b_down[e]

    yb = lax.map(expert_block, (xb, block_e)).reshape(-1, D_MODEL)
    y = jnp.zeros((t, D_MODEL), jnp.float32).at[row_tok].add(yb.astype(jnp.float32) * row_w[:, None])
    return y.astype(x.dtype).reshape(*lead, D_MODEL)

def _layer(x, sb_mix, mem_k, mem_v, shift0, wkv0, w_in, sb_bias, mu_rw, w_decay0, w_decay2, w_aaa0,
           w_aaa2, w_gate2, rw_k_k, rw_k_a, rw_r_k, rw_gn_g, rw_gn_b, w_sb_o, w_mem_o, w_rw_o, w_out,
           ln1_g, ln1_b, w_router, b_router, w_gate_up, b_gate_up, w_down, b_down, ln2_g, ln2_b):
    b, s, _ = x.shape
    q_sb, k_sb, v_sb, q_mem, p_rw, g_sb, g_mem, g_rw = _split(x @ w_in, IN_SPLITS)
    sb_heads = lambda t: t.reshape(b, s, SB_HEADS, SB_HEAD_DIM)
    k_sb, v_sb = sb_heads(k_sb), sb_heads(v_sb)
    o_sb = sb_mix(sb_heads(q_sb), k_sb, v_sb, sb_bias)
    o_mem = _mem_attend(q_mem.reshape(b, s, MEM_HEADS, MEM_HEAD_DIM), mem_k, mem_v).reshape(b, s, MEM_WIDTH)
    o_rw, shift, wkv = _rwkv7(p_rw, shift0, wkv0, mu_rw, w_decay0, w_decay2, w_aaa0, w_aaa2, w_gate2,
                              rw_k_k, rw_k_a, rw_r_k, rw_gn_g, rw_gn_b)
    merged = (jax.nn.sigmoid(g_sb) * (o_sb @ w_sb_o) + jax.nn.sigmoid(g_mem) * (o_mem @ w_mem_o)
              + jax.nn.sigmoid(g_rw) * (o_rw @ w_rw_o))
    h = _layer_norm(DN_ALPHA * x + merged @ w_out, ln1_g, ln1_b)
    y = _layer_norm(DN_ALPHA * h + _moe(h, w_router, b_router, w_gate_up, b_gate_up, w_down, b_down),
                    ln2_g, ln2_b)
    return y, k_sb, v_sb, shift, wkv

def setup_inputs(seed: int = 0) -> dict:
    key = jax.random.key(seed)
    keys = iter(jax.random.split(key, 48))

    def nrm(shape, scale):
        return scale * jax.random.normal(next(keys), shape, jnp.float32)

    n_pages = PAST_LEN // PAGE_SIZE
    n_used = DEC_BATCH * n_pages
    n_pool = n_used + max(n_used // 4, 1)
    page_table = jax.random.permutation(next(keys), n_pool)[:n_used].reshape(DEC_BATCH, n_pages).astype(jnp.int32)
    L = DEPTH
    decay_base = jnp.linspace(-6.0, -1.0, RW_WIDTH, dtype=jnp.float32)
    return {
        'x_prompt': nrm((BATCH, SEQ, D_MODEL), 1.0),
        'x_sample': nrm((DEC_BATCH, DEC_SEQ, D_MODEL), 1.0),
        'cache_sb_k': nrm((L, n_pool, PAGE_SIZE, SB_HEADS, SB_HEAD_DIM), 1.0),
        'cache_sb_v': nrm((L, n_pool, PAGE_SIZE, SB_HEADS, SB_HEAD_DIM), 1.0),
        'cache_mem_k': nrm((L, DEC_BATCH, N_MEM, MEM_HEADS, MEM_HEAD_DIM), 1.0),
        'cache_mem_v': nrm((L, DEC_BATCH, N_MEM, MEM_HEADS, MEM_HEAD_DIM), 1.0),
        'state_rw_shift': nrm((L, DEC_BATCH, RW_SHIFT_WIDTH), 1.0),
        'state_rw_wkv': nrm((L, DEC_BATCH, RW_HEADS, RW_HEAD_DIM, RW_HEAD_DIM), 1.0),
        'page_table': page_table,
        'mem_prompt': nrm((BATCH, N_MEM, D_MODEL), 1.0),
        'w_in': nrm((L, D_MODEL, IN_WIDTH), D_MODEL ** -0.5),
        'sb_bias': SB_BIAS_INIT + nrm((L, SB_HEADS), 0.1),
        'mu_rw': jax.random.uniform(next(keys), (L, RW_SHIFT_WIDTH), jnp.float32),
        'w_decay0': decay_base + nrm((L, RW_WIDTH), 0.1),
        'w_decay2': nrm((L, DECAY_LORA, RW_WIDTH), 0.1 * DECAY_LORA ** -0.5),
        'w_aaa0': nrm((L, RW_WIDTH), 0.5),
        'w_aaa2': nrm((L, AAA_LORA, RW_WIDTH), AAA_LORA ** -0.5),
        'w_gate2': nrm((L, GATE_LORA, RW_WIDTH), GATE_LORA ** -0.5),
        'rw_k_k': 0.85 + nrm((L, RW_WIDTH), 0.05),
        'rw_k_a': 1.0 + nrm((L, RW_WIDTH), 0.05),
        'rw_r_k': nrm((L, RW_HEADS, RW_HEAD_DIM), 0.1),
        'rw_gn_g': 1.0 + nrm((L, RW_WIDTH), 0.02),
        'rw_gn_b': nrm((L, RW_WIDTH), 0.02),
        'w_mem_kv': nrm((L, D_MODEL, 2 * MEM_WIDTH), D_MODEL ** -0.5),
        'w_sb_o': nrm((L, SB_WIDTH, D_MODEL), SB_WIDTH ** -0.5),
        'w_mem_o': nrm((L, MEM_WIDTH, D_MODEL), MEM_WIDTH ** -0.5),
        'w_rw_o': nrm((L, RW_WIDTH, D_MODEL), RW_WIDTH ** -0.5),
        'w_out': nrm((L, D_MODEL, D_MODEL), DN_BETA * D_MODEL ** -0.5),
        'ln1_g': 1.0 + nrm((L, D_MODEL), 0.02),
        'ln1_b': nrm((L, D_MODEL), 0.02),
        'w_router': nrm((L, D_MODEL, N_EXPERTS), D_MODEL ** -0.5),
        'b_router': nrm((L, N_EXPERTS), 0.01),
        'w_gate_up': nrm((L, N_EXPERTS, D_MODEL, 2 * D_FF), D_MODEL ** -0.5),
        'b_gate_up': nrm((L, N_EXPERTS, 2 * D_FF), 0.02),
        'w_down': nrm((L, N_EXPERTS, D_FF, D_MODEL), DN_BETA * D_FF ** -0.5),
        'b_down': nrm((L, N_EXPERTS, D_MODEL), 0.02),
        'ln2_g': 1.0 + nrm((L, D_MODEL), 0.02),
        'ln2_b': nrm((L, D_MODEL), 0.02),
    }

def reference(x_prompt, x_sample, cache_sb_k, cache_sb_v, cache_mem_k, cache_mem_v, state_rw_shift,
              state_rw_wkv, page_table, mem_prompt, w_in, sb_bias, mu_rw, w_decay0, w_decay2, w_aaa0,
              w_aaa2, w_gate2, rw_k_k, rw_k_a, rw_r_k, rw_gn_g, rw_gn_b, w_mem_kv, w_sb_o, w_mem_o,
              w_rw_o, w_out, ln1_g, ln1_b, w_router, b_router, w_gate_up, b_gate_up, w_down, b_down,
              ln2_g, ln2_b):
    layer_weights = (w_in, sb_bias, mu_rw, w_decay0, w_decay2, w_aaa0, w_aaa2, w_gate2, rw_k_k, rw_k_a,
                     rw_r_k, rw_gn_g, rw_gn_b, w_sb_o, w_mem_o, w_rw_o, w_out, ln1_g, ln1_b, w_router,
                     b_router, w_gate_up, b_gate_up, w_down, b_down, ln2_g, ln2_b)
    bp = x_prompt.shape[0]
    xp, xs = x_prompt, x_sample
    kp, vp, mkp, mvp, shp, wkp, ks, vs, shs, wks = ([] for _ in range(10))
    for l in range(DEPTH):
        lw = [p[l] for p in layer_weights]
        mem_k, mem_v = _split(mem_prompt @ w_mem_kv[l], (MEM_WIDTH, MEM_WIDTH))
        mem_k = mem_k.reshape(bp, N_MEM, MEM_HEADS, MEM_HEAD_DIM)
        mem_v = mem_v.reshape(bp, N_MEM, MEM_HEADS, MEM_HEAD_DIM)
        xp, k_p, v_p, sh_p, wkv_p = _layer(
            xp, _sb_prompt, mem_k, mem_v, jnp.zeros((bp, RW_SHIFT_WIDTH), xp.dtype),
            jnp.zeros((bp, RW_HEADS, RW_HEAD_DIM, RW_HEAD_DIM), jnp.float32), *lw)
        sb_past = lambda q, k, v, bias, l=l: _sb_sample(q, k, v, bias, cache_sb_k, cache_sb_v, l, page_table)
        xs, k_s, v_s, sh_s, wkv_s = _layer(
            xs, sb_past, cache_mem_k[l], cache_mem_v[l], state_rw_shift[l], state_rw_wkv[l], *lw)
        kp.append(k_p); vp.append(v_p); mkp.append(mem_k); mvp.append(mem_v)
        shp.append(sh_p); wkp.append(wkv_p)
        ks.append(k_s); vs.append(v_s); shs.append(sh_s); wks.append(wkv_s)
    y_prompt, y_sample = xp, xs
    sb_k_prompt, sb_v_prompt = jnp.stack(kp), jnp.stack(vp)
    mem_k_prompt, mem_v_prompt = jnp.stack(mkp), jnp.stack(mvp)
    rw_shift_prompt, rw_wkv_prompt = jnp.stack(shp), jnp.stack(wkp)
    sb_k_sample, sb_v_sample = jnp.stack(ks), jnp.stack(vs)
    rw_shift_sample, rw_wkv_sample = jnp.stack(shs), jnp.stack(wks)
    return (y_prompt, y_sample, sb_k_prompt, sb_v_prompt, mem_k_prompt, mem_v_prompt,
            rw_shift_prompt, rw_wkv_prompt, sb_k_sample, sb_v_sample, rw_shift_sample, rw_wkv_sample)


_drawn_inputs = setup_inputs


def setup_inputs(seed=0):
    import zlib

    import numpy as np

    out = dict(_drawn_inputs(seed))
    spreads = {}
    factors = {'sb_bias': 8.0,
     'w_decay2': 5.724,
     'rw_gn_g': 5.437,
     'rw_gn_b': 5.273,
     'b_router': 3.728,
     'b_gate_up': 8.0,
     'b_down': 6.497,
     'ln2_g': 7.174,
     'ln2_b': 7.285,
     'cache_mem_k': 2.942}
    for name, (base, spread) in spreads.items():
        noise = np.random.default_rng([zlib.crc32(name.encode()), seed]).standard_normal(out[name].shape)
        drawn = base * np.exp(spread * noise) if base else spread * noise
        out[name] = __import__('jax').numpy.asarray(drawn.astype(out[name].dtype))
    for name, factor in factors.items():
        out[name] = (out[name] * factor).astype(out[name].dtype)
    return out
```

```python
from contextlib import ExitStack

import numpy as np
import concourse.bass as bass
from concourse import mybir

F32 = mybir.dt.float32
I32 = mybir.dt.int32
ALU = mybir.AluOpType
ACT = mybir.ActivationFunctionType
AX = mybir.AxisListType

P = 128
D = 1024
KT = D // P
NP_TOK = 256
NB = 8
T = NP_TOK + NB
TOK = [(0, 128), (128, 128), (256, NB)]
PAGE = 128
PAGES = 16
N_PAGES = 160
SBH, SBD = 8, 64
MH, MD = 4, 128
W5 = 512
RWT = 14
FT = 30
IN_W = 6912
GATE0 = 3840
NE = 32
CAP = 64
ROUNDS = -(-T // CAP) - 1
SLOT = 4096
RING = 4
C = 64
ALPHA = 2.0 ** 0.25
SB_SCALE = 0.125
MEM_SCALE = 128.0 ** -0.5
GN_EPS = 64e-5
LN_EPS = 1e-5
DECAY = -float(np.exp(-0.5))
LIMIT = 7.0
SWA = 1.702

Q0, K0, V0, MQ0, RW0 = 0, 4, 8, 12, 16


def phase1_stream():
    s = [("win", 0)]
    for i in range(1, 8):
        s += [("win", i), ("K", 2 * i - 2), ("K", 2 * i - 1)]
    s += [("mkv", 0), ("K", 14), ("mkv", 1), ("K", 15)]
    s += [("V", i) for i in range(16)]
    s += [("mK", 0), ("mK", 1), ("mV", 0), ("mV", 1)]
    for br in range(3):
        s += [("wo", br), ("gate", br, 0), ("gate", br, 1)]
    s += [("wout", 0), ("wout", 1)]
    return s


def psum_plan():
    g = []
    add = lambda name, bank: g.append((name, bank))
    for k in range(KT):
        add(("xT", k), k)
    for k in range(KT):
        add(("memT", k), k)
    add("params", 0)
    add("shift_in", 1)
    for c in range(8):
        if c:
            add(("qb", c - 1), 6 + (c - 1) % 2)
        for ft in range(4 * c, min(4 * c + 4, FT)):
            add(("p", ft), ft % 6)
    add(("qb", 7), 7)
    for h in range(MH):
        add(("mk", h), h)
    for tt in range(2):
        add(("mv", tt), 4 + tt)
    for tt in range(3):
        add(("kt", tt), tt)
        add(("vt", tt), 3 + tt)
    for tt in range(2):
        add(("mkt", tt), tt)
    for j in range(4):
        add(("shift_out", j), 2 + j)
    for i in range(2):
        add(("cs_s", i), i)
    for g4 in range(4):
        for hp in range(2):
            add(("z", g4, hp), hp)
        add(("pv", g4), 6 + g4 % 2)
        for hp in range(2):
            add(("cs", g4, hp), 2 + hp)
        if g4 == 0:
            add("so_s", 5)
        add(("so", g4), 4)
    for h in range(MH):
        add(("mz", h), h % 2)
        add(("pv", 4 + h), 6 + h % 2)
        add(("mpT", h), 2 + h % 2)
        add(("mo", h), 4)
    add("so_sT", 2)
    for b in range(NB):
        add(("mqb", b), b % 2)
    add("mzT", 3)
    add("mpTs", 4)
    for i in range(2):
        add(("mpv", i), 6 + i)
    add("mo_s", 5)
    add("mo_sT", 2)
    for t in range(4):
        add(("dec", t), t)
    for t in range(4):
        add(("aaa", t), 4 + t)
    for t in range(4):
        add(("gr", t), t)
    for t in range(4):
        add(("kn", t), 4 + t)
    for t in range(4):
        add(("bon", t), t)
    for t in range(4):
        add(("st", t), 4 + t)
    for t in range(4):
        add(("sa", t), t)
    for t in range(4):
        add(("vb", t), 4 + t)
    for hp in range(2):
        add(("ys", hp), hp)
    for j in range(8):
        add(("so_out", j), j)
    for tt in range(2):
        for hh in range(2):
            n = (tt, hh)
            add(("tab",) + n, 6)
            add(("tkv",) + n, 7)
            for hp in range(2):
                add(("g1", hp) + n, hp)
            for hp in range(2):
                add(("g2", hp) + n, 2 + hp)
            for hp in range(2):
                add(("g3", hp) + n, 4 + hp)
            for lv in range(5):
                add(("X", lv) + n, 0)
                if lv < 4:
                    add(("TX", lv) + n, 1)
                add(("XT", lv) + n, 2)
            add(("MV",) + n, 3)
            add(("Z",) + n, 4)
            add(("WT",) + n, 5)
            for cc in range(2):
                add(("U", cc) + n, 6)
                add(("dS", cc) + n, 7)
            add(("Y",) + n, 3)
    add("wkv_out", 0)
    for t in range(4):
        add(("gm", t), 4 + t)
    for t in range(4):
        add(("gv", t), t)
    for br in range(3):
        for dt in range(KT):
            add(("gate", br, dt), 4 + dt % 2)
            add(("o", br, dt), 6 + dt % 2)
    for tt in range(3):
        for half in range(2):
            add(("res", tt, half), 2 * tt + half)
    for tt in range(3):
        for j in range(2):
            add(("h1T", tt, j), (6 + j) if tt != 1 else j)
    for tt in range(3):
        add(("logit", tt), 2 + tt)
    add("rank", 5)
    for j in range(2):
        add(("bT", j), 6)
    for tt in range(3):
        for half in range(2):
            add(("bd", tt, half), half)
    return g


class Groups:

    def __init__(self, plan):
        self.where, self.uses = {}, [0] * 8
        for name, bank in plan:
            assert name not in self.where, name
            self.where[name] = (bank, self.uses[bank])
            self.uses[bank] += 1


class Chain:

    def __init__(self, eng, sem):
        self.eng, self.sem, self.at, self.n = eng, sem, 0, 0

    def __call__(self, ins):
        ins.then_inc(self.sem, 1)
        self.at = self.at + 1
        self.n += 1
        self.eng.wait_ge(self.sem, self.at)


def rows_bc(ap, rows):
    return ap.partition_broadcast(rows)


def build(nc, A, O):
    stream = phase1_stream()
    slot_of = {name: (n % RING, n // RING) for n, name in enumerate(stream)}
    n_stream = len(stream)
    G = Groups(psum_plan())

    ctx = ExitStack()
    with ctx:
        def sb(name, shape, dt=F32):
            return ctx.enter_context(nc.sbuf_tensor(name, shape, dt))

        sems = {}

        def sem(name):
            if name not in sems:
                sems[name] = ctx.enter_context(nc.semaphore(name))
            return sems[name]

        bank = [ctx.enter_context(nc.psum_tensor(f"bank{i}", [P, 512], F32)) for i in range(8)]
        full = [sem(f"bank{i}_full") for i in range(8)]
        free = [sem(f"bank{i}_free") for i in range(8)]
        landed = [sem(f"slot{i}_landed") for i in range(RING)]

        ring = sb("ring", [P, RING, SLOT])
        pT = sb("projT", [P, FT, T])
        xT = sb("xT", [P, KT, T])
        memT = sb("memT", [P, KT, T])
        mergedT = memT
        ident = sb("ident", [P, P])
        ones = sb("ones", [P, P])
        tri_ge = sb("tri_ge", [P, P])
        tri_lt = sb("tri_lt", [P, P])
        lev = [sb(f"lev{i}", [P, P]) for i in range(6)]
        m_up = sb("m_up", [P, P])
        m_upi = sb("m_upi", [P, P])
        m_lo = sb("m_lo", [P, P])
        blk = sb("blk", [P, P])
        blk64 = sb("blk64", [P, P])
        idd = sb("idd", [P, 64])
        iota = sb("iota", [P, CAP])
        scanm = sb("scan_keep", [P, NP_TOK])
        eps = sb("eps", [P, 2])
        pcol = sb("param_cols", [P, 42])
        shT = sb("shift_inT", [P, RWT, NB])
        psh = sb("shift_out", [P, RWT, 9])
        m_page = sb("m_page", [P, W5])
        pick = sb("pick", [P, 15])
        pick4 = sb("pick4", [P, 12])
        sb_bias = sb("sb_bias_bc", [P, SBH])
        w_lora = sb("w_lora", [P, W5])
        w_gate2 = sb("w_gate2s", [P, W5])
        zs = sb("sample_logits", [P, NB, PAGES, SBH])
        pages = sb("pages", [1, NB * PAGES], I32)
        flag = sb("overflow", [P, 1], I32)
        arena = sb("arena", [P, 19220])
        YB = 13070

        def ar(off, *dims):
            n = int(np.prod(dims))
            assert off + n <= 19220
            v = arena[:, off:off + n]
            if len(dims) == 2:
                return v.rearrange("p (a b) -> p a b", a=dims[0])
            if len(dims) == 3:
                return v.rearrange("p (a b c) -> p a b c", a=dims[0], b=dims[1])
            return v

        ktok, vtok = ar(YB, 3, W5), ar(YB + 1536, 3, W5)
        mktok, mvtok = ar(YB + 3072, 2, W5), ar(YB + 4096, 2, W5)
        mkT = ar(YB + 5120, MH, NP_TOK)
        xr, memr = ar(0, 3, D), ar(3072, 2, D)
        shrow, prow = ar(7168, 1792), ar(8960, 128)
        same = [None] + [ar(9500 + 128 * i, P) for i in range(5)] + [blk[:]]
        sa_, sb_ = ar(0, NB * PAGES * SBH), ar(1024, NB * PAGES * SBH)
        spx = ar(2048, NB, PAGES, SBH)
        zp, np_, sp_, wp_ = (ar(3072 + 768 * i, 2, 384) for i in range(4))
        mp = ar(6144, 2, NP_TOK)
        mpT = ar(6656, 2, NP_TOK)
        mst = ar(7168, 16)
        zm, mps, mpTs = ar(7200, 2, 32), ar(7264, NP_TOK), ar(7520, 2, 32)
        shout = ar(7680, 1792)
        m_mem = [ar(10200 + 512 * i, W5) for i in range(2)]
        pvm = [ar(11300 + 512 * i, W5) for i in range(2)]
        orow = ar(12330, W5)
        LD, AA, KK, KM, GG, BON, T1, T2 = (ar(1056 * i, 4, T) for i in range(8))
        R0 = 8448
        SN = ar(R0, NB, 4, P)
        St = ar(R0 + 4096, 4, NB, 64)
        S1, S2 = ar(R0 + 6144, 4, NB, 64), ar(R0 + 8192, 4, NB, 64)
        tokAB, tokKV = ar(R0, 2, 256), ar(R0 + 512, 2, 256)
        Nl, Nt, Tm, Tt, Xm, AK, RB, RK = (ar(R0 + 1024 + 512 * i, 4, P) for i in range(8))
        Nm = [ar(R0 + 5120 + 512 * i, 4, P) for i in range(5)]
        MVs, Zs, Us = (ar(R0 + 7680 + 256 * i, 4, 64) for i in range(3))
        WTs, PM, tS = (ar(R0 + 8448 + 256 * i, 2, P) for i in range(3))
        Sb = [ar(R0 + 9216 + 512 * i, 4, P) for i in range(3)]
        assert R0 + 9216 + 1536 <= 19220
        sig, prod = ar(0, 2, T), ar(600, T)
        xres = ar(0, 3, D)
        h1 = ar(3072, 3, D)
        yacc = ar(6144, 3, D)
        lng, lnb, ln2g, ln2b = (ar(9216 + 1024 * i, D) for i in range(4))
        sq = ar(13312, D)
        st_ = ar(14336, 24)
        bdrow = ar(14400, D)
        wr = ar(15424, KT, NE)
        lg, sel, wt, tmpE = (ar(15680 + 128 * i, 3, 34) for i in range(4))
        pos = ar(16192, 3, 34)
        wTt = ar(16320, T)
        h1T = ar(16600, KT, T)
        brt = ar(18720, NE)
        mx8 = ar(18760, 24)
        oneh, onew = ar(0, 3, 2, CAP), ar(384, 3, 2, CAP)
        onewT = ar(768, T)
        ysb = ar(1040, D)
        gb, lb, hb = ([ar(2064 + 256 * j + 128 * i, P) for i in range(2)] for j in range(3))
        sg = [ar(13312 + 128 * i, P) for i in range(2)]
        pick_e = [ar(13568 + 64 * i, CAP) for i in range(2)]
        bup = ar(9216, 2048)
        xg = xT[:, :, 0:P]
        hT = [memT[:, :, CAP * i:CAP * i + CAP] for i in range(2)]

        MU, DE0, AA0, KKp, KAp, RKp, GNG, GNB = 0, 14, 18, 22, 26, 30, 34, 38

        def slot(name):
            return ring[:, slot_of[name][0], :]

        def arrived(eng, name):
            s = slot_of[name][0]
            if name in page_count:
                eng.wait_ge(sem(f"page{s}_landed"), page_count[name])
            elif name in mem_count:
                eng.wait_ge(sem(f"mem{s}_landed"), mem_count[name])
            else:
                eng.wait_ge(landed[s], landed_count[name])

        def full_of(name):
            b, use = G.where[name]
            return full[b], use + 1

        def last_reader(name):
            kind, i = name[0], name[1]
            if kind == "win":
                return full_of(("p", min(4 * i + 3, FT - 1)))
            if kind == "mkv":
                return full_of(("mk", 3) if i == 0 else ("mv", 1))
            if kind == "K":
                return sem("k_used"), i + 1
            if kind == "V":
                return full_of(("pv", i // 2))
            if kind == "mK":
                return sem("mk_used"), i + 1
            if kind == "mV":
                return full_of(("mpv", i))
            if kind == "wo":
                return full_of(("o", i, KT - 1))
            if kind == "gate":
                return full_of(("gate", i, 4 * name[2] + 3))
            return full_of(("res", 2, 1))

        page_count, mem_count = {}, {}
        for s in range(RING):
            np_so_far = nm_so_far = 0
            for name in stream:
                if slot_of[name][0] == s and name[0] in ("K", "V"):
                    np_so_far += 16 * 8
                    page_count[name] = np_so_far
                if slot_of[name][0] == s and name[0] in ("mK", "mV"):
                    nm_so_far += 16 * 4
                    mem_count[name] = nm_so_far
        landed_count, seen = {}, [0] * RING
        for name in stream:
            if name[0] not in ("K", "V", "mK", "mV"):
                seen[slot_of[name][0]] += 16
                landed_count[name] = seen[slot_of[name][0]]

        def take(eng, name):
            b, use = G.where[name]
            eng.wait_ge(full[b], use + 1)
            return bank[b]

        def gone(eng, name):
            b, use = G.where[name]
            eng.wait_ge(free[b], use + 1)

        def freed_by(name):
            return free[G.where[name][0]]

        col = lambda i: pcol[:, i:i + 1]
        block = ctx.enter_context(nc.Block())

        @block.sync
        def _(sp):
            sp.dma_start(pages[:], A["page_table"].rearrange("b n -> (b n)").unsqueeze(0)).then_inc(sem("pages_in"), 16)
            win = A["w_in"][0].rearrange("(k p) n -> p k n", p=P)
            mkv = A["w_mem_kv"][0].rearrange("(k p) n -> p k n", p=P)
            kc = A["cache_sb_k"][0].rearrange("g p h d -> g p (h d)")
            vc = A["cache_sb_v"][0].rearrange("g p h d -> g p (h d)")
            mkc = A["cache_mem_k"][0].rearrange("b (m p) h d -> p b m (h d)", p=P)
            mvc = A["cache_mem_v"][0].rearrange("b (m p) h d -> p b m (h d)", p=P)
            wo = [A[n][0].rearrange("(k p) n -> p k n", p=P) for n in ("w_sb_o", "w_mem_o", "w_rw_o")]
            wout = A["w_out"][0].rearrange("(k p) n -> p k n", p=P)
            sp.wait_ge(sem("pages_in"), 16)
            for n, name in enumerate(stream):
                s, use = slot_of[name]
                if use:
                    sp.wait_ge(*last_reader(stream[n - RING]))
                dst = slot(name)
                d8 = dst.rearrange("p (k n) -> p k n", k=KT)
                if name[0] == "win":
                    c0 = 512 * name[1]
                    w = min(512, GATE0 - c0)
                    sp.dma_start(d8[:, :, 0:w], win[:, :, c0:c0 + w]).then_inc(landed[s], 16)
                elif name[0] == "gate":
                    c0 = GATE0 + 1024 * name[1] + 512 * name[2]
                    sp.dma_start(d8, win[:, :, c0:c0 + 512]).then_inc(landed[s], 16)
                elif name[0] == "mkv":
                    c0 = 512 * name[1]
                    sp.dma_start(d8, mkv[:, :, c0:c0 + 512]).then_inc(landed[s], 16)
                elif name[0] in ("K", "V"):
                    src = kc if name[0] == "K" else vc
                    for j in range(8):
                        at = 8 * name[1] + j
                        page = sp.value_load(pages[0:1, at:at + 1], min_val=0, max_val=N_PAGES - 1)
                        sp.dma_start(d8[:, j, :], src[bass.ds(page, 1), :, :].rearrange("g p n -> p (g n)")).then_inc(
                            sem(f"page{s}_landed"), 16)
                elif name[0] in ("mK", "mV"):
                    src = mkc if name[0] == "mK" else mvc
                    for b in range(4):
                        sp.dma_start(dst.rearrange("p (b m n) -> p b m n", b=4, m=2)[:, b], src[:, 4 * name[1] + b]).then_inc(
                            sem(f"mem{s}_landed"), 16)
                elif name[0] == "wo":
                    sp.dma_start(dst.rearrange("p (k n) -> p k n", k=4), wo[name[1]]).then_inc(landed[s], 16)
                else:
                    sp.dma_start(dst.rearrange("p (k n) -> p k n", k=4),
                                 wout[:, 4 * name[1]:4 * name[1] + 4, :]).then_inc(landed[s], 16)

            wgu = A["w_gate_up"][0].rearrange("e (k p) n -> e p k n", p=P)
            wdn = A["w_down"][0].rearrange("e (k p) n -> e p k n", p=P)

            def pair_loads(p, it, first=False):
                for c in range(12):
                    s = (n_stream + c) % RING
                    e = 2 * p + c // 6
                    prev = c - RING
                    if first and prev < 0:
                        sp.wait_ge(*last_reader(stream[n_stream + prev]))
                    else:
                        ei, j = prev % 12 // 6, prev % 12 % 6
                        wraps = 1 if prev < 0 else 0
                        if j < 4:
                            sp.wait_ge(sem("up_full"), it * 8 + (4 * ei + j + 1 - 8 * wraps))
                        else:
                            sp.wait_ge(sem("down_full"), it * 4 + (2 * ei + j - 4 + 1 - 4 * wraps))
                    if c % 6 < 4:
                        sp.dma_start(ring[:, s, :].rearrange("p (k n) -> p k n", k=KT),
                                     wgu[bass.ds(e, 1), :, :, 512 * (c % 6):512 * (c % 6) + 512].rearrange("e p k n -> p (e k) n")
                                     ).then_inc(sem(f"expert{s}_landed"), 16)
                    else:
                        k0 = 4 * (c % 6 - 4)
                        sp.dma_start(ring[:, s, :].rearrange("p (k n) -> p k n", k=4),
                                     wdn[bass.ds(e, 1), :, k0:k0 + 4, :].rearrange("e p k n -> p (e k) n")
                                     ).then_inc(sem(f"expert{s}_landed"), 16)

            pair_loads(0, 0, True)
            with sp.Fori(1, NE // 2) as p:
                pair_loads(p, p)
            sp.wait_ge(sem("flag_ready"), 1)
            over = sp.value_load(flag[0:1, 0:1], min_val=0, max_val=T)
            with sp.If(over > CAP):
                with sp.Fori(0, ROUNDS) as r:
                    with sp.Fori(0, NE // 2) as p:
                        pair_loads(p, (r + 1) * (NE // 2) + p)

        @block.gpsimd
        def _(g):
            link = Chain(g, sem("pool_chain"))
            xs = A["x_prompt"][0].rearrange("(t p) d -> p t d", p=P)
            g.dma_start(xr[:, 0:2, :], xs).then_inc(sem("x_in"), 16)
            g.dma_start(xr[0:NB, 2, :], A["x_sample"].rearrange("b s d -> (b s) d")).then_inc(sem("x_in"), 16)
            g.memset(ident[:], 0.0).then_inc(sem("pool_chain"), 1)
            g.memset(ones[:], 1.0).then_inc(sem("pool_chain"), 1)
            link.at = 2
            g.wait_ge(sem("pool_chain"), 2)
            link(g.affine_select(out=ident[:], in_=ident[:], compare_op=ALU.not_equal, fill=1.0, base=0,
                                 pattern=[[-1, P]], channel_multiplier=1))
            g.sem_inc(sem("ident_ready"), 1)
            g.dma_start(memr[:, :, :], A["mem_prompt"][0].rearrange("(t p) d -> p t d", p=P)).then_inc(sem("mem_in"), 16)
            vec = lambda n, k: A[n].rearrange("l (t p) -> (l t) p", p=P)
            r0 = 0
            for n, k in (("mu_rw", 14), ("w_decay0", 4), ("w_aaa0", 4), ("rw_k_k", 4), ("rw_k_a", 4)):
                g.dma_start(prow[r0:r0 + k, :], vec(n, k)).then_inc(sem("param_in"), 16)
                r0 += k
            g.dma_start(prow[r0:r0 + 4, :], A["rw_r_k"].rearrange("l (t a) d -> (l t) (a d)", a=2)).then_inc(sem("param_in"), 16)
            r0 += 4
            for n in ("rw_gn_g", "rw_gn_b"):
                g.dma_start(prow[r0:r0 + 4, :], vec(n, 4)).then_inc(sem("param_in"), 16)
                r0 += 4
            g.dma_start(shrow[0:NB, :], A["state_rw_shift"][0]).then_inc(sem("param_in"), 16)
            g.dma_start(sb_bias[:], rows_bc(A["sb_bias"][0], P)).then_inc(sem("bias_in"), 16)
            g.dma_start(w_lora[0:64, :], A["w_decay2"][0]).then_inc(sem("lora_in"), 16)
            g.dma_start(w_lora[64:128, :], A["w_aaa2"][0]).then_inc(sem("lora_in"), 16)
            g.dma_start(w_gate2[:], A["w_gate2"][0]).then_inc(sem("lora_in"), 16)
            sel = lambda m, src, op, base, pat, cm: link(g.affine_select(
                out=m, in_=src, compare_op=op, fill=0.0, base=base, pattern=pat, channel_multiplier=cm))
            sel(tri_ge[:], ones[:], ALU.is_ge, 0, [[-1, P]], 1)
            sel(tri_lt[:], ones[:], ALU.is_gt, 0, [[1, P]], -1)
            g.sem_inc(sem("tri_ready"), 1)
            for i in range(1, 7):
                m = 1 << i
                v = same[i].rearrange("p (g j) -> p g j", j=m)
                link(g.memset(same[i], 1.0))
                sel(v, v, ALU.is_ge, 0, [[-m, P // m], [0, m]], 1)
                sel(v, v, ALU.is_ge, m - 1, [[m, P // m], [0, m]], -1)
            for i in range(6):
                lo = ident[:] if i == 0 else same[i]
                g.tensor_tensor(lev[i][:], same[i + 1], lo, ALU.subtract).then_inc(sem("masks"), 1)
            link(g.tensor_tensor(m_up[:], tri_lt[:], blk[:], ALU.mult))
            link(g.tensor_tensor(m_upi[:], m_up[:], ident[:], ALU.add))
            link(g.tensor_tensor(m_lo[:], blk[:], m_upi[:], ALU.subtract))
            link(g.tensor_scalar(blk64[:], blk[:], 1.0 / 64, 0.0, ALU.mult, ALU.add))
            link(g.tensor_tensor(idd[:], ident[:, 0:64], ident[:, 64:128], ALU.add))
            link(g.iota(iota[:], pattern=[[1, CAP]], base=0, channel_multiplier=0, allow_small_or_imprecise_dtypes=True))
            link(g.memset(scanm[:], 1.0))
            link(g.memset(scanm[:].rearrange("p (c j) -> p c j", j=C)[:, :, 0:1], 0.0))
            link(g.memset(eps[:, 0:1], GN_EPS))
            link(g.memset(eps[:, 1:2], LN_EPS))
            link(g.memset(pick[:], 0.0))
            link(g.memset(pick[:, 7:8], 1.0))
            link(g.memset(pick4[:], 1.0))
            sel(pick4[:], pick4[:], ALU.is_ge, 128, [[-32, 12]], 1)
            sel(pick4[:], pick4[:], ALU.is_ge, 31 - 128, [[32, 12]], -1)
            for m, step, offs, n in [(m_page[:], 40, 0, SBH), (m_mem[0], 36, 0, MH), (m_mem[1], 36, 16, MH)]:
                link(g.memset(m, 0.0))
                mv_ = m.rearrange("p (h d) -> p h d", h=n)
                for q in range(4):
                    link(g.affine_select(out=mv_, in_=mv_, compare_op=ALU.not_equal, fill=1.0, base=-step * q - offs,
                                         pattern=[[-1, n], [0, W5 // n]], channel_multiplier=1))
            g.sem_inc(sem("masks"), 1)

            def out(dst, src):
                g.dma_start(dst, src).then_inc(sem("out_done"), 16)

            n_out = 0
            for tt in range(3):
                gone(g, ("kt", tt))
                gone(g, ("vt", tt))
            for nm, src in (("sb_k", ktok), ("sb_v", vtok)):
                out(O[nm + "_prompt"][0, 0].rearrange("(t p) h d -> p t (h d)", p=P), src[:, 0:2, :])
                out(O[nm + "_sample"][0].rearrange("b s h d -> b (s h d)"), src[0:NB, 2, :])
            for tt in range(2):
                gone(g, ("mkt", tt))
                gone(g, ("mv", tt))
            for j in range(4):
                gone(g, ("shift_out", j))
            out(O["mem_k"][0, 0].rearrange("(t p) h d -> p t (h d)", p=P), mktok)
            out(O["mem_v"][0, 0].rearrange("(t p) h d -> p t (h d)", p=P), mvtok)
            out(O["shift_prompt"][0], shout[0:1, :])
            out(O["shift_sample"][0], shout[1:9, :])
            n_out += 8
            g.wait_ge(sem("out_done"), 16 * n_out)
            g.sem_inc(sem("arena_clear"), 1)
            g.wait_ge(sem("rw_clear"), 1)
            for b in range(NB):
                g.dma_start(SN[0:64, b].rearrange("v t (hp k) -> v (t hp) k", hp=2),
                            A["state_rw_wkv"][0, b].rearrange("h v k -> v h k")).then_inc(sem("state_in"), 16)
            for j in range(8):
                gone(g, ("so_out", j))
            for b in range(NB):
                g.dma_start(O["wkv_sample"][0, b].rearrange("h v k -> v h k"),
                            SN[0:64, b].rearrange("v t (hp k) -> v (t hp) k", hp=2)).then_inc(sem("out_done"), 16)
            n_out += NB
            g.wait_ge(sem("out_done"), 16 * n_out)
            g.sem_inc(sem("arena_clear"), 1)
            for it in range(4):
                n = (it // 2, it % 2)
                gone(g, ("g1", 0) + n)
                gone(g, ("g1", 1) + n)
                for lv in range(5):
                    g.tensor_tensor(Nm[lv], Nt, lev[lv + 1][:].unsqueeze(1).to_broadcast([P, 4, P]),
                                    ALU.mult).then_inc(sem("Nm_ready"), 1)
            gone(g, "wkv_out")
            for hp in range(2):
                g.dma_start(O["wkv_prompt"][0, 0].rearrange("(t hp) v k -> hp v t k", hp=2)[hp],
                            Nm[0][64 * hp:64 * hp + 64, :, 64 * hp:64 * hp + 64]).then_inc(sem("out_done"), 16)
            n_out += 2
            g.wait_ge(sem("out_done"), 16 * n_out)
            g.wait_ge(sem("rw_done"), 1)
            for dst, nm in ((lng, "ln1_g"), (lnb, "ln1_b"), (ln2g, "ln2_g"), (ln2b, "ln2_b")):
                g.dma_start(dst, rows_bc(A[nm][0], P)).then_inc(sem("ln_in"), 16)
            g.dma_start(bdrow[0:NE, :], A["b_down"][0]).then_inc(sem("ln_in"), 16)
            g.dma_start(wr, A["w_router"][0].rearrange("(k p) e -> p k e", p=P)).then_inc(sem("ln_in"), 16)
            g.dma_start(brt, rows_bc(A["b_router"][0], P)).then_inc(sem("ln_in"), 16)
            g.wait_ge(sem("merged"), 1)
            g.dma_start(xres[:, 0:2, :], xs).then_inc(sem("ln_in"), 16)
            g.dma_start(xres[0:NB, 2, :], A["x_sample"].rearrange("b s d -> (b s) d")).then_inc(sem("ln_in"), 16)
            g.wait_ge(sem("h1"), 3)
            link(g.memset(bup, 0.0))
            g.dma_start(bup[0:NE, :], A["b_gate_up"][0]).then_inc(sem("bias_up_in"), 16)
            for tt, (t0, rows) in enumerate(TOK):
                g.wait_ge(sem("y_ready"), tt + 1)
                dst = O["y_prompt"][0, t0:t0 + rows, :] if tt < 2 else O["y_sample"].rearrange("b s d -> (b s) d")
                g.dma_start(dst, yacc[0:rows, tt, :]).then_inc(sem("out_done"), 16)
                n_out += 1
            g.wait_ge(sem("out_done"), 16 * n_out)

        @block.tensor
        def _(pe):
            opened = [0] * 8

            def start(name):
                b, use = G.where[name]
                assert opened[b] == use, name
                opened[b] += 1
                if use:
                    pe.wait_ge(free[b], use)
                return bank[b]

            def done(name, ins):
                ins.then_inc(full[G.where[name][0]], 1)

            mm = lambda out, l, r, first, last, **k: pe.matmul(out, l, r, start=first, stop=last, **k)
            tr = lambda out, src, rows=P: pe.transpose(out, src, ident[0:rows, 0:rows])

            pe.wait_ge(sem("ident_ready"), 1)
            pe.wait_ge(sem("x_in"), 32)
            for k in range(KT):
                b = start(("xT", k))
                for tt, (t0, rows) in enumerate(TOK):
                    last = tr(b[:, t0:t0 + rows], xr[0:rows, tt, k * P:(k + 1) * P], rows)
                done(("xT", k), last)
            pe.wait_ge(sem("mem_in"), 16)
            for k in range(KT):
                b = start(("memT", k))
                for tt in range(2):
                    last = tr(b[:, tt * P:tt * P + P], memr[:, tt, k * P:(k + 1) * P])
                done(("memT", k), last)
            pe.wait_ge(sem("param_in"), 144)
            b = start("params")
            done("params", tr(b[:, 0:42], prow[0:42, :], 42))
            b = start("shift_in")
            for t in range(RWT):
                last = tr(b[:, NB * t:NB * t + NB], shrow[0:NB, t * P:t * P + P], NB)
            done("shift_in", last)
            def q_broadcast(name, b0, tile0, tok):
                b = start(name)
                for t in range(4):
                    last = mm(b[:, t * P:t * P + P], pT[:, tile0 + t, tok:tok + 1].to_broadcast([P, P]), ident[:], True, True)
                done(name, last)

            for c in range(8):
                if c:
                    gone(pe, ("p", 3))
                    q_broadcast(("qb", c - 1), c - 1, Q0, NP_TOK + c - 1)
                arrived(pe, ("win", c))
                w = slot(("win", c)).rearrange("p (k n) -> p k n", k=KT)
                if c == 0:
                    for k in range(KT):
                        gone(pe, ("xT", k))
                for ft in range(4 * c, min(4 * c + 4, FT)):
                    b = start(("p", ft))
                    j = ft - 4 * c
                    for k in range(KT):
                        last = mm(b[:, 0:T], w[:, k, j * P:j * P + P], xT[:, k, :], k == 0, k == KT - 1)
                    done(("p", ft), last)
            q_broadcast(("qb", 7), 7, Q0, NP_TOK + 7)
            arrived(pe, ("mkv", 0))
            w = slot(("mkv", 0)).rearrange("p (k n) -> p k n", k=KT)
            for k in range(KT):
                gone(pe, ("memT", k))
            for h in range(MH):
                b = start(("mk", h))
                for k in range(KT):
                    last = mm(b[:, 0:NP_TOK], w[:, k, h * P:h * P + P], memT[:, k, 0:NP_TOK], k == 0, k == KT - 1)
                done(("mk", h), last)
            arrived(pe, ("mkv", 1))
            w = slot(("mkv", 1)).rearrange("p (k n) -> p k n", k=KT)
            for tt in range(2):
                b = start(("mv", tt))
                for k in range(KT):
                    last = mm(b[:, :], memT[:, k, tt * P:tt * P + P], w[:, k, :], k == 0, k == KT - 1)
                done(("mv", tt), last)
            for ft in range(K0, K0 + 8):
                gone(pe, ("p", ft))
            for tt, (t0, rows) in enumerate(TOK):
                for nm, f0 in (("kt", K0), ("vt", V0)):
                    b = start((nm, tt))
                    for t in range(4):
                        last = tr(b[0:rows, t * P:t * P + P], pT[:, f0 + t, t0:t0 + rows])
                    done((nm, tt), last)
            for h in range(MH):
                gone(pe, ("mk", h))
            for tt in range(2):
                b = start(("mkt", tt))
                for h in range(MH):
                    last = tr(b[:, h * P:h * P + P], mkT[:, h, tt * P:tt * P + P])
                done(("mkt", tt), last)
            for ft in range(24, FT):
                gone(pe, ("p", ft))
            pe.wait_ge(sem("shift_cut"), 1)
            for j in range(4):
                b = start(("shift_out", j))
                for t in range(4 * j, min(4 * j + 4, RWT)):
                    last = tr(b[0:9, (t % 4) * P:(t % 4) * P + P], psh[:, t, :])
                done(("shift_out", j), last)

            pe.wait_ge(sem("tri_ready"), 1)
            pe.wait_ge(sem("sp_s"), 1)
            spf, spxf = sb_, spx.rearrange("p b n h -> p (b n h)")
            for i in range(2):
                b = start(("cs_s", i))
                mm(b[:, :], tri_ge[:], spf[:, 512 * i:512 * i + 512], True, False)
                done(("cs_s", i), mm(b[:, :], ones[:], spxf[:, 512 * i:512 * i + 512], False, True))

            def sample_values(bq):
                if bq == 0:
                    pe.wait_ge(sem("w_s"), 1)
                arrived(pe, ("V", 2 * bq))
                b = start(("pv", bq))
                for n in range(PAGES):
                    if n == 8:
                        arrived(pe, ("V", 2 * bq + 1))
                    v = slot(("V", 2 * bq + n // 8)).rearrange("p (k n) -> p k n", k=8)
                    i, q = n // 4, n % 4
                    last = mm(b[32 * q:32 * q + 32, :], zs[:, bq, 4 * i:4 * i + 4, :].rearrange("p n h -> p (n h)"),
                              v[:, n % 8, :], i == 0, i == 3)
                done(("pv", bq), last)

            def sample_sum(bq):
                pe.wait_ge(sem("pv_kept"), bq + 1)
                b = start("so_s") if bq == 0 else bank[5]
                last = mm(b[0:NB, :], pick[:, 7 - bq:15 - bq], pvm[bq % 2], bq == 0, bq == NB - 1)
                last.then_inc(sem("pv_summed"), 1) if bq < NB - 1 else done("so_s", last)

            for g4 in range(4):
                for hp in range(2):
                    b = start(("z", g4, hp))
                    q = pT[64 * hp:64 * hp + 64, Q0 + g4, :]
                    k = pT[64 * hp:64 * hp + 64, K0 + g4, :]
                    mm(b[:, 0:256], k[:, 0:128], q[:, 0:256], True, True)
                    done(("z", g4, hp), mm(b[:, 256:384], k[:, 128:256], q[:, 128:256], True, True))
                sample_values(g4)
                pe.wait_ge(sem("sp_p"), g4 + 1)
                for hp in range(2):
                    b = start(("cs", g4, hp))
                    mm(b[:, 0:384], tri_ge[:], sp_[:, hp, :], True, True)
                    done(("cs", g4, hp), mm(b[:, 128:256], ones[:], sp_[:, hp, 256:384], False, True, skip_group_check=True))
                sample_sum(g4)
                gone(pe, ("vt", 0))
                gone(pe, ("vt", 1))
                pe.wait_ge(sem("w_p"), g4 + 1)
                b = start(("so", g4))
                for hp in range(2):
                    h = 2 * g4 + hp
                    o = b[64 * hp:64 * hp + 64, :]
                    mm(o[:, 0:256], vtok[:, 0, h * 64:h * 64 + 64], wp_[:, hp, 0:256], True, True)
                    last = mm(o[:, 128:256], vtok[:, 1, h * 64:h * 64 + 64], wp_[:, hp, 256:384], False, True, skip_group_check=True)
                done(("so", g4), last)

            for h in range(MH):
                b = start(("mz", h))
                for qt in range(2):
                    last = mm(b[:, 256 * qt:256 * qt + 256], pT[:, MQ0 + h, qt * P:qt * P + P], mkT[:, h, :], True, True)
                done(("mz", h), last)
                sample_values(4 + h)
                pe.wait_ge(sem("mp"), h + 1)
                b = start(("mpT", h))
                for mt in range(2):
                    for qt in range(2):
                        last = tr(b[:, 256 * mt + qt * P:256 * mt + qt * P + P], mp[:, qt, mt * P:mt * P + P])
                done(("mpT", h), last)
                sample_sum(4 + h)
                gone(pe, ("mpT", h))
                gone(pe, ("mv", 0))
                gone(pe, ("mv", 1))
                b = start(("mo", h))
                for mt in range(2):
                    last = mm(b[:, 0:256], mvtok[:, mt, h * P:h * P + P], mpT[:, mt, :], mt == 0, mt == 1)
                done(("mo", h), last)
            def row_to_features(name, row):
                gone(pe, row)
                b = start(name)
                for t in range(4):
                    last = tr(b[:, NB * t:NB * t + NB], orow[0:NB, t * P:t * P + P], NB)
                done(name, last)

            row_to_features("so_sT", "so_s")
            for bq in range(NB):
                q_broadcast(("mqb", bq), bq, MQ0, NP_TOK + bq)
            pe.wait_ge(sem("zm"), 1)
            b = start("mzT")
            for mt in range(2):
                last = tr(b[0:32, mt * P:mt * P + P], zm[:, mt, :])
            done("mzT", last)
            pe.wait_ge(sem("mps"), 1)
            b = start("mpTs")
            for mt in range(2):
                last = tr(b[:, 32 * mt:32 * mt + 32], mps[0:32, mt * P:mt * P + P], 32)
            done("mpTs", last)
            gone(pe, "mpTs")
            for i in range(2):
                arrived(pe, ("mV", i))
                b = start(("mpv", i))
                v = slot(("mV", i)).rearrange("p (b m n) -> p b m n", b=4, m=2)
                for mt in range(2):
                    for q in range(4):
                        last = mm(b[32 * q:32 * q + 32, :], mpTs[:, mt, :], v[:, q, mt, :], mt == 0, mt == 1)
                done(("mpv", i), last)
            b = start("mo_s")
            for i in range(2):
                gone(pe, ("mpv", i))
                last = mm(b[0:NB, :], pick4[:, 4 - 4 * i:12 - 4 * i], pvm[i], i == 0, i == 1)
            done("mo_s", last)
            row_to_features("mo_sT", "mo_s")

            pe.wait_ge(sem("lora_in"), 48)
            pe.wait_ge(sem("lora_act"), 2)
            for nm, rows in (("dec", slice(0, 64)), ("aaa", slice(64, 128))):
                for t in range(4):
                    b = start((nm, t))
                    done((nm, t), mm(b[:, 0:T], w_lora[rows, t * P:t * P + P], pT[rows, 28, :], True, True))
            for t in range(4):
                b = start(("gr", t))
                done(("gr", t), mm(b[:, 0:T], w_gate2[:, t * P:t * P + P], pT[:, 29, :], True, True))

            def over_heads(nm, src, ready, mat=blk):
                pe.wait_ge(sem(ready), 1)
                for t in range(4):
                    b = start((nm, t))
                    done((nm, t), mm(b[:, 0:src.shape[2]], mat[:], src[:, t, :], True, True))

            pe.wait_ge(sem("masks"), 7)
            over_heads("kn", T1, "kk_sq")
            over_heads("bon", T1, "rk_prod")
            pe.wait_ge(sem("state_in"), 16 * NB)
            for t in range(4):
                b = start(("st", t))
                for bq in range(NB):
                    last = tr(b[:, 64 * bq:64 * bq + 64], SN[0:64, bq, t, :], 64)
                done(("st", t), last)
            flat = lambda a: a.rearrange("p t b v -> p t (b v)")
            over_heads("sa", flat(S1), "s_kk")
            over_heads("vb", flat(S2), "s_v")
            pe.wait_ge(sem("s_new"), 1)
            bs = [start(("ys", hp)) for hp in range(2)]
            for hp in range(2):
                rows = slice(64 * hp, 64 * hp + 64)
                for t in range(4):
                    for bq in range(NB):
                        last = mm(bs[hp][rows, NB * t + bq:NB * t + bq + 1], St[rows, t, bq, :],
                                  pT[rows, RW0 + t, NP_TOK + bq:NP_TOK + bq + 1], True, True)
                done(("ys", hp), last)
            for j in range(8):
                b = start(("so_out", j))
                for i in range(4):
                    last = tr(b[0:64, i * P:i * P + P], St[:, j // 2, 4 * (j % 2) + i, :])
                done(("so_out", j), last)

            for tt in range(2):
                for hh in range(2):
                    n = (tt, hh)
                    cols = slice(tt * P, tt * P + P)
                    it = 2 * tt + hh
                    tiles = (2 * hh, 2 * hh + 1)
                    if it == 0:
                        pe.wait_ge(sem("hats"), 1)
                    for nm, srcs in (("tab", (KK, AA)), ("tkv", (KM, pT[:, 24:28, :]))):
                        b = start((nm,) + n)
                        for i, src in enumerate(srcs):
                            for tl, t in enumerate(tiles):
                                last = tr(b[:, 256 * i + P * tl:256 * i + P * tl + P], src[:, t, cols])
                        done((nm,) + n, last)
                    hats = {"A": KK, "B": AA, "K": KM, "R": pT[:, RW0:RW0 + 4, :]}
                    for nm, prods in (("g1", ("BA", "AB")), ("g2", ("BR", "KA")), ("g3", ("KR",))):
                        for hp in range(2):
                            b = start((nm, hp) + n)
                            rows = slice(64 * hp, 64 * hp + 64)
                            for i, lr in enumerate(prods):
                                for tl, t in enumerate(tiles):
                                    c0 = 256 * i + P * tl
                                    last = mm(b[:, c0:c0 + P], hats[lr[0]][rows, t, cols], hats[lr[1]][rows, t, cols], True, True)
                            done((nm, hp) + n, last)
                    pe.wait_ge(sem("T_ready"), it + 1)
                    for lv in range(5):
                        if lv:
                            gone(pe, ("TX", lv - 1) + n)
                            gone(pe, ("XT", lv - 1) + n)
                        pe.wait_ge(sem("Nm_ready"), 5 * it + lv + 1)
                        b = start(("X", lv) + n)
                        for u in range(4):
                            last = mm(b[:, u * P:u * P + P], Nm[lv][:, u, :], Tm[:, u, :], True, True)
                        done(("X", lv) + n, last)
                        gone(pe, ("X", lv) + n)
                        if lv < 4:
                            b = start(("TX", lv) + n)
                            for u in range(4):
                                last = mm(b[:, u * P:u * P + P], Tt[:, u, :], Xm[:, u, :], True, True)
                            done(("TX", lv) + n, last)
                        b = start(("XT", lv) + n)
                        for u in range(4):
                            last = mm(b[:, u * P:u * P + P], Xm[:, u, :], Tt[:, u, :], True, True)
                        done(("XT", lv) + n, last)
                    b = start(("MV",) + n)
                    gone(pe, ("tkv",) + n)
                    for hp in range(2):
                        gone(pe, ("g2", hp) + n)
                        gone(pe, ("g3", hp) + n)
                    for tl in range(2):
                        for hp in range(2):
                            u, c0 = 2 * hp + tl, 64 * (2 * tl + hp)
                            last = mm(b[:, c0:c0 + 64], AK[:, u, :], tokKV[:, 1, c0:c0 + 64], True, True)
                    done(("MV",) + n, last)
                    gone(pe, ("MV",) + n)
                    gone(pe, ("XT", 4) + n)
                    b = start(("Z",) + n)
                    for tl in range(2):
                        for hp in range(2):
                            u, j = 2 * hp + tl, 2 * tl + hp
                            last = mm(b[:, 64 * j:64 * j + 64], Tt[:, u, :], MVs[:, j, :], True, True)
                    done(("Z",) + n, last)
                    b = start(("WT",) + n)
                    for tl in range(2):
                        for hp in range(2):
                            u, c0 = 2 * hp + tl, 64 * (2 * tl + hp)
                            last = mm(b[64 * hp:64 * hp + 64, P * tl:P * tl + P], tokAB[:, 0, c0:c0 + 64], Tt[:, u, :], True, True)
                    done(("WT",) + n, last)
                    gone(pe, ("WT",) + n)
                    gone(pe, ("tab",) + n)
                    for cc in range(2):
                        c = 2 * tt + cc
                        rows = slice(64 * cc, 64 * cc + 64)
                        if 2 * it + cc:
                            pe.wait_ge(sem("S_ready"), 2 * it + cc)
                        else:
                            pe.wait_ge(sem("S_zero"), 1)
                        b = start(("U", cc) + n)
                        for tl, t in enumerate(tiles):
                            last = mm(b[rows, P * tl:P * tl + P], WTs[:, tl, rows], Sb[c % 3][:, t, :], True, True)
                        done(("U", cc) + n, last)
                        gone(pe, ("U", cc) + n)
                        b = start(("dS", cc) + n)
                        for tl in range(2):
                            o = b[:, P * tl:P * tl + P]
                            uc = Us.rearrange("p a b -> p (a b)")[rows, P * tl:P * tl + P]
                            mm(o, tokAB[rows, 1, P * tl:P * tl + P], uc, True, False)
                            last = mm(o, tokKV[rows, 0, P * tl:P * tl + P], tokKV[rows, 1, P * tl:P * tl + P], False, True)
                        done(("dS", cc) + n, last)
                    b = start(("Y",) + n)
                    for tl, t in enumerate(tiles):
                        for cc in range(2):
                            c = 2 * tt + cc
                            mm(b[:, P * tl + 64 * cc:P * tl + 64 * cc + 64], Sb[c % 3][:, t, :],
                               pT[:, RW0 + t, c * C:c * C + C], cc == 0, True, skip_group_check=True)
                        for hp in range(2):
                            u, j = 2 * hp + tl, 2 * tl + hp
                            o = b[64 * hp:64 * hp + 64, P * tl:P * tl + P]
                            mm(o, Us[:, j, :], RB[:, u, :], False, True, skip_group_check=True)
                            last = mm(o, tokKV[:, 1, 64 * j:64 * j + 64], RK[:, u, :], False, True, skip_group_check=True)
                    done(("Y",) + n, last)
            pe.wait_ge(sem("S_ready"), 8)
            b = start("wkv_out")
            for t in range(4):
                last = tr(b[:, P * t:P * t + P], Sb[1][:, t, :])
            done("wkv_out", last)
            gone(pe, ("ys", 0))
            gone(pe, ("ys", 1))
            gone(pe, ("Y", 1, 0))
            gone(pe, ("Y", 1, 1))
            for t in range(4):
                b = start(("gm", t))
                done(("gm", t), mm(b[:, 0:T], blk64[:], T1[:, t, :], True, True))
            over_heads("gv", T2, "y_sq", blk64)

            for br in range(3):
                src0 = (Q0, MQ0, RW0)[br]
                arrived(pe, ("wo", br))
                wo_ = slot(("wo", br)).rearrange("p (k n) -> p k n", k=4)
                if br == 0:
                    for g4 in range(4):
                        gone(pe, ("so", g4))
                    gone(pe, "so_sT")
                elif br == 1:
                    for h in range(MH):
                        gone(pe, ("mo", h))
                    gone(pe, "mo_sT")
                else:
                    pe.wait_ge(sem("rw_done"), 1)
                for dt in range(KT):
                    if dt % 4 == 0:
                        arrived(pe, ("gate", br, dt // 4))
                    wg = slot(("gate", br, dt // 4)).rearrange("p (k n) -> p k n", k=KT)
                    b = start(("gate", br, dt))
                    j = (dt % 4) * P
                    for k in range(KT):
                        last = mm(b[:, 0:T], wg[:, k, j:j + P], xT[:, k, :], k == 0, k == KT - 1)
                    done(("gate", br, dt), last)
                    b = start(("o", br, dt))
                    for k in range(4):
                        last = mm(b[:, 0:T], wo_[:, k, dt * P:dt * P + P], pT[:, src0 + k, :], k == 0, k == 3)
                    done(("o", br, dt), last)
            pe.wait_ge(sem("merged"), 1)
            bs = {}
            for half2 in range(2):
                arrived(pe, ("wout", half2))
                w = slot(("wout", half2)).rearrange("p (k n) -> p k n", k=4)
                for tt, (t0, rows) in enumerate(TOK):
                    for half in range(2):
                        nm = ("res", tt, half)
                        if half2 == 0:
                            bs[nm] = start(nm)
                        for k in range(4):
                            last = mm(bs[nm][0:rows, :], mergedT[:, 4 * half2 + k, t0:t0 + rows],
                                      w[:, k, 512 * half:512 * half + 512], half2 == 0 and k == 0, half2 == 1 and k == 3)
                        if half2 == 1:
                            done(nm, last)
            for tt, (t0, rows) in enumerate(TOK):
                pe.wait_ge(sem("h1"), tt + 1)
                for j in range(2):
                    b = start(("h1T", tt, j))
                    for k in range(4):
                        kk = 4 * j + k
                        last = tr(b[:, P * k:P * k + rows], h1[0:rows, tt, kk * P:kk * P + P], rows)
                    done(("h1T", tt, j), last)
            pe.wait_ge(sem("ln_in"), 144)
            for tt, (t0, rows) in enumerate(TOK):
                for j in range(2):
                    gone(pe, ("h1T", tt, j))
                b = start(("logit", tt))
                for k in range(KT):
                    last = mm(b[0:rows, 0:NE], h1T[:, k, t0:t0 + rows], wr[:, k, :], k == 0, k == KT - 1)
                done(("logit", tt), last)
            pe.wait_ge(sem("sel_ready"), 1)
            b = start("rank")
            for tt, (t0, rows) in enumerate(TOK):
                o = b[0:rows, NE * tt:NE * tt + NE]
                for t2 in range(tt):
                    mm(o, ones[:, 0:rows], sel[:, t2, 0:NE], t2 == 0, False)
                mm(o, tri_lt[0:rows, 0:rows], sel[0:rows, tt, 0:NE], tt == 0, True)
            for tt, (t0, rows) in enumerate(TOK):
                last = mm(b[:, 96:96 + NE], ones[0:rows, :], sel[0:rows, tt, 0:NE], tt == 0, tt == 2)
            done("rank", last)
            b = start(("bT", 0))
            for tt, (t0, rows) in enumerate(TOK):
                last = tr(b[0:NE, t0:t0 + rows], wt[0:rows, tt, 0:NE], rows)
            done(("bT", 0), last)
            gone(pe, ("bT", 0))
            for tt, (t0, rows) in enumerate(TOK):
                for half in range(2):
                    b = start(("bd", tt, half))
                    done(("bd", tt, half), mm(b[0:rows, :], wTt[0:NE, t0:t0 + rows], bdrow[0:NE, 512 * half:512 * half + 512], True, True))

            for b in range(8):
                if opened[b]:
                    pe.wait_ge(free[b], opened[b])

            def gather(n_before):
                pe.wait_ge(sem("oneh_ready"), n_before + 1)
                for k in range(KT):
                    for tt, (t0, rows) in enumerate(TOK):
                        last = mm(bank[k // 4][:, (k % 4) * P:(k % 4) * P + P], h1[0:rows, tt, k * P:k * P + P],
                                  oneh[0:rows, tt].rearrange("p a b -> p (a b)"), tt == 0, tt == 2)
                last.then_inc(sem("gathered"), 1)

            def up(it, c, ei, j):
                s = (n_stream + c) % RING
                u = 4 * ei + j
                pe.wait_ge(sem(f"expert{s}_landed"), it * 48 + 16 * (c // RING + 1))
                w = ring[:, s, :].rearrange("p (k n) -> p k n", k=KT)
                for k in range(KT + 1):
                    for hf in range(2):
                        o = bank[2 + j % 2][64 * hf:64 * hf + 64, 0:256]
                        if k < KT:
                            mm(o, xg[:, k, CAP * ei:CAP * ei + CAP], w[:, k, 256 * hf:256 * hf + 256], k == 0, False)
                        else:
                            last = mm(o, pick_e[ei], bup[:, 512 * j + 256 * hf:512 * j + 256 * hf + 256], False, True)
                last.then_inc(sem("up_full"), 1)

            def turn(it, ei, j):
                u = 4 * ei + j
                pe.wait_ge(sem("h_ready"), it * 8 + (u + 1))
                if u == 0:
                    pe.wait_ge(sem("scatter_added"), it * 6 + 1)
                elif j >= 2:
                    pe.wait_ge(sem("hT_ready"), it * 8 + (u - 1))
                tr(bank[6 + j % 2][:, 0:P], hb[j % 2]).then_inc(sem("h_turned"), 1)

            def down(it, c, ei, j):
                s = (n_stream + c) % RING
                pe.wait_ge(sem(f"expert{s}_landed"), it * 48 + 16 * (c // RING + 1))
                w = ring[:, s, :].rearrange("p (k n) -> p k n", k=4)
                for k in range(4):
                    kf = 4 * j + k
                    if kf % 2 == 0:
                        pe.wait_ge(sem("hT_ready"), it * 8 + (4 * ei + kf // 2 + 1))
                    for half in range(2):
                        r0 = 64 * (half ^ ei)
                        last = mm(bank[4 + half][r0:r0 + 64, :], hT[ei][:, kf, :],
                                  w[:, k, 512 * half:512 * half + 512], kf == 0, kf == KT - 1)
                last.then_inc(sem("down_full"), 1)

            def pair(it, gathers):
                pe.wait_ge(sem("xg_ready"), gathers * 2)
                pe.wait_ge(sem("pick_ready"), it + 1)
                for ei in range(2):
                    c = 6 * ei
                    up(it, c, ei, 0)
                    up(it, c + 1, ei, 1)
                    turn(it, ei, 0)
                    up(it, c + 2, ei, 2)
                    turn(it, ei, 1)
                    up(it, c + 3, ei, 3)
                    turn(it, ei, 2)
                    down(it, c + 4, ei, 0)
                    turn(it, ei, 3)
                    down(it, c + 5, ei, 1)
                gather(gathers)
                pe.wait_ge(sem("onew_ready"), it + 1)
                for tt, (t0, rows) in enumerate(TOK):
                    last = tr(bank[2][:, t0:t0 + rows], onew[0:rows, tt].rearrange("p a b -> p (a b)"), rows)
                last.then_inc(sem("onewT_full"), 1)
                pe.wait_ge(sem("onewT_ready"), it + 1)
                pe.wait_ge(sem("y_moved"), it + 1)
                for i in range(6):
                    tt, half = i // 2, i % 2
                    t0, rows = TOK[tt]
                    pe.wait_ge(sem("scatter_added"), it * 6 + (max(i - 1, 0) + 1))
                    mm(bank[6 + i % 2][0:rows, :], onewT[:, t0:t0 + rows], ysb[:, 512 * half:512 * half + 512],
                       True, True).then_inc(sem("scatter_full"), 1)

            pe.wait_ge(sem("bias_up_in"), 16)
            pe.sem_inc(sem("onewT_full"), 1)
            gather(0)
            with pe.Fori(0, NE // 2) as p:
                pair(p, p + 1)
            pe.wait_ge(sem("flag_ready"), 1)
            over = pe.value_load(flag[0:1, 0:1], min_val=0, max_val=T)
            with pe.If(over > CAP):
                with pe.Fori(0, ROUNDS) as r:
                    gather((r + 1) * (NE // 2 + 1))
                    with pe.Fori(0, NE // 2) as p:
                        pair((r + 1) * (NE // 2) + p, (r + 1) * (NE // 2 + 1) + p + 1)

        @block.scalar
        def _(act):
            link = Chain(act, sem("act_chain"))

            def move(name, dst, src_of, func=ACT.Copy, **k):
                b = take(act, name)
                act.activation(dst, src_of(b), func, **k).then_inc(freed_by(name), 1)

            for k in range(0, KT, 2):
                move(("xT", k), xT[:, k, :], lambda b: b[:, 0:T])
            for k in range(0, KT, 2):
                move(("memT", k), memT[:, k, 0:NP_TOK], lambda b: b[:, 0:NP_TOK])
            for ft in range(FT):
                move(("p", ft), pT[:, ft, :], lambda b: b[:, 0:T])
            gone(act, "params")
            for h in range(MH):
                move(("mk", h), mkT[:, h, :], lambda b: b[:, 0:NP_TOK])
            for tt in range(2):
                move(("mv", tt), mvtok[:, tt, :], lambda b: b[:, :])
            for tt, (t0, rows) in enumerate(TOK):
                move(("kt", tt), ktok[0:rows, tt, :], lambda b: b[0:rows, :])
                move(("vt", tt), vtok[0:rows, tt, :], lambda b: b[0:rows, :])
            for tt in range(2):
                move(("mkt", tt), mktok[:, tt, :], lambda b: b[:, :])
            for j in range(4):
                w = min(512, RWT * P - 512 * j)
                move(("shift_out", j), shout[0:9, 512 * j:512 * j + w], lambda b: b[0:9, 0:w])

            act.wait_ge(sem("negabs_s"), 1)
            link(act.activation(sa_, sa_, ACT.Exp))
            act.activation(sa_, sa_, ACT.Ln, bias=1.0).then_inc(sem("ln_s"), 1)
            act.wait_ge(sem("arg_s"), 2)
            zsf = zs[:].rearrange("p b n h -> p (b n h)")
            act.activation(zsf, sa_, ACT.Exp).then_inc(sem("w_s"), 1)
            for g4 in range(4):
                for hp in range(2):
                    h = 2 * g4 + hp
                    move(("z", g4, hp), zp[:, hp, :], lambda b: b[:, 0:384], ACT.Identity, scale=SB_SCALE, bias=sb_bias[:, h:h + 1])
                act.wait_ge(sem("negabs_p"), g4 + 1)
                link(act.activation(np_, np_, ACT.Exp))
                act.activation(np_, np_, ACT.Ln, bias=1.0).then_inc(sem("ln_p"), 1)
                act.wait_ge(sem("arg_p"), g4 + 1)
                act.activation(wp_, zp, ACT.Exp).then_inc(sem("exp_p"), 1)
                move(("so", g4), pT[:, Q0 + g4, 0:256], lambda b: b[:, 0:256])
            for h in range(MH):
                act.wait_ge(sem("mem_max"), h + 1)
                b = take(act, ("mz", h))
                for qt in range(2):
                    ins = act.activation(mp[:, qt, :], b[:, 256 * qt:256 * qt + 256], ACT.Exp, scale=MEM_SCALE,
                                         bias=mst[:, 2 + qt:3 + qt], accum_out=mst[:, 4 + qt:5 + qt])
                ins.then_inc(freed_by(("mz", h)), 1)
                move(("mpT", h), mpT.rearrange("p a b -> p (a b)"), lambda b: b[:, :])
                move(("mo", h), pT[:, MQ0 + h, 0:256], lambda b: b[:, 0:256])
            move("so_s", orow[0:NB, :], lambda b: b[0:NB, :])
            move("so_sT", pT[:, Q0:Q0 + 4, NP_TOK:T], lambda b: b[:, 0:32].rearrange("p (t b) -> p t b", t=4))
            act.wait_ge(sem("mem_max_s"), 1)
            b = take(act, "mzT")
            act.activation(mps[0:32, :], b[0:32, 0:256], ACT.Exp, scale=MEM_SCALE, bias=mst[0:32, 8:9],
                           accum_out=mst[0:32, 9:10]).then_inc(freed_by("mzT"), 1)
            move("mpTs", mpTs.rearrange("p a b -> p (a b)"), lambda b: b[:, 0:64])
            move("mo_s", orow[0:NB, :], lambda b: b[0:NB, :])
            move("mo_sT", pT[:, MQ0:MQ0 + 4, NP_TOK:T], lambda b: b[:, 0:32].rearrange("p (t b) -> p t b", t=4))

            act.wait_ge(sem("mixed"), 1)
            act.activation(pT[0:64, 28, :], pT[0:64, 28, :], ACT.Tanh).then_inc(sem("lora_act"), 1)
            act.activation(pT[:, 29, :], pT[:, 29, :], ACT.Sigmoid).then_inc(sem("lora_act"), 1)
            for t in range(4):
                move(("dec", t), LD[:, t, :], lambda b: b[:, 0:T], ACT.Sigmoid, bias=col(DE0 + t))
            for t in range(4):
                move(("aaa", t), AA[:, t, :], lambda b: b[:, 0:T], ACT.Sigmoid, bias=col(AA0 + t))
            for t in range(4):
                move(("gr", t), GG[:, t, :], lambda b: b[:, 0:T])
            for t in range(4):
                move(("kn", t), T2[:, t, :], lambda b: b[:, 0:T], ACT.Sqrt)
            act.wait_ge(sem("cum"), 1)
            act.activation(T2[:, :, 0:256], T2[:, :, 0:256], ACT.Exp)
            act.activation(LD[:, :, 256:T], LD[:, :, 256:T], ACT.Exp)
            act.activation(LD[:, :, 0:256], T1[:, :, 0:256], ACT.Exp).then_inc(sem("act_chain"), 1)
            link.at = link.at + 1
            act.wait_ge(sem("act_chain"), link.at)
            act.activation(T1[:, :, 0:256], T1[:, :, 0:256], ACT.Exp, scale=-1.0).then_inc(sem("decays"), 1)
            for t in range(4):
                move(("st", t), St[:, t].rearrange("p b v -> p (b v)"), lambda b: b[:, :])
            act.wait_ge(sem("hats"), 1)
            for hp in range(2):
                rows = slice(64 * hp, 64 * hp + 64)
                move(("ys", hp), T1[rows, :, 256:T], lambda b: b[rows, 0:32].rearrange("p (t b) -> p t b", t=4))
            for j in range(8):
                move(("so_out", j), SN[0:64, 4 * (j % 2):4 * (j % 2) + 4, j // 2, :],
                     lambda b: b[0:64, :].rearrange("p (i n) -> p i n", i=4))
            act.wait_ge(sem("arena_clear"), 2)
            for it in range(4):
                tt, hh = it // 2, it % 2
                n = (tt, hh)
                move(("tab",) + n, tokAB.rearrange("p a b -> p (a b)"), lambda b: b[:, :])
                move(("tkv",) + n, tokKV.rearrange("p a b -> p (a b)"), lambda b: b[:, :])
                for lv in range(5):
                    move(("X", lv) + n, Xm.rearrange("p a b -> p (a b)"), lambda b: b[:, :])
                move(("MV",) + n, MVs.rearrange("p a b -> p (a b)"), lambda b: b[:, 0:256])
                move(("Z",) + n, Zs.rearrange("p a b -> p (a b)"), lambda b: b[:, 0:256])
                move(("WT",) + n, WTs.rearrange("p a b -> p (a b)"), lambda b: b[:, 0:256])
                move(("Y",) + n, T1[:, 2 * hh:2 * hh + 2, tt * P:tt * P + P], lambda b: b[:, 0:256].rearrange("p (a b) -> p a b", a=2))
            move("wkv_out", Nm[0].rearrange("p a b -> p (a b)"), lambda b: b[:, :])
            for t in range(4):
                move(("gv", t), T2[:, t, :], lambda b: b[:, 0:T], ACT.Sqrt, bias=eps[:, 0:1])

            act.wait_ge(sem("rw_done"), 1)
            for br in range(3):
                for dt in range(KT):
                    if (br, dt) >= (0, 2):
                        gone(act, ("o", (br * KT + dt - 2) // KT, (dt - 2) % KT))
                    move(("gate", br, dt), sig[:, dt % 2, :], lambda b: b[:, 0:T], ACT.Sigmoid)

            def norm_moments(i):
                act.wait_ge(sem("centred"), i + 1)
                tt = i % 3
                rows = TOK[tt][1]
                src = (h1 if i < 3 else yacc)
                link(act.activation(sq[0:rows, :], src[0:rows, tt, :], ACT.Square, accum_out=st_[0:rows, 8 * tt + 1:8 * tt + 2]))
                act.activation(st_[0:rows, 8 * tt + 2:8 * tt + 3], st_[0:rows, 8 * tt + 1:8 * tt + 2], ACT.Sqrt,
                               scale=1.0 / D, bias=eps[0:rows, 1:2]).then_inc(sem("deviation"), 1)

            for i in range(3):
                norm_moments(i)
            for tt, (t0, rows) in enumerate(TOK):
                for j in range(2):
                    move(("h1T", tt, j), h1T[:, 4 * j:4 * j + 4, t0:t0 + rows],
                         lambda b: b[:, :].rearrange("p (k n) -> p k n", k=4)[:, :, 0:rows])
            for tt, (t0, rows) in enumerate(TOK):
                act.wait_ge(sem("logits"), tt + 1)
                act.activation(tmpE[0:rows, tt, 0:NE], lg[0:rows, tt, 0:NE], ACT.Exp, bias=st_[0:rows, 8 * tt:8 * tt + 1]
                               ).then_inc(sem("exp_logits"), 1)
            move(("bT", 0), wTt[0:NE, :], lambda b: b[0:NE, 0:T])

            def gathered_rows(n_before):
                act.wait_ge(sem("gathered"), n_before + 1)
                for i in range(2):
                    act.activation(xg[:, 4 * i:4 * i + 4, :], bank[i][:, :].rearrange("p (k n) -> p k n", k=4),
                                   ACT.Copy).then_inc(sem("xg_ready"), 1)

            def pair(it, gathers):
                def gate(u):
                    act.wait_ge(sem("g_ready"), it * 8 + (u + 1))
                    act.activation(sg[u % 2], gb[u % 2], ACT.Sigmoid, scale=SWA).then_inc(sem("sg_ready"), 1)

                def turned(u):
                    act.wait_ge(sem("h_turned"), it * 8 + (u + 1))
                    ei, j = u // 4, u % 4
                    act.activation(hT[ei][:, 2 * j:2 * j + 2, :], bank[6 + j % 2][:, 0:P].rearrange("p (a b) -> p a b", a=2),
                                   ACT.Copy).then_inc(sem("hT_ready"), 1)

                for u in (0, 4):
                    gate(u)
                    gate(u + 1)
                    turned(u)
                    gate(u + 2)
                    turned(u + 1)
                    gate(u + 3)
                    turned(u + 2)
                    turned(u + 3)
                act.wait_ge(sem("down_full"), it * 4 + 4)
                act.activation(ysb[:, 0:512], bank[4][:, :], ACT.Copy)
                act.activation(ysb[0:64, 512:D], bank[5][64:128, :], ACT.Copy)
                act.activation(ysb[64:128, 512:D], bank[5][0:64, :], ACT.Copy).then_inc(sem("y_moved"), 1)
                gathered_rows(gathers)
                act.wait_ge(sem("onewT_full"), it + 2)
                act.activation(onewT, bank[2][:, 0:T], ACT.Copy).then_inc(sem("onewT_ready"), 1)

            gathered_rows(0)
            with act.Fori(0, NE // 2) as p:
                pair(p, p + 1)
            act.wait_ge(sem("flag_ready"), 1)
            over = act.value_load(flag[0:1, 0:1], min_val=0, max_val=T)
            with act.If(over > CAP):
                with act.Fori(0, ROUNDS) as r:
                    gathered_rows((r + 1) * (NE // 2 + 1))
                    with act.Fori(0, NE // 2) as p:
                        pair((r + 1) * (NE // 2) + p, (r + 1) * (NE // 2 + 1) + p + 1)
            for i in range(3, 6):
                norm_moments(i)

        @block.vector
        def _(v):
            link = Chain(v, sem("dve_chain"))
            tt_, ts, stt = v.tensor_tensor, v.tensor_scalar, v.scalar_tensor_tensor

            def move(name, dst, src_of):
                b = take(v, name)
                v.tensor_copy(dst, src_of(b)).then_inc(freed_by(name), 1)

            for k in range(1, KT, 2):
                move(("xT", k), xT[:, k, :], lambda b: b[:, 0:T])
            for k in range(1, KT, 2):
                move(("memT", k), memT[:, k, 0:NP_TOK], lambda b: b[:, 0:NP_TOK])
            move("params", pcol[:], lambda b: b[:, 0:42])
            move("shift_in", shT[:].rearrange("p t b -> p (t b)"), lambda b: b[:, 0:RWT * NB])

            for b_ in range(NB):
                q = take(v, ("qb", b_))
                for half in range(2):
                    name = ("K", 2 * b_ + half)
                    arrived(v, name)
                    k = slot(name).rearrange("p (n f) -> p n f", n=8)
                    prod_ = tt_(k, k, q[:, :].unsqueeze(1).to_broadcast([P, 8, W5]), ALU.mult)
                    if half:
                        prod_.then_inc(freed_by(("qb", b_)), 1)
                        gone(v, ("qb", b_))
                    else:
                        link(prod_)
                    v.tensor_reduce(zs[:, b_, 8 * half:8 * half + 8, :], slot(name).rearrange("p (n h d) -> p n h d", n=8, h=SBH),
                                    AX.X, ALU.add).then_inc(sem("k_used"), 1)
            for ft in range(RW0, FT):
                gone(v, ("p", ft))
            v.tensor_copy(psh[:], pT[:, RW0:FT, 255:T]).then_inc(sem("shift_cut"), 1)
            v.wait_ge(sem("k_used"), 2 * NB)
            v.wait_ge(sem("bias_in"), 16)
            z2 = zs[:].rearrange("p b n h -> p (b n) h")
            link(stt(z2, z2, SB_SCALE, sb_bias[:].unsqueeze(1).to_broadcast([P, NB * PAGES, SBH]), ALU.mult, ALU.add))
            zsf = zs[:].rearrange("p b n h -> p (b n h)")
            stt(sa_, zsf, -1.0, zsf, ALU.mult, ALU.min).then_inc(sem("negabs_s"), 1)
            v.wait_ge(sem("ln_s"), 1)
            link(stt(sb_, zsf, 0.0, sa_, ALU.max, ALU.add))
            link(v.memset(spx[:, :, PAGES - 1, :], 0.0))
            spv = sb_.rearrange("p (b n h) -> p b n h", b=NB, n=PAGES)
            for n in range(PAGES - 2, -1, -1):
                ins = tt_(spx[:, :, n, :], spx[:, :, n + 1, :], spv[:, :, n + 1, :], ALU.add)
                if n:
                    link(ins)
                else:
                    ins.then_inc(sem("sp_s"), 1)
            for i in range(2):
                b = take(v, ("cs_s", i))
                c = slice(512 * i, 512 * i + 512)
                ins = tt_(sa_[:, c], zsf[:, c], b[:, :], ALU.subtract)
                ins.then_inc(freed_by(("cs_s", i)), 1)
            for i in range(2):
                gone(v, ("cs_s", i))
            v.sem_inc(sem("arg_s"), 2)

            v.wait_ge(sem("tri_ready"), 1)
            tri2 = tri_lt[:].unsqueeze(1).to_broadcast([P, 2, P])

            def causal(buf):
                tt_(buf[:, :, 0:128], buf[:, :, 0:128], tri2, ALU.mult)
                return tt_(buf[:, :, 256:384], buf[:, :, 256:384], tri2, ALU.mult)

            def keep_own(bq):
                b = take(v, ("pv", bq))
                if bq >= 2:
                    v.wait_ge(sem("pv_summed"), bq - 1)
                tt_(pvm[bq % 2], b[:, :], m_page[:], ALU.mult).then_inc(freed_by(("pv", bq)), 1)
                gone(v, ("pv", bq))
                v.sem_inc(sem("pv_kept"), 1)

            v.wait_ge(sem("masks"), 7)
            for g4 in range(4):
                for hp in range(2):
                    gone(v, ("z", g4, hp))
                stt(np_, zp, -1.0, zp, ALU.mult, ALU.min).then_inc(sem("negabs_p"), 1)
                v.wait_ge(sem("ln_p"), g4 + 1)
                link(stt(sp_, zp, 0.0, np_, ALU.max, ALU.add))
                causal(sp_).then_inc(sem("sp_p"), 1)
                keep_own(g4)
                for hp in range(2):
                    b = take(v, ("cs", g4, hp))
                    tt_(zp[:, hp, :], zp[:, hp, :], b[:, 0:384], ALU.subtract).then_inc(freed_by(("cs", g4, hp)), 1)
                for hp in range(2):
                    gone(v, ("cs", g4, hp))
                ts(zp, zp, 0.0, None, ALU.min).then_inc(sem("arg_p"), 1)
                v.wait_ge(sem("exp_p"), g4 + 1)
                causal(wp_).then_inc(sem("w_p"), 1)

            for h in range(MH):
                b = take(v, ("mz", h))
                link(v.reduce_max(mst[:, 0:2], b[:, :].rearrange("p (a b) -> p a b", a=2), AX.X))
                ts(mst[:, 2:4], mst[:, 0:2], -MEM_SCALE, None, ALU.mult).then_inc(sem("mem_max"), 1)
                gone(v, ("mz", h))
                link(v.reciprocal(mst[:, 6:8], mst[:, 4:6]))
                for qt in range(2):
                    ins = ts(mp[:, qt, :], mp[:, qt, :], mst[:, 6 + qt:7 + qt], None, ALU.mult)
                ins.then_inc(sem("mp"), 1)
                keep_own(4 + h)
            for b_ in range(NB):
                name = ("mK", b_ // 4)
                q = take(v, ("mqb", b_))
                arrived(v, name)
                k = slot(name).rearrange("p (b m f) -> p b m f", b=4, m=2)[:, b_ % 4]
                tt_(k, k, q[:, :].unsqueeze(1).to_broadcast([P, 2, W5]), ALU.mult).then_inc(freed_by(("mqb", b_)), 1)
                gone(v, ("mqb", b_))
                ins = v.tensor_reduce(zm[:, :, MH * b_:MH * b_ + MH], k.rearrange("p m (h d) -> p m h d", h=MH), AX.X, ALU.add)
                if b_ % 4 == 3:
                    ins.then_inc(sem("mk_used"), 1)
                else:
                    link(ins)
            v.wait_ge(sem("mk_used"), 2)
            v.sem_inc(sem("zm"), 1)
            b = take(v, "mzT")
            link(v.reduce_max(mst[0:32, 10:11], b[0:32, 0:256], AX.X))
            ts(mst[0:32, 8:9], mst[0:32, 10:11], -MEM_SCALE, None, ALU.mult).then_inc(sem("mem_max_s"), 1)
            gone(v, "mzT")
            link(v.reciprocal(mst[0:32, 11:12], mst[0:32, 9:10]))
            ts(mps[0:32, :], mps[0:32, :], mst[0:32, 11:12], None, ALU.mult).then_inc(sem("mps"), 1)
            v.wait_ge(*full_of("so_s"))
            for i in range(2):
                b = take(v, ("mpv", i))
                tt_(pvm[i], b[:, :], m_mem[i], ALU.mult).then_inc(freed_by(("mpv", i)), 1)

            v.wait_ge(*full_of("mo_sT"))
            v.wait_ge(sem("arena_clear"), 1)
            v.sem_inc(sem("rw_clear"), 1)
            for g0 in range(0, RWT, 4):
                n = min(4, RWT - g0)
                p = pT[:, RW0 + g0:RW0 + g0 + n, :]
                d = T1[:, 0:n, :]
                tt_(d[:, :, 1:256], p[:, :, 0:255], p[:, :, 1:256], ALU.subtract)
                ts(d[:, :, 0:1], p[:, :, 0:1], -1.0, None, ALU.mult)
                link(tt_(d[:, :, 256:T], shT[:, g0:g0 + n, :], p[:, :, 256:T], ALU.subtract))
                for i in range(n):
                    ins = stt(p[:, i, :], d[:, i, :], col(MU + g0 + i), p[:, i, :], ALU.mult, ALU.add)
                link(ins)
            v.sem_inc(sem("mixed"), 1)
            R, Kx, Vx = pT[:, RW0:RW0 + 4, :], pT[:, 20:24, :], pT[:, 24:28, :]

            def per_tile(dst, src, c0, op=ALU.mult, op1=None, s2=None):
                for t in range(4):
                    if op1 is None:
                        ins = ts(dst[:, t, :], src[:, t, :], col(c0 + t), None, op)
                    else:
                        ins = ts(dst[:, t, :], src[:, t, :], s2, col(c0 + t), op, op1)
                return ins

            link(per_tile(KK, Kx, KKp))
            tt_(T1, KK, KK, ALU.mult).then_inc(sem("kk_sq"), 1)
            for t in range(4):
                gone(v, ("kn", t))
            link(ts(T2, T2, 1e-12, None, ALU.max))
            link(v.reciprocal(T2, T2))
            link(tt_(KK, KK, T2, ALU.mult))
            for t in range(4):
                gone(v, ("aaa", t))
            link(per_tile(T2, AA, KAp, ALU.add, ALU.mult, -1.0))
            link(stt(KM, T2, 1.0, Kx, ALU.add, ALU.mult))
            link(tt_(T1, R, KM, ALU.mult))
            per_tile(T1, T1, RKp).then_inc(sem("rk_prod"), 1)
            link(ts(LD, LD, DECAY, None, ALU.mult))
            for t in range(4):
                b = take(v, ("bon", t))
                tt_(BON[:, t, :], b[:, 0:T], Vx[:, t, :], ALU.mult).then_inc(freed_by(("bon", t)), 1)
            link(tt_(AA, KK, AA, ALU.mult))
            v.wait_ge(sem("masks"), 7)
            for t in range(4):
                ins = v.tensor_tensor_scan(T1[:, t, 0:256], scanm[:], LD[:, t, 0:256], 0.0, ALU.mult, ALU.add)
            link(ins)
            tt_(T2[:, :, 0:256], T1[:, :, 0:256], LD[:, :, 0:256], ALU.subtract).then_inc(sem("cum"), 1)
            v.wait_ge(sem("decays"), 1)
            pr = slice(0, 256)
            stt(KK[:, :, pr], KK[:, :, pr], -1.0, T2[:, :, pr], ALU.mult, ALU.mult)
            tt_(AA[:, :, pr], AA[:, :, pr], T1[:, :, pr], ALU.mult)
            tt_(KM[:, :, pr], KM[:, :, pr], T1[:, :, pr], ALU.mult)
            tt_(R[:, :, pr], R[:, :, pr], LD[:, :, pr], ALU.mult).then_inc(sem("hats"), 1)

            sv = lambda a: a[:, :, NP_TOK:T].unsqueeze(3).to_broadcast([P, 4, NB, 64])
            sv1 = lambda a, t: a[:, t, NP_TOK:T].unsqueeze(2).to_broadcast([P, NB, 64])
            for t in range(4):
                gone(v, ("st", t))
            for t in range(4):
                ins = tt_(S1[:, t], St[:, t], sv1(KK, t), ALU.mult)
            ins.then_inc(sem("s_kk"), 1)
            for t in range(4):
                ins = tt_(S2[:, t], idd[:].unsqueeze(1).to_broadcast([P, NB, 64]), sv1(Vx, t), ALU.mult)
            ins.then_inc(sem("s_v"), 1)
            for t in range(4):
                ins = tt_(St[:, t], St[:, t], sv1(LD, t), ALU.mult)
            link(ins)
            for nm, coef, op in (("sa", AA, ALU.subtract), ("vb", KM, ALU.add)):
                for t in range(4):
                    b = take(v, (nm, t))
                    tt_(S1[:, t], b[:, :].rearrange("p (b v) -> p b v", b=NB), sv1(coef, t), ALU.mult).then_inc(freed_by((nm, t)), 1)
                for t in range(4):
                    gone(v, (nm, t))
                for t in range(4):
                    ins = tt_(St[:, t], St[:, t], S1[:, t], op)
                if nm == "sa":
                    link(ins)
                else:
                    ins.then_inc(sem("s_new"), 1)

            v.wait_ge(sem("arena_clear"), 2)
            v.memset(Sb[0], 0.0).then_inc(sem("S_zero"), 1)
            v.wait_ge(sem("S_zero"), 1)
            m2 = lambda m: m[:].unsqueeze(1).to_broadcast([P, 2, P])
            m4 = lambda m: m[:].unsqueeze(1).to_broadcast([P, 4, P])
            for it in range(4):
                tt, hh = it // 2, it % 2
                n = (tt, hh)
                part = lambda b, i: b[:, 256 * i:256 * i + 256].rearrange("p (a b) -> p a b", a=2)
                for hp in range(2):
                    u = slice(2 * hp, 2 * hp + 2)
                    b = take(v, ("g1", hp) + n)
                    tt_(Nl[:, u], part(b, 1), m2(m_lo), ALU.mult)
                    tt_(Nt[:, u], part(b, 0), m2(m_up), ALU.mult).then_inc(freed_by(("g1", hp) + n), 1)
                for hp in range(2):
                    gone(v, ("g1", hp) + n)
                tt_(Tm, Nl, m4(lev[0]), ALU.mult)
                link(tt_(Tt, Nt, m4(lev[0]), ALU.mult))
                tt_(Tm, Tm, m4(ident), ALU.add)
                tt_(Tt, Tt, m4(ident), ALU.add).then_inc(sem("T_ready"), 1)
                for hp in range(2):
                    u = slice(2 * hp, 2 * hp + 2)
                    b = take(v, ("g2", hp) + n)
                    tt_(RB[:, u], part(b, 0), m2(m_upi), ALU.mult)
                    tt_(AK[:, u], part(b, 1), m2(m_up), ALU.mult).then_inc(freed_by(("g2", hp) + n), 1)
                    b = take(v, ("g3", hp) + n)
                    tt_(RK[:, u], part(b, 0), m2(m_upi), ALU.mult).then_inc(freed_by(("g3", hp) + n), 1)
                v.wait_ge(sem("T_ready"), it + 1)
                for lv in range(5):
                    if lv < 4:
                        b = take(v, ("TX", lv) + n)
                        tt_(Tm, Tm, b[:, :].rearrange("p (a b) -> p a b", a=4), ALU.add).then_inc(freed_by(("TX", lv) + n), 1)
                        gone(v, ("TX", lv) + n)
                    b = take(v, ("XT", lv) + n)
                    tt_(Tt, Tt, b[:, :].rearrange("p (a b) -> p a b", a=4), ALU.add).then_inc(freed_by(("XT", lv) + n), 1)
                    gone(v, ("XT", lv) + n)
                gone(v, ("Z",) + n)
                for cc in range(2):
                    c = 2 * tt + cc
                    rows = slice(64 * cc, 64 * cc + 64)
                    for tl in range(2):
                        ins = ts(PM[:, tl, :], blk[:], LD[:, 2 * hh + tl, C * c + C - 1:C * c + C], None, ALU.mult)
                    link(ins)
                    b = take(v, ("U", cc) + n)
                    tt_(Us.rearrange("p a b -> p (a b)")[rows], b[rows, 0:256], Zs.rearrange("p a b -> p (a b)")[rows],
                        ALU.add).then_inc(freed_by(("U", cc) + n), 1)
                    b = take(v, ("dS", cc) + n)
                    tt_(tS, b[:, 0:256].rearrange("p (a b) -> p a b", a=2), Sb[c % 3][:, 2 * hh:2 * hh + 2, :],
                        ALU.add).then_inc(freed_by(("dS", cc) + n), 1)
                    gone(v, ("dS", cc) + n)
                    tt_(Sb[(c + 1) % 3][:, 2 * hh:2 * hh + 2, :], tS, PM, ALU.mult).then_inc(sem("S_ready"), 1)
                    v.wait_ge(sem("S_ready"), 2 * it + cc + 1)
            for t in range(4):
                b = take(v, ("gm", t))
                tt_(T1[:, t, :], T1[:, t, :], b[:, 0:T], ALU.subtract).then_inc(freed_by(("gm", t)), 1)
            for t in range(4):
                gone(v, ("gm", t))
            tt_(T2, T1, T1, ALU.mult).then_inc(sem("y_sq"), 1)
            for t in range(4):
                gone(v, ("gv", t))
            link(v.reciprocal(T2, T2))
            link(tt_(T1, T1, T2, ALU.mult))
            for t in range(4):
                ins = ts(T1[:, t, :], T1[:, t, :], col(GNG + t), col(GNB + t), ALU.mult, ALU.add)
            link(ins)
            link(tt_(T1, T1, BON, ALU.add))
            link(tt_(R, T1, GG, ALU.mult))
            v.sem_inc(sem("rw_done"), 3)

            for br in range(3):
                for dt in range(KT):
                    gone(v, ("gate", br, dt))
                    b = take(v, ("o", br, dt))
                    if br == 0:
                        tt_(mergedT[:, dt, :], b[:, 0:T], sig[:, dt % 2, :], ALU.mult).then_inc(freed_by(("o", br, dt)), 1)
                        gone(v, ("o", br, dt))
                    else:
                        tt_(prod, b[:, 0:T], sig[:, dt % 2, :], ALU.mult).then_inc(freed_by(("o", br, dt)), 1)
                        gone(v, ("o", br, dt))
                        link(tt_(mergedT[:, dt, :], mergedT[:, dt, :], prod, ALU.add))
            v.sem_inc(sem("merged"), 1)

            def normalise(x, tt, i, g_, b_, ready):
                rows = TOK[tt][1]
                xr_ = x[0:rows, tt, :]
                s = lambda j: st_[0:rows, 8 * tt + j:8 * tt + j + 1]
                link(v.reduce_sum(s(0), xr_, AX.X))
                link(ts(s(3), s(0), 1.0 / D, None, ALU.mult))
                ts(xr_, xr_, s(3), None, ALU.subtract).then_inc(sem("centred"), 1)
                v.wait_ge(sem("deviation"), i + 1)
                link(v.reciprocal(s(4), s(2)))
                link(stt(xr_, xr_, s(4), g_[0:rows, :], ALU.mult, ALU.mult))
                tt_(xr_, xr_, b_[0:rows, :], ALU.add).then_inc(sem(ready), 1)

            v.wait_ge(sem("ln_in"), 144)
            for tt, (t0, rows) in enumerate(TOK):
                for half in range(2):
                    b = take(v, ("res", tt, half))
                    c = slice(512 * half, 512 * half + 512)
                    stt(h1[0:rows, tt, c], xres[0:rows, tt, c], ALPHA, b[0:rows, :], ALU.mult, ALU.add
                        ).then_inc(freed_by(("res", tt, half)), 1)
                for half in range(2):
                    gone(v, ("res", tt, half))
                normalise(h1, tt, tt, lng, lnb, "h1")
            v.memset(pos, -1.0)
            link(v.memset(wt, 0.0))
            for tt, (t0, rows) in enumerate(TOK):
                s = lambda j, n=1: st_[0:rows, 8 * tt + j:8 * tt + j + n]
                L, E, S_, W_ = (a[0:rows, tt, 0:NE] for a in (lg, tmpE, sel, wt))
                b = take(v, ("logit", tt))
                tt_(L, b[0:rows, 0:NE], brt[0:rows, :], ALU.add).then_inc(freed_by(("logit", tt)), 1)
                gone(v, ("logit", tt))
                link(v.max(mx8[0:rows, 8 * tt:8 * tt + 8], L))
                m = lambda j: mx8[0:rows, 8 * tt + j:8 * tt + j + 1]
                ts(s(0), m(0), -1.0, None, ALU.mult).then_inc(sem("logits"), 1)
                link(ts(S_, L, m(3), None, ALU.is_gt))
                link(ts(W_, L, m(3), None, ALU.is_equal))
                link(v.reduce_sum(s(1), S_, AX.X))
                link(ts(s(2), s(1), -1.0, 4.0, ALU.mult, ALU.add))
                link(v.tensor_tensor_scan(pos[0:rows, tt, 0:NE], ones[0:rows, 0:NE], W_, 0.0, ALU.mult, ALU.add))
                link(stt(W_, pos[0:rows, tt, 0:NE], s(2), W_, ALU.is_le, ALU.mult))
                link(tt_(S_, S_, W_, ALU.add))
                v.wait_ge(sem("exp_logits"), tt + 1)
                link(tt_(E, E, S_, ALU.mult))
                link(v.reduce_sum(s(3), E, AX.X))
                link(v.reciprocal(s(4), s(3)))
                link(ts(W_, E, s(4), None, ALU.mult))
            v.sem_inc(sem("sel_ready"), 1)
            b = take(v, "rank")
            for tt, (t0, rows) in enumerate(TOK):
                link(stt(pos[0:rows, tt, 0:NE], b[0:rows, NE * tt:NE * tt + NE], 1.0, sel[0:rows, tt, 0:NE], ALU.add, ALU.mult))
                link(ts(pos[0:rows, tt, 0:NE], pos[0:rows, tt, 0:NE], -1.0, None, ALU.add))
            v.reduce_max(st_[:, 5:6], b[:, 96:96 + NE], AX.X).then_inc(freed_by("rank"), 1)
            gone(v, "rank")
            v.tensor_copy(flag[:], st_[:, 5:6]).then_inc(sem("flag_ready"), 1)
            for tt, (t0, rows) in enumerate(TOK):
                for half in range(2):
                    b = take(v, ("bd", tt, half))
                    v.tensor_copy(yacc[0:rows, tt, 512 * half:512 * half + 512], b[0:rows, :]).then_inc(freed_by(("bd", tt, half)), 1)
            for tt in range(3):
                for half in range(2):
                    gone(v, ("bd", tt, half))

            def one_hot(p, n_before, first=False):
                if not first:
                    v.wait_ge(sem("gathered"), n_before)
                tt_(oneh, iota[:].unsqueeze(1).unsqueeze(1).to_broadcast([P, 3, 2, CAP]),
                    pos[:, :, bass.ds(2 * p, 2)].unsqueeze(3).to_broadcast([P, 3, 2, CAP]), ALU.is_equal
                    ).then_inc(sem("oneh_ready"), 1)

            def pair(p, it, gathers):
                v.wait_ge(sem("onewT_full"), it + 1)
                v.wait_ge(sem("oneh_ready"), gathers)
                tt_(onew, oneh, wt[:, :, bass.ds(2 * p, 2)].unsqueeze(3).to_broadcast([P, 3, 2, CAP]), ALU.mult
                    ).then_inc(sem("onew_ready"), 1)
                v.wait_ge(sem("onew_ready"), it + 1)
                one_hot(p + 1, gathers)
                for ei in range(2):
                    ins = v.tensor_copy(pick_e[ei], ident[:, bass.ds(2 * p + ei, 1)].to_broadcast([P, CAP]))
                ins.then_inc(sem("pick_ready"), 1)
                for u in range(8):
                    ei, j = u // 4, u % 4
                    g_, l_, h_, s_ = gb[u % 2], lb[u % 2], hb[u % 2], sg[u % 2]
                    v.wait_ge(sem("up_full"), it * 8 + (u + 1))
                    chunk = bank[2 + j % 2]
                    ts(g_, chunk[:, 0:256:2], LIMIT, None, ALU.min).then_inc(sem("g_ready"), 1)
                    ts(l_, chunk[:, 1:256:2], LIMIT, -LIMIT, ALU.min, ALU.max).then_inc(sem("swiglu_step"), 1)
                    v.wait_ge(sem("swiglu_step"), it * 16 + (2 * u + 1))
                    v.wait_ge(sem("g_ready"), it * 8 + (u + 1))
                    stt(l_, l_, 1.0, g_, ALU.add, ALU.mult).then_inc(sem("swiglu_step"), 1)
                    v.wait_ge(sem("swiglu_step"), it * 16 + (2 * u + 2))
                    v.wait_ge(sem("sg_ready"), it * 8 + (u + 1))
                    tt_(h_, l_, s_, ALU.mult).then_inc(sem("h_ready"), 1)
                for i in range(6):
                    tt, half = i // 2, i % 2
                    rows = TOK[tt][1]
                    c = slice(512 * half, 512 * half + 512)
                    v.wait_ge(sem("scatter_full"), it * 6 + (i + 1))
                    v.wait_ge(sem("scatter_added"), it * 6 + (i + 1))
                    tt_(yacc[0:rows, tt, c], yacc[0:rows, tt, c], bank[6 + i % 2][0:rows, :], ALU.add
                        ).then_inc(sem("scatter_added"), 1)

            v.sem_inc(sem("scatter_added"), 1)
            one_hot(0, 0, True)
            with v.Fori(0, NE // 2) as p:
                pair(p, p, p + 1)
            v.wait_ge(sem("flag_ready"), 1)
            over = v.value_load(flag[0:1, 0:1], min_val=0, max_val=T)
            with v.If(over > CAP):
                with v.Fori(0, ROUNDS) as r:
                    ts(pos, pos, float(-CAP), None, ALU.add).then_inc(sem("pos_moved"), 1)
                    v.wait_ge(sem("pos_moved"), r + 1)
                    one_hot(0, (r + 1) * (NE // 2 + 1))
                    with v.Fori(0, NE // 2) as p:
                        pair(p, (r + 1) * (NE // 2) + p, (r + 1) * (NE // 2 + 1) + p + 1)
                v.wait_ge(sem("scatter_added"), 6 * (ROUNDS + 1) * (NE // 2) + 1)
            v.wait_ge(sem("scatter_added"), 6 * (NE // 2) + 1)
            for tt, (t0, rows) in enumerate(TOK):
                link(stt(yacc[0:rows, tt, :], h1[0:rows, tt, :], ALPHA, yacc[0:rows, tt, :], ALU.mult, ALU.add))
                normalise(yacc, tt, 3 + tt, ln2g, ln2b, "y_ready")


_INS = ["x_prompt", "x_sample", "cache_sb_k", "cache_sb_v", "cache_mem_k", "cache_mem_v", "state_rw_shift",
        "state_rw_wkv", "page_table", "mem_prompt", "w_in", "sb_bias", "mu_rw", "w_decay0", "w_decay2", "w_aaa0",
        "w_aaa2", "w_gate2", "rw_k_k", "rw_k_a", "rw_r_k", "rw_gn_g", "rw_gn_b", "w_mem_kv", "w_sb_o", "w_mem_o",
        "w_rw_o", "w_out", "ln1_g", "ln1_b", "w_router", "b_router", "w_gate_up", "b_gate_up", "w_down", "b_down",
        "ln2_g", "ln2_b"]
_OUTS = {"y_prompt": (1, 256, 1024), "y_sample": (8, 1, 1024), "sb_k_prompt": (1, 1, 256, 8, 64),
         "sb_v_prompt": (1, 1, 256, 8, 64), "mem_k": (1, 1, 256, 4, 128), "mem_v": (1, 1, 256, 4, 128),
         "shift_prompt": (1, 1, 1792), "wkv_prompt": (1, 1, 8, 64, 64), "sb_k_sample": (1, 8, 1, 8, 64),
         "sb_v_sample": (1, 8, 1, 8, 64), "shift_sample": (1, 8, 1792), "wkv_sample": (1, 8, 8, 64, 64)}


def kernel(**inputs):
    import concourse.bacc as bacc
    from concourse.bass_utils import run_bass_kernel_spmd

    nc = bacc.Bacc("TRN2", target_bir_lowering=False, num_devices=1)
    arrays, ins = {}, {}
    for name in _INS:
        a = np.ascontiguousarray(inputs[name])
        arrays[f"in_{name}"] = a
        ins[name] = nc.dram_tensor(f"in_{name}", a.shape, mybir.dt.from_np(a.dtype), kind="ExternalInput").ap()
    outs = {n: nc.dram_tensor(f"out_{n}", s, F32, kind="ExternalOutput").ap() for n, s in _OUTS.items()}
    build(nc, ins, outs)
    r = run_bass_kernel_spmd(nc, [arrays], core_ids=[0])
    return tuple(r.results[0][f"out_{n}"] for n in _OUTS)
```

```python
from contextlib import ExitStack

import numpy as np
import concourse.bass as bass
from concourse import mybir

F32 = mybir.dt.float32
I32 = mybir.dt.int32
ALU = mybir.AluOpType
ACT = mybir.ActivationFunctionType
AX = mybir.AxisListType

P = 128
D = 1024
KT = D // P
NP_TOK = 256
NB = 8
T = NP_TOK + NB
TOK = [(0, 128), (128, 128), (256, NB)]
H1_ORDER = (2, 0, 1)
PAGES = 16
N_PAGES = 160
SBH = 8
MH = 4
W5 = 512
RWT = 14
FT = 30
GATE0 = 3840
NE = 32
CAP = 64
ROUNDS = -(-T // CAP) - 1
SLOT = 4096
RING = 4
C = 64
ALPHA = 2.0 ** 0.25
SB_SCALE = 0.125
MEM_SCALE = 128.0 ** -0.5
GN_EPS = 64e-5
LN_EPS = 1e-5
DECAY = -float(np.exp(-0.5))
LIMIT = 7.0
SWA = 1.702

Q0, K0, V0, MQ0, RW0 = 0, 4, 8, 12, 16


def phase1_stream():
    s = [("win", 0)]
    for i in range(1, 8):
        s += [("win", i), ("K", 2 * i - 2), ("K", 2 * i - 1)]
    s += [("mkv", 0), ("K", 14), ("mkv", 1), ("K", 15)]
    s += [("V", i) for i in range(10)] + [("gate", 0, 0)]
    s += [("V", i) for i in range(10, 14)] + [("gate", 0, 1), ("V", 14), ("V", 15)]
    s += [("mK", 0), ("mK", 1), ("mV", 0), ("mV", 1)]
    s += [("wo", 0), ("gate", 1, 0), ("gate", 1, 1), ("wo", 1), ("gate", 2, 0), ("gate", 2, 1), ("wo", 2)]
    s += [("wout", 0), ("wout", 1)]
    return s


def beside():
    g = []
    for kind, br in (("gate", 0), ("o", 0), ("gate", 1), ("o", 1), ("gate", 2)):
        g += [(kind, br, dt) for dt in range(KT)]
    return g


GROUP_FIRST, GROUP_STEP = 160, 22
PLACES = {"start": (0, 4), "X0": (4, 6), "X1": (6, 8), "X2": (8, 10), "X3": (10, 12), "X4": (12, 14),
          "MV": (14, 16), "WT": (16, 18), "U0": (18, 20), "U1": (20, 22)}


def at_place(it, place):
    a, b = PLACES[place]
    return GROUP_FIRST + GROUP_STEP * it + a, GROUP_FIRST + GROUP_STEP * it + b


def ending_at(it, place):
    first, last = at_place(it, place)
    at, ends = 0, []
    for name in beside():
        at += KT if name[0] == "gate" else 4
        if first < at <= last:
            ends.append(name)
    return ends


def psum_plan():
    g = []
    add = lambda name, bank: g.append((name, bank))
    for k in range(KT):
        add(("xT", k), k)
    for c in range(8):
        if c == 2:
            for k in range(KT):
                add(("memT", k), k % 6)
            add("params", 0)
            add("shift_in", 1)
        if c:
            add(("qb", c - 1), 6 + (c - 1) % 2)
        for ft in range(4 * c, min(4 * c + 4, FT)):
            add(("p", ft), ft % 6)
    add(("qb", 7), 7)
    for h in range(MH):
        add(("mk", h), h)
    for tt in range(2):
        add(("mv", tt), 4 + tt)
    for tt in range(3):
        add(("kt", tt), tt)
        add(("vt", tt), 3 + tt)
    for tt in range(2):
        add(("mkt", tt), tt)
    for j in range(4):
        add(("shift_out", j), 2 + j)
    for i in range(2):
        add(("cs_s", i), i)
    for g4 in range(4):
        for hp in range(2):
            add(("z", g4, hp), hp)
        add(("pv", g4), 6 + g4 % 2)
        for hp in range(2):
            add(("cs", g4, hp), 2 + hp)
        if g4 == 0:
            add("so_s", 5)
        add(("so", g4), 4)
    for i, name in enumerate(beside()):
        add(name, (3, 7)[i % 2])
    for h in range(MH):
        add(("mz", h), h % 2)
        add(("pv", 4 + h), 6)
        add(("mpT", h), 2)
        add(("mo", h), 4)
    add("so_sT", 2)
    for b in range(NB):
        add(("mqb", b), b % 2)
    add("mzT", 2)
    add("mpTs", 4)
    for i in range(2):
        add(("mpv", i), 5 + i)
    add("mo_s", 4)
    add("mo_sT", 2)
    six = (0, 1, 2, 4, 5, 6)
    turn = 0
    for nm, n in (("dec", 4), ("aaa", 4), ("gr", 4), ("kn", 4), ("bon", 4), ("st", 4), ("sa", 4), ("vb", 4),
                  ("so_out", 8), ("ys", 2)):
        for t in range(n):
            add((nm, t), six[turn % 6])
            turn += 1
    for tt in range(2):
        for hh in range(2):
            n = (tt, hh)
            add(("tab",) + n, six[4])
            add(("tkv",) + n, six[5])
            for hp in range(2):
                add(("g1", hp) + n, six[hp])
            for hp in range(2):
                add(("g2", hp) + n, six[2 + hp])
            for hp in range(2):
                add(("g3", hp) + n, six[4 + hp])
            for lv in range(5):
                add(("X", lv) + n, six[0])
                if lv < 4:
                    add(("TX", lv) + n, six[1])
                add(("XT", lv) + n, six[2])
            add(("MV",) + n, six[3])
            add(("Z",) + n, six[4])
            add(("WT",) + n, six[5])
            for cc in range(2):
                add(("U", cc) + n, six[0])
                add(("dS", cc) + n, six[1])
            add(("Y",) + n, six[3])
    add("wkv_out", 0)
    for t in range(4):
        add(("gm", t), six[1 + t])
    for t in range(4):
        add(("gv", t), six[(5 + t) % 6])
    for dt in range(KT):
        add(("o", 2, dt), 6 + dt % 2)
    add("res_s", 4)
    for tt in range(2):
        for half in range(2):
            add(("res", tt, half), 2 * tt + half)
        tp = (2, 0)[tt]
        for j in range(2):
            add(("h1T", tp, j), 6 + j)
        add(("logit", tp), 5)
    for j in range(2):
        add(("h1T", 1, j), 6 + j)
    add(("logit", 1), 4)
    add("rank", 5)
    return g


class Groups:

    def __init__(self, plan):
        self.where, self.uses = {}, [0] * 8
        for name, bank in plan:
            assert name not in self.where, name
            self.where[name] = (bank, self.uses[bank])
            self.uses[bank] += 1


class Chain:

    def __init__(self, eng, sem):
        self.eng, self.sem, self.at, self.n = eng, sem, 0, 0

    def __call__(self, ins):
        ins.then_inc(self.sem, 1)
        self.at = self.at + 1
        self.n += 1
        self.eng.wait_ge(self.sem, self.at)


def build(nc, A, O):
    stream = phase1_stream()
    slot_of = {name: (n % RING, n // RING) for n, name in enumerate(stream)}
    n_stream = len(stream)
    G = Groups(psum_plan())

    ctx = ExitStack()
    with ctx:
        def sb(name, shape, dt=F32):
            return ctx.enter_context(nc.sbuf_tensor(name, shape, dt))

        sems = {}

        def sem(name):
            if name not in sems:
                sems[name] = ctx.enter_context(nc.semaphore(name))
            return sems[name]

        bank = [ctx.enter_context(nc.psum_tensor(f"bank{i}", [P, 512], F32)) for i in range(8)]
        full = [sem(f"bank{i}_full") for i in range(8)]
        free = [sem(f"bank{i}_free") for i in range(8)]
        landed = [sem(f"slot{i}_landed") for i in range(RING)]

        ring = sb("ring", [P, RING, SLOT])
        pT = sb("projT", [P, FT, T])
        xT = sb("xT", [P, KT, T])
        memT = sb("memT", [P, KT, T])
        mergedT = memT
        ident = sb("ident", [P, P])
        ones = sb("ones", [P, P])
        tri_ge = sb("tri_ge", [P, P])
        tri_lt = sb("tri_lt", [P, P])
        lev = [sb(f"lev{i}", [P, P]) for i in range(6)]
        m_up = sb("m_up", [P, P])
        m_upi = sb("m_upi", [P, P])
        m_lo = sb("m_lo", [P, P])
        blk = sb("blk", [P, P])
        blk64 = sb("blk64", [P, P])
        idd = sb("idd", [P, 64])
        iota = sb("iota", [P, CAP])
        scanm = sb("scan_keep", [P, NP_TOK])
        eps = sb("eps", [P, 2])
        pcol = sb("param_cols", [P, 42])
        shT = sb("shift_inT", [P, RWT, NB])
        psh = sb("shift_out", [P, RWT, 9])
        m_page = sb("m_page", [P, W5])
        pick = sb("pick", [P, 15])
        pick4 = sb("pick4", [P, 12])
        sb_bias = sb("sb_bias_bc", [P, SBH])
        w_lora = sb("w_lora", [P, W5])
        w_gate2 = sb("w_gate2s", [P, W5])
        zs = sb("sample_logits", [P, NB, PAGES, SBH])
        pages = sb("pages", [1, NB * PAGES], I32)
        flag = sb("overflow", [P, 1], I32)
        arena = sb("arena", [P, 19220])
        YB = 13070

        def ar(off, *dims):
            n = int(np.prod(dims))
            assert off + n <= 19220
            v = arena[:, off:off + n]
            if len(dims) == 2:
                return v.rearrange("p (a b) -> p a b", a=dims[0])
            if len(dims) == 3:
                return v.rearrange("p (a b c) -> p a b c", a=dims[0], b=dims[1])
            return v

        ktok, vtok = ar(YB, 3, W5), ar(YB + 1536, 3, W5)
        mktok, mvtok = ar(YB + 3072, 2, W5), ar(YB + 4096, 2, W5)
        mkT = ar(YB + 5120, MH, NP_TOK)
        xr, memr = ar(0, 3, D), ar(3072, 2, D)
        shrow, prow = ar(7168, 1792), ar(8960, 128)
        same = [None] + [ar(9500 + 128 * i, P) for i in range(5)] + [blk[:]]
        sa_, sb_ = ar(0, NB * PAGES * SBH), ar(1024, NB * PAGES * SBH)
        spx = ar(2048, NB, PAGES, SBH)
        zp, np_, sp_, wp_ = (ar(3072 + 768 * i, 2, 384) for i in range(4))
        mp = ar(6144, 2, NP_TOK)
        mpT = ar(6656, 2, NP_TOK)
        mst = ar(7168, 16)
        zm, mps, mpTs = ar(7200, 2, 32), ar(7264, NP_TOK), ar(7520, 2, 32)
        shout = ar(7680, 1792)
        m_mem = [ar(10200 + 512 * i, W5) for i in range(2)]
        pvm = [ar(11300 + 512 * i, W5) for i in range(2)]
        orow = ar(12330, W5)
        LD, AA, KK, KM, GG, BON, T1, T2 = (ar(1056 * i, 4, T) for i in range(8))
        R0 = 8448
        SN = ar(R0, NB, 4, P)
        St = ar(R0 + 4096, 4, NB, 64)
        S1, S2 = ar(R0 + 6144, 4, NB, 64), ar(R0 + 8192, 4, NB, 64)
        tokAB, tokKV = ar(R0, 2, 256), ar(R0 + 512, 2, 256)
        Nl, Nt, Tm, Tt, Xm, AK, RB, RK = (ar(R0 + 1024 + 512 * i, 4, P) for i in range(8))
        Nm = [ar(R0 + 5120 + 512 * i, 4, P) for i in range(5)]
        MVs, Zs, Us = (ar(R0 + 7680 + 256 * i, 4, 64) for i in range(3))
        WTs, PM, tS = (ar(R0 + 8448 + 256 * i, 2, P) for i in range(3))
        Sb = [ar(R0 + 9216 + 512 * i, 4, P) for i in range(3)]
        assert R0 + 9216 + 1536 <= 19220
        xres = ar(0, 3, D)
        h1 = ar(3072, 3, D)
        yacc = ar(6144, 3, D)
        lng, lnb, ln2g, ln2b = (ar(9216 + 1024 * i, D) for i in range(4))
        sq = ar(13312, D)
        st_ = ar(14336, 24)
        bdrow = ar(14400, D)
        wr = ar(15424, KT, NE)
        lg, sel, wt, tmpE = (ar(15680 + 128 * i, 3, 34) for i in range(4))
        pos = ar(16192, 3, 34)
        h1T = ar(16600, KT, T)
        brt = ar(18720, NE)
        mx8 = ar(18760, 24)
        oneh, onew = ar(0, 3, 2, CAP), ar(384, 3, 2, CAP)
        onewT = ar(768, T)
        ysb = ar(1040, D)
        gb, lb, hb = ([ar(2064 + 256 * j + 128 * i, P) for i in range(2)] for j in range(3))
        sg = [ar(13312 + 128 * i, P) for i in range(2)]
        pick_e = [ar(13568 + 64 * i, CAP) for i in range(2)]
        bup = ar(9216, 2048)
        xg = xT[:, :, 0:P]
        hT = [memT[:, :, CAP * i:CAP * i + CAP] for i in range(2)]

        gate_at = lambda dt: pT[:, (V0 if dt < 4 else K0 - 4) + dt, :]
        gates = pT[:, K0:K0 + KT, :]
        o_mem = [zs[:].rearrange("p b n h -> p (b n h)")[:, T * i:T * i + T] for i in range(3)]
        MU, DE0, AA0, KKp, KAp, RKp, GNG, GNB = 0, 14, 18, 22, 26, 30, 34, 38

        def slot(name):
            return ring[:, slot_of[name][0], :]

        def arrived(eng, name):
            s = slot_of[name][0]
            if name in page_count:
                eng.wait_ge(sem(f"page{s}_landed"), page_count[name])
            elif name in mem_count:
                eng.wait_ge(sem(f"mem{s}_landed"), mem_count[name])
            else:
                eng.wait_ge(landed[s], landed_count[name])

        def full_of(name):
            b, use = G.where[name]
            return full[b], use + 1

        def last_reader(name):
            kind, i = name[0], name[1]
            if kind == "win":
                return full_of(("p", min(4 * i + 3, FT - 1)))
            if kind == "mkv":
                return full_of(("mk", 3) if i == 0 else ("mv", 1))
            if kind == "K":
                return sem("k_used"), i + 1
            if kind == "V":
                return full_of(("pv", i // 2))
            if kind == "mK":
                return sem("mk_used"), i + 1
            if kind == "mV":
                return full_of(("mpv", i))
            if kind == "wo":
                return full_of(("o", i, KT - 1))
            if kind == "gate":
                return full_of(("gate", i, 4 * name[2] + 3))
            return full_of(("res", 1, 1))

        page_count, mem_count = {}, {}
        for s in range(RING):
            np_so_far = nm_so_far = 0
            for name in stream:
                if slot_of[name][0] == s and name[0] in ("K", "V"):
                    np_so_far += 16 * 8
                    page_count[name] = np_so_far
                if slot_of[name][0] == s and name[0] in ("mK", "mV"):
                    nm_so_far += 16 * 4
                    mem_count[name] = nm_so_far
        landed_count, seen = {}, [0] * RING
        for name in stream:
            if name[0] not in ("K", "V", "mK", "mV"):
                seen[slot_of[name][0]] += 16
                landed_count[name] = seen[slot_of[name][0]]

        def take(eng, name):
            b, use = G.where[name]
            eng.wait_ge(full[b], use + 1)
            return bank[b]

        def gone(eng, name):
            b, use = G.where[name]
            eng.wait_ge(free[b], use + 1)

        def freed_by(name):
            return free[G.where[name][0]]

        col = lambda i: pcol[:, i:i + 1]
        block = ctx.enter_context(nc.Block())

        @block.sync
        def _(sp):
            sp.dma_start(pages[:], A["page_table"].rearrange("b n -> (b n)").unsqueeze(0)).then_inc(sem("pages_in"), 16)
            win = A["w_in"][0].rearrange("(k p) n -> p k n", p=P)
            mkv = A["w_mem_kv"][0].rearrange("(k p) n -> p k n", p=P)
            kc = A["cache_sb_k"][0].rearrange("g p h d -> g p (h d)")
            vc = A["cache_sb_v"][0].rearrange("g p h d -> g p (h d)")
            mkc = A["cache_mem_k"][0].rearrange("b (m p) h d -> p b m (h d)", p=P)
            mvc = A["cache_mem_v"][0].rearrange("b (m p) h d -> p b m (h d)", p=P)
            wo = [A[n][0].rearrange("(k p) n -> p k n", p=P) for n in ("w_sb_o", "w_mem_o", "w_rw_o")]
            wout = A["w_out"][0].rearrange("(k p) n -> p k n", p=P)
            sp.wait_ge(sem("pages_in"), 16)
            for n, name in enumerate(stream):
                s, use = slot_of[name]
                if use:
                    sp.wait_ge(*last_reader(stream[n - RING]))
                dst = slot(name)
                d8 = dst.rearrange("p (k n) -> p k n", k=KT)
                if name[0] == "win":
                    c0 = 512 * name[1]
                    w = min(512, GATE0 - c0)
                    sp.dma_start(d8[:, :, 0:w], win[:, :, c0:c0 + w]).then_inc(landed[s], 16)
                elif name[0] == "gate":
                    c0 = GATE0 + 1024 * name[1] + 512 * name[2]
                    sp.dma_start(d8, win[:, :, c0:c0 + 512]).then_inc(landed[s], 16)
                elif name[0] == "mkv":
                    c0 = 512 * name[1]
                    sp.dma_start(d8, mkv[:, :, c0:c0 + 512]).then_inc(landed[s], 16)
                elif name[0] in ("K", "V"):
                    src = kc if name[0] == "K" else vc
                    for j in range(8):
                        at = 8 * name[1] + j
                        page = sp.value_load(pages[0:1, at:at + 1], min_val=0, max_val=N_PAGES - 1)
                        sp.dma_start(d8[:, j, :], src[bass.ds(page, 1), :, :].rearrange("g p n -> p (g n)")).then_inc(
                            sem(f"page{s}_landed"), 16)
                elif name[0] in ("mK", "mV"):
                    src = mkc if name[0] == "mK" else mvc
                    for b in range(4):
                        sp.dma_start(dst.rearrange("p (b m n) -> p b m n", b=4, m=2)[:, b], src[:, 4 * name[1] + b]).then_inc(
                            sem(f"mem{s}_landed"), 16)
                elif name[0] == "wo":
                    sp.dma_start(dst.rearrange("p (k n) -> p k n", k=4), wo[name[1]]).then_inc(landed[s], 16)
                else:
                    sp.dma_start(dst.rearrange("p (k n) -> p k n", k=4),
                                 wout[:, 4 * name[1]:4 * name[1] + 4, :]).then_inc(landed[s], 16)

            wgu = A["w_gate_up"][0].rearrange("e (k p) n -> e p k n", p=P)
            wdn = A["w_down"][0].rearrange("e (k p) n -> e p k n", p=P)

            def pair_loads(p, it, first=False):
                for c in range(12):
                    s = (n_stream + c) % RING
                    e = 2 * p + c // 6
                    prev = c - RING
                    if first and prev < 0:
                        sp.wait_ge(*last_reader(stream[n_stream + prev]))
                    else:
                        ei, j = prev % 12 // 6, prev % 12 % 6
                        wraps = 1 if prev < 0 else 0
                        if j < 4:
                            sp.wait_ge(sem("up_full"), it * 8 + (4 * ei + j + 1 - 8 * wraps))
                        else:
                            sp.wait_ge(sem("down_full"), it * 4 + (2 * ei + j - 4 + 1 - 4 * wraps))
                    if c % 6 < 4:
                        sp.dma_start(ring[:, s, :].rearrange("p (k n) -> p k n", k=KT),
                                     wgu[bass.ds(e, 1), :, :, 512 * (c % 6):512 * (c % 6) + 512].rearrange("e p k n -> p (e k) n")
                                     ).then_inc(sem(f"expert{s}_landed"), 16)
                    else:
                        k0 = 4 * (c % 6 - 4)
                        sp.dma_start(ring[:, s, :].rearrange("p (k n) -> p k n", k=4),
                                     wdn[bass.ds(e, 1), :, k0:k0 + 4, :].rearrange("e p k n -> p (e k) n")
                                     ).then_inc(sem(f"expert{s}_landed"), 16)

            pair_loads(0, 0, True)
            with sp.Fori(1, NE // 2) as p:
                pair_loads(p, p)
            sp.wait_ge(sem("flag_ready"), 1)
            over = sp.value_load(flag[0:1, 0:1], min_val=0, max_val=T)
            with sp.If(over > CAP):
                with sp.Fori(0, ROUNDS) as r:
                    with sp.Fori(0, NE // 2) as p:
                        pair_loads(p, (r + 1) * (NE // 2) + p)

        @block.gpsimd
        def _(g):
            link = Chain(g, sem("pool_chain"))
            xs = A["x_prompt"][0].rearrange("(t p) d -> p t d", p=P)
            g.dma_start(xr[:, 0:2, :], xs).then_inc(sem("x_in"), 16)
            g.dma_start(xr[0:NB, 2, :], A["x_sample"].rearrange("b s d -> (b s) d")).then_inc(sem("x_in"), 16)
            g.memset(ident[:], 0.0).then_inc(sem("pool_chain"), 1)
            g.memset(ones[:], 1.0).then_inc(sem("pool_chain"), 1)
            link.at = 2
            g.wait_ge(sem("pool_chain"), 2)
            link(g.affine_select(out=ident[:], in_=ident[:], compare_op=ALU.not_equal, fill=1.0, base=0,
                                 pattern=[[-1, P]], channel_multiplier=1))
            g.sem_inc(sem("ident_ready"), 1)
            g.dma_start(memr[:, :, :], A["mem_prompt"][0].rearrange("(t p) d -> p t d", p=P)).then_inc(sem("mem_in"), 16)
            vec = lambda n, k: A[n].rearrange("l (t p) -> (l t) p", p=P)
            r0 = 0
            for n, k in (("mu_rw", 14), ("w_decay0", 4), ("w_aaa0", 4), ("rw_k_k", 4), ("rw_k_a", 4)):
                g.dma_start(prow[r0:r0 + k, :], vec(n, k)).then_inc(sem("param_in"), 16)
                r0 += k
            g.dma_start(prow[r0:r0 + 4, :], A["rw_r_k"].rearrange("l (t a) d -> (l t) (a d)", a=2)).then_inc(sem("param_in"), 16)
            r0 += 4
            for n in ("rw_gn_g", "rw_gn_b"):
                g.dma_start(prow[r0:r0 + 4, :], vec(n, 4)).then_inc(sem("param_in"), 16)
                r0 += 4
            g.dma_start(shrow[0:NB, :], A["state_rw_shift"][0]).then_inc(sem("param_in"), 16)
            g.dma_start(sb_bias[:], A["sb_bias"][0].partition_broadcast(P)).then_inc(sem("bias_in"), 16)
            g.dma_start(w_lora[0:64, :], A["w_decay2"][0]).then_inc(sem("lora_in"), 16)
            g.dma_start(w_lora[64:128, :], A["w_aaa2"][0]).then_inc(sem("lora_in"), 16)
            g.dma_start(w_gate2[:], A["w_gate2"][0]).then_inc(sem("lora_in"), 16)
            sel = lambda m, src, op, base, pat, cm: link(g.affine_select(
                out=m, in_=src, compare_op=op, fill=0.0, base=base, pattern=pat, channel_multiplier=cm))
            sel(tri_ge[:], ones[:], ALU.is_ge, 0, [[-1, P]], 1)
            sel(tri_lt[:], ones[:], ALU.is_gt, 0, [[1, P]], -1)
            g.sem_inc(sem("tri_ready"), 1)
            for i in range(1, 7):
                m = 1 << i
                v = same[i].rearrange("p (g j) -> p g j", j=m)
                link(g.memset(same[i], 1.0))
                sel(v, v, ALU.is_ge, 0, [[-m, P // m], [0, m]], 1)
                sel(v, v, ALU.is_ge, m - 1, [[m, P // m], [0, m]], -1)
            for i in range(6):
                lo = ident[:] if i == 0 else same[i]
                g.tensor_tensor(lev[i][:], same[i + 1], lo, ALU.subtract).then_inc(sem("masks"), 1)
            link(g.tensor_tensor(m_up[:], tri_lt[:], blk[:], ALU.mult))
            link(g.tensor_tensor(m_upi[:], m_up[:], ident[:], ALU.add))
            link(g.tensor_tensor(m_lo[:], blk[:], m_upi[:], ALU.subtract))
            link(g.tensor_scalar(blk64[:], blk[:], 1.0 / 64, 0.0, ALU.mult, ALU.add))
            link(g.tensor_tensor(idd[:], ident[:, 0:64], ident[:, 64:128], ALU.add))
            link(g.iota(iota[:], pattern=[[1, CAP]], base=1, channel_multiplier=0, allow_small_or_imprecise_dtypes=True))
            link(g.memset(scanm[:], 1.0))
            link(g.memset(scanm[:].rearrange("p (c j) -> p c j", j=C)[:, :, 0:1], 0.0))
            link(g.memset(eps[:, 0:1], GN_EPS))
            link(g.memset(eps[:, 1:2], LN_EPS))
            link(g.memset(pick[:], 0.0))
            link(g.memset(pick[:, 7:8], 1.0))
            link(g.memset(pick4[:], 1.0))
            sel(pick4[:], pick4[:], ALU.is_ge, 128, [[-32, 12]], 1)
            sel(pick4[:], pick4[:], ALU.is_ge, 31 - 128, [[32, 12]], -1)
            for m, step, offs, n in [(m_page[:], 40, 0, SBH), (m_mem[0], 36, 0, MH), (m_mem[1], 36, 16, MH)]:
                link(g.memset(m, 0.0))
                mv_ = m.rearrange("p (h d) -> p h d", h=n)
                for q in range(4):
                    link(g.affine_select(out=mv_, in_=mv_, compare_op=ALU.not_equal, fill=1.0, base=-step * q - offs,
                                         pattern=[[-1, n], [0, W5 // n]], channel_multiplier=1))
            g.sem_inc(sem("masks"), 1)

            def out(dst, src):
                g.dma_start(dst, src).then_inc(sem("out_done"), 16)

            n_out = 0
            for tt in range(3):
                gone(g, ("kt", tt))
                gone(g, ("vt", tt))
            for nm, src in (("sb_k", ktok), ("sb_v", vtok)):
                out(O[nm + "_prompt"][0, 0].rearrange("(t p) h d -> p t (h d)", p=P), src[:, 0:2, :])
                out(O[nm + "_sample"][0].rearrange("b s h d -> b (s h d)"), src[0:NB, 2, :])
            for tt in range(2):
                gone(g, ("mkt", tt))
                gone(g, ("mv", tt))
            for j in range(4):
                gone(g, ("shift_out", j))
            out(O["mem_k"][0, 0].rearrange("(t p) h d -> p t (h d)", p=P), mktok)
            out(O["mem_v"][0, 0].rearrange("(t p) h d -> p t (h d)", p=P), mvtok)
            out(O["shift_prompt"][0], shout[0:1, :])
            out(O["shift_sample"][0], shout[1:9, :])
            n_out += 8
            g.wait_ge(sem("out_done"), 16 * n_out)
            g.sem_inc(sem("arena_clear"), 1)
            g.wait_ge(sem("rw_clear"), 1)
            g.dma_start(SN[0:64].rearrange("v b t (hp k) -> v (b t hp) k", hp=2),
                        A["state_rw_wkv"][0].rearrange("b h v k -> v (b h) k")).then_inc(sem("state_in"), 16)

            def gated(br, tiles):
                g.wait_ge(sem("gates_ready"), br + 1)
                for dt in tiles:
                    gone(g, ("o", br, dt))
                    if br == 0:
                        g.tensor_tensor(mergedT[:, dt, :], mergedT[:, dt, :], gate_at(dt), ALU.mult
                                        ).then_inc(sem("branch_summed"), 1)
                    else:
                        link(g.tensor_tensor(gate_at(dt), o_mem[dt % 3], gate_at(dt), ALU.mult))
                        g.tensor_tensor(mergedT[:, dt, :], mergedT[:, dt, :], gate_at(dt), ALU.add
                                        ).then_inc(sem("branch_summed"), 1)

            gated(0, range(KT))
            g.wait_ge(sem("kk_sq"), 1)
            for t in range(4):
                ins = g.tensor_tensor(S2[:, t], idd[:].unsqueeze(1).to_broadcast([P, NB, 64]),
                                      pT[:, 24 + t, NP_TOK:T].unsqueeze(2).to_broadcast([P, NB, 64]), ALU.mult)
            ins.then_inc(sem("s_v"), 1)
            for j in range(8):
                gone(g, ("so_out", j))
            g.dma_start(O["wkv_sample"][0].rearrange("b h v k -> v (b h) k"),
                        SN[0:64].rearrange("v b t (hp k) -> v (b t hp) k", hp=2)).then_inc(sem("out_done"), 16)
            n_out += 1
            g.wait_ge(sem("out_done"), 16 * n_out)
            g.sem_inc(sem("arena_clear"), 1)
            for it in range(4):
                n = (it // 2, it % 2)
                gone(g, ("g1", 0) + n)
                gone(g, ("g1", 1) + n)
                for lv in range(5):
                    g.tensor_tensor(Nm[lv], Nt, lev[lv + 1][:].unsqueeze(1).to_broadcast([P, 4, P]),
                                    ALU.mult).then_inc(sem("Nm_ready"), 1)
                gated(1, [name[2] for place in PLACES for name in ending_at(it, place) if name[0] == "o"])
            gone(g, "wkv_out")
            for hp in range(2):
                g.dma_start(O["wkv_prompt"][0, 0].rearrange("(t hp) v k -> hp v t k", hp=2)[hp],
                            Nm[0][64 * hp:64 * hp + 64, :, 64 * hp:64 * hp + 64]).then_inc(sem("out_done"), 16)
            n_out += 2
            g.wait_ge(sem("out_done"), 16 * n_out)
            g.wait_ge(sem("rw_done"), 1)
            g.memset(yacc, 0.0).then_inc(sem("y_zero"), 1)
            for dst, nm in ((lng, "ln1_g"), (lnb, "ln1_b"), (ln2g, "ln2_g"), (ln2b, "ln2_b")):
                g.dma_start(dst, A[nm][0].partition_broadcast(P)).then_inc(sem("ln_in"), 16)
            link(g.memset(bdrow, 0.0))
            g.dma_start(bdrow[0:NE, :], A["b_down"][0]).then_inc(sem("ln_in"), 16)
            g.dma_start(wr, A["w_router"][0].rearrange("(k p) e -> p k e", p=P)).then_inc(sem("ln_in"), 16)
            g.dma_start(brt, A["b_router"][0].partition_broadcast(P)).then_inc(sem("ln_in"), 16)
            g.dma_start(xres[:, 0:2, :], xs).then_inc(sem("ln_in"), 16)
            g.dma_start(xres[0:NB, 2, :], A["x_sample"].rearrange("b s d -> (b s) d")).then_inc(sem("ln_in"), 16)
            g.wait_ge(sem("h1"), 3)
            link(g.memset(bup, 0.0))
            g.dma_start(bup[0:NE, :], A["b_gate_up"][0]).then_inc(sem("bias_up_in"), 16)
            for i, tt in enumerate(H1_ORDER):
                t0, rows = TOK[tt]
                g.wait_ge(sem("y_ready"), i + 1)
                dst = O["y_prompt"][0, t0:t0 + rows, :] if tt < 2 else O["y_sample"].rearrange("b s d -> (b s) d")
                g.dma_start(dst, yacc[0:rows, tt, :]).then_inc(sem("out_done"), 16)
                n_out += 1
            g.wait_ge(sem("out_done"), 16 * n_out)

        @block.tensor
        def _(pe):
            opened = [0] * 8

            def start(name):
                b, use = G.where[name]
                assert opened[b] == use, name
                opened[b] += 1
                if use:
                    pe.wait_ge(free[b], use)
                return bank[b]

            def done(name, ins):
                ins.then_inc(full[G.where[name][0]], 1)

            mm = lambda out, l, r, first, last, **k: pe.matmul(out, l, r, start=first, stop=last, **k)
            tr = lambda out, src, rows=P: pe.transpose(out, src, ident[0:rows, 0:rows])

            pe.wait_ge(sem("ident_ready"), 1)
            pe.wait_ge(sem("x_in"), 32)
            for k in range(KT):
                b = start(("xT", k))
                for tt, (t0, rows) in enumerate(TOK):
                    last = tr(b[:, t0:t0 + rows], xr[0:rows, tt, k * P:(k + 1) * P], rows)
                done(("xT", k), last)
            def q_broadcast(name, tile0, tok):
                b = start(name)
                for t in range(4):
                    last = mm(b[:, t * P:t * P + P], pT[:, tile0 + t, tok:tok + 1].to_broadcast([P, P]), ident[:], True, True)
                done(name, last)

            for c in range(8):
                if c == 2:
                    pe.wait_ge(sem("mem_in"), 16)
                    for k in range(KT):
                        b = start(("memT", k))
                        for tt in range(2):
                            last = tr(b[:, tt * P:tt * P + P], memr[:, tt, k * P:(k + 1) * P])
                        done(("memT", k), last)
                    pe.wait_ge(sem("param_in"), 144)
                    b = start("params")
                    done("params", tr(b[:, 0:42], prow[0:42, :], 42))
                    b = start("shift_in")
                    for t in range(RWT):
                        last = tr(b[:, NB * t:NB * t + NB], shrow[0:NB, t * P:t * P + P], NB)
                    done("shift_in", last)
                if c:
                    gone(pe, ("p", 3))
                    q_broadcast(("qb", c - 1), Q0, NP_TOK + c - 1)
                arrived(pe, ("win", c))
                w = slot(("win", c)).rearrange("p (k n) -> p k n", k=KT)
                if c == 0:
                    for k in range(KT):
                        gone(pe, ("xT", k))
                for ft in range(4 * c, min(4 * c + 4, FT)):
                    b = start(("p", ft))
                    j = ft - 4 * c
                    for k in range(KT):
                        last = mm(b[:, 0:T], w[:, k, j * P:j * P + P], xT[:, k, :], k == 0, k == KT - 1)
                    done(("p", ft), last)
            q_broadcast(("qb", 7), Q0, NP_TOK + 7)
            arrived(pe, ("mkv", 0))
            w = slot(("mkv", 0)).rearrange("p (k n) -> p k n", k=KT)
            for k in range(KT):
                gone(pe, ("memT", k))
            for h in range(MH):
                b = start(("mk", h))
                for k in range(KT):
                    last = mm(b[:, 0:NP_TOK], w[:, k, h * P:h * P + P], memT[:, k, 0:NP_TOK], k == 0, k == KT - 1)
                done(("mk", h), last)
            arrived(pe, ("mkv", 1))
            w = slot(("mkv", 1)).rearrange("p (k n) -> p k n", k=KT)
            for tt in range(2):
                b = start(("mv", tt))
                for k in range(KT):
                    last = mm(b[:, :], memT[:, k, tt * P:tt * P + P], w[:, k, :], k == 0, k == KT - 1)
                done(("mv", tt), last)
            for ft in range(K0, K0 + 8):
                gone(pe, ("p", ft))
            for tt, (t0, rows) in enumerate(TOK):
                for nm, f0 in (("kt", K0), ("vt", V0)):
                    b = start((nm, tt))
                    for t in range(4):
                        last = tr(b[0:rows, t * P:t * P + P], pT[:, f0 + t, t0:t0 + rows])
                    done((nm, tt), last)
            for h in range(MH):
                gone(pe, ("mk", h))
            for tt in range(2):
                b = start(("mkt", tt))
                for h in range(MH):
                    last = tr(b[:, h * P:h * P + P], mkT[:, h, tt * P:tt * P + P])
                done(("mkt", tt), last)
            for ft in range(24, FT):
                gone(pe, ("p", ft))
            pe.wait_ge(sem("shift_cut"), 1)
            for j in range(4):
                b = start(("shift_out", j))
                for t in range(4 * j, min(4 * j + 4, RWT)):
                    last = tr(b[0:9, (t % 4) * P:(t % 4) * P + P], psh[:, t, :])
                done(("shift_out", j), last)

            pe.wait_ge(sem("tri_ready"), 1)
            pe.wait_ge(sem("sp_s"), 1)
            spf, spxf = sb_, spx.rearrange("p b n h -> p (b n h)")
            for i in range(2):
                b = start(("cs_s", i))
                mm(b[:, :], tri_ge[:], spf[:, 512 * i:512 * i + 512], True, False)
                done(("cs_s", i), mm(b[:, :], ones[:], spxf[:, 512 * i:512 * i + 512], False, True))

            def branches(first, last):
                at = 0
                for name in beside():
                    kind, br, dt = name
                    n = KT if kind == "gate" else 4
                    lo, hi = max(first - at, 0), min(last - at, n)
                    at += n
                    if lo >= hi:
                        continue
                    b = start(name) if lo == 0 else bank[G.where[name][0]]
                    if kind == "gate":
                        arrived(pe, ("gate", br, dt // 4))
                        w = slot(("gate", br, dt // 4)).rearrange("p (k n) -> p k n", k=KT)[:, :, (dt % 4) * P:(dt % 4) * P + P]
                        src = xT
                    else:
                        arrived(pe, ("wo", br))
                        w = slot(("wo", br)).rearrange("p (k n) -> p k n", k=4)[:, :, dt * P:dt * P + P]
                        f0 = (Q0, MQ0)[br]
                        src = pT[:, f0:f0 + 4, :]
                    for k in range(lo, hi):
                        ins = mm(b[:, 0:T], w[:, k, :], src[:, k, :], k == 0, k == n - 1)
                    if hi == n:
                        done(name, ins)

            def sample_values(bq):
                if bq == 0:
                    pe.wait_ge(sem("w_s"), 1)
                arrived(pe, ("V", 2 * bq))
                b = start(("pv", bq))
                for n in range(PAGES):
                    if n == 8:
                        arrived(pe, ("V", 2 * bq + 1))
                    v = slot(("V", 2 * bq + n // 8)).rearrange("p (k n) -> p k n", k=8)
                    i, q = n // 4, n % 4
                    last = mm(b[32 * q:32 * q + 32, :], zs[:, bq, 4 * i:4 * i + 4, :].rearrange("p n h -> p (n h)"),
                              v[:, n % 8, :], i == 0, i == 3)
                done(("pv", bq), last)

            def sample_sum(bq):
                pe.wait_ge(sem("pv_kept"), bq + 1)
                b = start("so_s") if bq == 0 else bank[5]
                last = mm(b[0:NB, :], pick[:, 7 - bq:15 - bq], pvm[bq % 2], bq == 0, bq == NB - 1)
                last.then_inc(sem("pv_summed"), 1) if bq < NB - 1 else done("so_s", last)

            for g4 in range(4):
                for hp in range(2):
                    b = start(("z", g4, hp))
                    q = pT[64 * hp:64 * hp + 64, Q0 + g4, :]
                    k = pT[64 * hp:64 * hp + 64, K0 + g4, :]
                    mm(b[:, 0:256], k[:, 0:128], q[:, 0:256], True, True)
                    done(("z", g4, hp), mm(b[:, 256:384], k[:, 128:256], q[:, 128:256], True, True))
                sample_values(g4)
                pe.wait_ge(sem("sp_p"), g4 + 1)
                for hp in range(2):
                    b = start(("cs", g4, hp))
                    mm(b[:, 0:384], tri_ge[:], sp_[:, hp, :], True, True)
                    done(("cs", g4, hp), mm(b[:, 128:256], ones[:], sp_[:, hp, 256:384], False, True, skip_group_check=True))
                sample_sum(g4)
                gone(pe, ("vt", 0))
                gone(pe, ("vt", 1))
                pe.wait_ge(sem("w_p"), g4 + 1)
                b = start(("so", g4))
                for hp in range(2):
                    h = 2 * g4 + hp
                    o = b[64 * hp:64 * hp + 64, :]
                    mm(o[:, 0:256], vtok[:, 0, h * 64:h * 64 + 64], wp_[:, hp, 0:256], True, True)
                    last = mm(o[:, 128:256], vtok[:, 1, h * 64:h * 64 + 64], wp_[:, hp, 256:384], False, True, skip_group_check=True)
                done(("so", g4), last)

            for h in range(MH):
                b = start(("mz", h))
                for qt in range(2):
                    last = mm(b[:, 256 * qt:256 * qt + 256], pT[:, MQ0 + h, qt * P:qt * P + P], mkT[:, h, :], True, True)
                done(("mz", h), last)
                sample_values(4 + h)
                branches(16 * h, 16 * h + 8)
                pe.wait_ge(sem("mp"), h + 1)
                b = start(("mpT", h))
                for mt in range(2):
                    for qt in range(2):
                        last = tr(b[:, 256 * mt + qt * P:256 * mt + qt * P + P], mp[:, qt, mt * P:mt * P + P])
                done(("mpT", h), last)
                sample_sum(4 + h)
                branches(16 * h + 8, 16 * h + 16)
                gone(pe, ("mpT", h))
                gone(pe, ("mv", 0))
                gone(pe, ("mv", 1))
                b = start(("mo", h))
                for mt in range(2):
                    last = mm(b[:, 0:256], mvtok[:, mt, h * P:h * P + P], mpT[:, mt, :], mt == 0, mt == 1)
                done(("mo", h), last)
            def row_to_features(name, row):
                gone(pe, row)
                b = start(name)
                for t in range(4):
                    last = tr(b[:, NB * t:NB * t + NB], orow[0:NB, t * P:t * P + P], NB)
                done(name, last)

            row_to_features("so_sT", "so_s")
            for bq in range(NB):
                q_broadcast(("mqb", bq), MQ0, NP_TOK + bq)
            pe.wait_ge(sem("zm"), 1)
            b = start("mzT")
            for mt in range(2):
                last = tr(b[0:32, mt * P:mt * P + P], zm[:, mt, :])
            done("mzT", last)
            pe.wait_ge(sem("mps"), 1)
            b = start("mpTs")
            for mt in range(2):
                last = tr(b[:, 32 * mt:32 * mt + 32], mps[0:32, mt * P:mt * P + P], 32)
            done("mpTs", last)
            gone(pe, "mpTs")
            for i in range(2):
                arrived(pe, ("mV", i))
                b = start(("mpv", i))
                v = slot(("mV", i)).rearrange("p (b m n) -> p b m n", b=4, m=2)
                for mt in range(2):
                    for q in range(4):
                        last = mm(b[32 * q:32 * q + 32, :], mpTs[:, mt, :], v[:, q, mt, :], mt == 0, mt == 1)
                done(("mpv", i), last)
            b = start("mo_s")
            for i in range(2):
                gone(pe, ("mpv", i))
                last = mm(b[0:NB, :], pick4[:, 4 - 4 * i:12 - 4 * i], pvm[i], i == 0, i == 1)
            done("mo_s", last)
            row_to_features("mo_sT", "mo_s")

            for g4 in range(4):
                gone(pe, ("so", g4))
            gone(pe, "so_sT")
            branches(64, 80)
            pe.wait_ge(sem("lora_in"), 48)
            pe.wait_ge(sem("lora_act"), 2)
            for nm, rows in (("dec", slice(0, 64)), ("aaa", slice(64, 128))):
                for t in range(4):
                    b = start((nm, t))
                    done((nm, t), mm(b[:, 0:T], w_lora[rows, t * P:t * P + P], pT[rows, 28, :], True, True))
            for t in range(4):
                b = start(("gr", t))
                done(("gr", t), mm(b[:, 0:T], w_gate2[:, t * P:t * P + P], pT[:, 29, :], True, True))

            def over_heads(nm, src, ready, mat=blk):
                pe.wait_ge(sem(ready), 1)
                for t in range(4):
                    b = start((nm, t))
                    done((nm, t), mm(b[:, 0:src.shape[2]], mat[:], src[:, t, :], True, True))

            pe.wait_ge(sem("masks"), 7)
            over_heads("kn", T1, "kk_sq")
            branches(80, 128)
            over_heads("bon", T1, "rk_prod")
            branches(128, 144)
            pe.wait_ge(sem("state_in"), 16)
            for t in range(4):
                b = start(("st", t))
                for bq in range(NB):
                    last = tr(b[:, 64 * bq:64 * bq + 64], SN[0:64, bq, t, :], 64)
                done(("st", t), last)
            branches(144, 160)
            flat = lambda a: a.rearrange("p t b v -> p t (b v)")
            over_heads("sa", flat(S1), "s_kk")
            over_heads("vb", flat(S2), "s_v")
            for h in range(MH):
                gone(pe, ("mo", h))
            gone(pe, "mo_sT")
            pe.wait_ge(sem("s_new"), 1)
            for j in range(8):
                b = start(("so_out", j))
                for i in range(4):
                    last = tr(b[0:64, i * P:i * P + P], St[:, j // 2, 4 * (j % 2) + i, :])
                done(("so_out", j), last)
            bs = [start(("ys", hp)) for hp in range(2)]
            for hp in range(2):
                rows = slice(64 * hp, 64 * hp + 64)
                for t in range(4):
                    for bq in range(NB):
                        last = mm(bs[hp][rows, NB * t + bq:NB * t + bq + 1], St[rows, t, bq, :],
                                  pT[rows, RW0 + t, NP_TOK + bq:NP_TOK + bq + 1], True, True)
                done(("ys", hp), last)

            for tt in range(2):
                for hh in range(2):
                    n = (tt, hh)
                    cols = slice(tt * P, tt * P + P)
                    it = 2 * tt + hh
                    tiles = (2 * hh, 2 * hh + 1)
                    if it == 0:
                        pe.wait_ge(sem("hats"), 1)
                    for nm, srcs in (("tab", (KK, AA)), ("tkv", (KM, pT[:, 24:28, :]))):
                        b = start((nm,) + n)
                        for i, src in enumerate(srcs):
                            for tl, t in enumerate(tiles):
                                last = tr(b[:, 256 * i + P * tl:256 * i + P * tl + P], src[:, t, cols])
                        done((nm,) + n, last)
                    hats = {"A": KK, "B": AA, "K": KM, "R": pT[:, RW0:RW0 + 4, :]}
                    for nm, prods in (("g1", ("BA", "AB")), ("g2", ("BR", "KA")), ("g3", ("KR",))):
                        for hp in range(2):
                            b = start((nm, hp) + n)
                            rows = slice(64 * hp, 64 * hp + 64)
                            for i, lr in enumerate(prods):
                                for tl, t in enumerate(tiles):
                                    c0 = 256 * i + P * tl
                                    last = mm(b[:, c0:c0 + P], hats[lr[0]][rows, t, cols], hats[lr[1]][rows, t, cols], True, True)
                            done((nm, hp) + n, last)
                    branches(*at_place(it, "start"))
                    pe.wait_ge(sem("T_ready"), it + 1)
                    for lv in range(5):
                        if lv:
                            gone(pe, ("TX", lv - 1) + n)
                        pe.wait_ge(sem("Nm_ready"), 5 * it + lv + 1)
                        b = start(("X", lv) + n)
                        for u in range(4):
                            last = mm(b[:, u * P:u * P + P], Nm[lv][:, u, :], Tm[:, u, :], True, True)
                        done(("X", lv) + n, last)
                        branches(*at_place(it, f"X{lv}"))
                        if lv:
                            gone(pe, ("XT", lv - 1) + n)
                        gone(pe, ("X", lv) + n)
                        if lv < 4:
                            b = start(("TX", lv) + n)
                            for u in range(4):
                                last = mm(b[:, u * P:u * P + P], Tt[:, u, :], Xm[:, u, :], True, True)
                            done(("TX", lv) + n, last)
                        b = start(("XT", lv) + n)
                        for u in range(4):
                            last = mm(b[:, u * P:u * P + P], Xm[:, u, :], Tt[:, u, :], True, True)
                        done(("XT", lv) + n, last)
                    b = start(("MV",) + n)
                    gone(pe, ("tkv",) + n)
                    for hp in range(2):
                        gone(pe, ("g2", hp) + n)
                        gone(pe, ("g3", hp) + n)
                    for tl in range(2):
                        for hp in range(2):
                            u, c0 = 2 * hp + tl, 64 * (2 * tl + hp)
                            last = mm(b[:, c0:c0 + 64], AK[:, u, :], tokKV[:, 1, c0:c0 + 64], True, True)
                    done(("MV",) + n, last)
                    branches(*at_place(it, "MV"))
                    gone(pe, ("MV",) + n)
                    gone(pe, ("XT", 4) + n)
                    b = start(("Z",) + n)
                    for tl in range(2):
                        for hp in range(2):
                            u, j = 2 * hp + tl, 2 * tl + hp
                            last = mm(b[:, 64 * j:64 * j + 64], Tt[:, u, :], MVs[:, j, :], True, True)
                    done(("Z",) + n, last)
                    b = start(("WT",) + n)
                    for tl in range(2):
                        for hp in range(2):
                            u, c0 = 2 * hp + tl, 64 * (2 * tl + hp)
                            last = mm(b[64 * hp:64 * hp + 64, P * tl:P * tl + P], tokAB[:, 0, c0:c0 + 64], Tt[:, u, :], True, True)
                    done(("WT",) + n, last)
                    branches(*at_place(it, "WT"))
                    gone(pe, ("WT",) + n)
                    gone(pe, ("tab",) + n)
                    for cc in range(2):
                        c = 2 * tt + cc
                        rows = slice(64 * cc, 64 * cc + 64)
                        if 2 * it + cc:
                            pe.wait_ge(sem("S_ready"), 2 * it + cc)
                        else:
                            pe.wait_ge(sem("S_zero"), 1)
                        b = start(("U", cc) + n)
                        for tl, t in enumerate(tiles):
                            last = mm(b[rows, P * tl:P * tl + P], WTs[:, tl, rows], Sb[c % 3][:, t, :], True, True)
                        done(("U", cc) + n, last)
                        branches(*at_place(it, f"U{cc}"))
                        gone(pe, ("U", cc) + n)
                        b = start(("dS", cc) + n)
                        for tl in range(2):
                            o = b[:, P * tl:P * tl + P]
                            uc = Us.rearrange("p a b -> p (a b)")[rows, P * tl:P * tl + P]
                            mm(o, tokAB[rows, 1, P * tl:P * tl + P], uc, True, False)
                            last = mm(o, tokKV[rows, 0, P * tl:P * tl + P], tokKV[rows, 1, P * tl:P * tl + P], False, True)
                        done(("dS", cc) + n, last)
                    b = start(("Y",) + n)
                    for tl, t in enumerate(tiles):
                        for cc in range(2):
                            c = 2 * tt + cc
                            mm(b[:, P * tl + 64 * cc:P * tl + 64 * cc + 64], Sb[c % 3][:, t, :],
                               pT[:, RW0 + t, c * C:c * C + C], cc == 0, True, skip_group_check=True)
                        for hp in range(2):
                            u, j = 2 * hp + tl, 2 * tl + hp
                            o = b[64 * hp:64 * hp + 64, P * tl:P * tl + P]
                            mm(o, Us[:, j, :], RB[:, u, :], False, True, skip_group_check=True)
                            last = mm(o, tokKV[:, 1, 64 * j:64 * j + 64], RK[:, u, :], False, True, skip_group_check=True)
                    done(("Y",) + n, last)
            pe.wait_ge(sem("S_ready"), 8)
            b = start("wkv_out")
            for t in range(4):
                last = tr(b[:, P * t:P * t + P], Sb[1][:, t, :])
            done("wkv_out", last)
            gone(pe, ("ys", 0))
            gone(pe, ("ys", 1))
            gone(pe, ("Y", 1, 0))
            gone(pe, ("Y", 1, 1))
            for t in range(4):
                b = start(("gm", t))
                done(("gm", t), mm(b[:, 0:T], blk64[:], T1[:, t, :], True, True))
            over_heads("gv", T2, "y_sq", blk64)
            branches(248, 256)

            arrived(pe, ("wo", 2))
            w = slot(("wo", 2)).rearrange("p (k n) -> p k n", k=4)
            pe.wait_ge(sem("rw_done"), 1)
            for dt in range(KT):
                b = start(("o", 2, dt))
                for k in range(4):
                    last = mm(b[:, 0:T], w[:, k, dt * P:dt * P + P], pT[:, RW0 + k, :], k == 0, k == 3)
                done(("o", 2, dt), last)
            pe.wait_ge(sem("merged"), 1)
            w = [slot(("wout", i)).rearrange("p (k n) -> p k n", k=4) for i in range(2)]
            arrived(pe, ("wout", 0))
            arrived(pe, ("wout", 1))
            b = start("res_s")
            for k in range(4):
                for q in range(4):
                    last = mm(b[32 * q:32 * q + NB, :], mergedT[:, 4 * (q // 2) + k, NP_TOK:T],
                              w[q // 2][:, k, 512 * (q % 2):512 * (q % 2) + 512], k == 0, k == 3)
            done("res_s", last)

            def logits(tt):
                t0, rows = TOK[tt]
                pe.wait_ge(sem("h1"), H1_ORDER.index(tt) + 1)
                for j in range(2):
                    b = start(("h1T", tt, j))
                    for k in range(4):
                        kk = 4 * j + k
                        last = tr(b[:, P * k:P * k + rows], h1[0:rows, tt, kk * P:kk * P + P], rows)
                    done(("h1T", tt, j), last)
                pe.wait_ge(sem("ln_in"), 144)
                for j in range(2):
                    gone(pe, ("h1T", tt, j))
                b = start(("logit", tt))
                for k in range(KT):
                    last = mm(b[0:rows, 0:NE], h1T[:, k, t0:t0 + rows], wr[:, k, :], k == 0, k == KT - 1)
                done(("logit", tt), last)

            for tt in range(2):
                bs = [start(("res", tt, half)) for half in range(2)]
                for k in range(KT):
                    for half in range(2):
                        last = mm(bs[half][:, :], mergedT[:, k, tt * P:tt * P + P], w[k // 4][:, k % 4, 512 * half:512 * half + 512],
                                  k == 0, k == KT - 1)
                        if k == KT - 1:
                            done(("res", tt, half), last)
                logits((2, 0)[tt])
            logits(1)
            pe.wait_ge(sem("sel_ready"), 1)
            b = start("rank")
            for tt, (t0, rows) in enumerate(TOK):
                o = b[0:rows, NE * tt:NE * tt + NE]
                for t2 in range(tt):
                    mm(o, ones[:, 0:rows], sel[:, t2, 0:NE], t2 == 0, False)
                mm(o, tri_lt[0:rows, 0:rows], sel[0:rows, tt, 0:NE], tt == 0, True)
            for tt, (t0, rows) in enumerate(TOK):
                last = mm(b[:, 96:96 + NE], ones[0:rows, :], sel[0:rows, tt, 0:NE], tt == 0, tt == 2)
            done("rank", last)

            rank_bank = G.where["rank"][0]
            for b in range(8):
                if b != rank_bank:
                    pe.wait_ge(free[b], opened[b])

            def gather(n_before):
                pe.wait_ge(sem("oneh_ready"), n_before + 1)
                for k in range(KT):
                    for tt, (t0, rows) in enumerate(TOK):
                        last = mm(bank[k // 4][:, (k % 4) * P:(k % 4) * P + P], h1[0:rows, tt, k * P:k * P + P],
                                  oneh[0:rows, tt].rearrange("p a b -> p (a b)"), tt == 0, tt == 2)
                last.then_inc(sem("gathered"), 1)

            def up(it, c, ei, j):
                s = (n_stream + c) % RING
                u = 4 * ei + j
                pe.wait_ge(sem(f"expert{s}_landed"), it * 48 + 16 * (c // RING + 1))
                w = ring[:, s, :].rearrange("p (k n) -> p k n", k=KT)
                for k in range(KT + 1):
                    for hf in range(2):
                        o = bank[2 + j % 2][64 * hf:64 * hf + 64, 0:256]
                        if k < KT:
                            mm(o, xg[:, k, CAP * ei:CAP * ei + CAP], w[:, k, 256 * hf:256 * hf + 256], k == 0, False)
                        else:
                            last = mm(o, pick_e[ei], bup[:, 512 * j + 256 * hf:512 * j + 256 * hf + 256], False, True)
                last.then_inc(sem("up_full"), 1)

            def turn(it, ei, j):
                u = 4 * ei + j
                pe.wait_ge(sem("h_ready"), it * 8 + (u + 1))
                if u == 0:
                    pe.wait_ge(sem("scatter_added"), it * 6 + 1)
                elif j >= 2:
                    pe.wait_ge(sem("hT_ready"), it * 8 + (u - 1))
                tr(bank[6 + j % 2][:, 0:P], hb[j % 2]).then_inc(sem("h_turned"), 1)

            def down(it, c, ei, j):
                s = (n_stream + c) % RING
                pe.wait_ge(sem(f"expert{s}_landed"), it * 48 + 16 * (c // RING + 1))
                w = ring[:, s, :].rearrange("p (k n) -> p k n", k=4)
                for k in range(4):
                    kf = 4 * j + k
                    if kf % 2 == 0:
                        pe.wait_ge(sem("hT_ready"), it * 8 + (4 * ei + kf // 2 + 1))
                    for half in range(2):
                        r0 = 64 * (half ^ ei)
                        last = mm(bank[4 + half][r0:r0 + 64, :], hT[ei][:, kf, :],
                                  w[:, k, 512 * half:512 * half + 512], kf == 0, False)
                if j == 0:
                    last.then_inc(sem("down_full"), 1)
                    return
                for half in range(2):
                    r0 = 64 * (half ^ ei)
                    last = mm(bank[4 + half][r0:r0 + 64, :], pick_e[ei], bdrow[:, 512 * half:512 * half + 512], False, True)
                last.then_inc(sem("down_full"), 1)

            def pair(it, gathers):
                pe.wait_ge(sem("xg_ready"), gathers * 2)
                pe.wait_ge(sem("pick_ready"), it + 1)
                for ei in range(2):
                    c = 6 * ei
                    up(it, c, ei, 0)
                    up(it, c + 1, ei, 1)
                    turn(it, ei, 0)
                    up(it, c + 2, ei, 2)
                    turn(it, ei, 1)
                    up(it, c + 3, ei, 3)
                    turn(it, ei, 2)
                    if ei:
                        pe.wait_ge(sem("onew_ready"), it + 1)
                        for tt, (t0, rows) in enumerate(TOK):
                            last = tr(bank[2][:, t0:t0 + rows], onew[0:rows, tt].rearrange("p a b -> p (a b)"), rows)
                        last.then_inc(sem("onewT_full"), 1)
                        gather(gathers)
                    down(it, c + 4, ei, 0)
                    turn(it, ei, 3)
                    down(it, c + 5, ei, 1)
                pe.wait_ge(sem("onewT_ready"), it + 1)
                pe.wait_ge(sem("y_moved"), it + 1)
                for i in range(6):
                    tt, half = i // 2, i % 2
                    t0, rows = TOK[tt]
                    pe.wait_ge(sem("scatter_added"), it * 6 + (max(i - 1, 0) + 1))
                    mm(bank[6 + i % 2][0:rows, :], onewT[:, t0:t0 + rows], ysb[:, 512 * half:512 * half + 512],
                       True, True).then_inc(sem("scatter_full"), 1)

            pe.wait_ge(sem("bias_up_in"), 16)
            pe.sem_inc(sem("onewT_full"), 1)
            gather(0)
            pe.wait_ge(free[rank_bank], opened[rank_bank])
            with pe.Fori(0, NE // 2) as p:
                pair(p, p + 1)
            pe.wait_ge(sem("flag_ready"), 1)
            over = pe.value_load(flag[0:1, 0:1], min_val=0, max_val=T)
            with pe.If(over > CAP):
                with pe.Fori(0, ROUNDS) as r:
                    gather((r + 1) * (NE // 2 + 1))
                    with pe.Fori(0, NE // 2) as p:
                        pair((r + 1) * (NE // 2) + p, (r + 1) * (NE // 2 + 1) + p + 1)

        @block.scalar
        def _(act):
            link = Chain(act, sem("act_chain"))

            def move(name, dst, src_of, func=ACT.Copy, **k):
                b = take(act, name)
                act.activation(dst, src_of(b), func, **k).then_inc(freed_by(name), 1)

            for k in range(0, KT, 2):
                move(("xT", k), xT[:, k, :], lambda b: b[:, 0:T])
            for ft in range(FT):
                if ft == 8:
                    for k in range(KT):
                        move(("memT", k), memT[:, k, 0:NP_TOK], lambda b: b[:, 0:NP_TOK])
                    move("params", pcol[:], lambda b: b[:, 0:42])
                    move("shift_in", shT[:].rearrange("p t b -> p (t b)"), lambda b: b[:, 0:RWT * NB])
                move(("p", ft), pT[:, ft, :], lambda b: b[:, 0:T])
            gone(act, "params")
            for h in range(MH):
                move(("mk", h), mkT[:, h, :], lambda b: b[:, 0:NP_TOK])
            for tt in range(2):
                move(("mv", tt), mvtok[:, tt, :], lambda b: b[:, :])
            for tt, (t0, rows) in enumerate(TOK):
                move(("kt", tt), ktok[0:rows, tt, :], lambda b: b[0:rows, :])
                move(("vt", tt), vtok[0:rows, tt, :], lambda b: b[0:rows, :])
            for tt in range(2):
                move(("mkt", tt), mktok[:, tt, :], lambda b: b[:, :])
            for j in range(4):
                w = min(512, RWT * P - 512 * j)
                move(("shift_out", j), shout[0:9, 512 * j:512 * j + w], lambda b: b[0:9, 0:w])

            act.wait_ge(sem("negabs_s"), 1)
            link(act.activation(sa_, sa_, ACT.Exp))
            act.activation(sa_, sa_, ACT.Ln, bias=1.0).then_inc(sem("ln_s"), 1)
            act.wait_ge(sem("arg_s"), 2)
            zsf = zs[:].rearrange("p b n h -> p (b n h)")
            act.activation(zsf, sa_, ACT.Exp).then_inc(sem("w_s"), 1)
            for g4 in range(4):
                for hp in range(2):
                    h = 2 * g4 + hp
                    move(("z", g4, hp), zp[:, hp, :], lambda b: b[:, 0:384], ACT.Identity, scale=SB_SCALE, bias=sb_bias[:, h:h + 1])
                act.wait_ge(sem("negabs_p"), g4 + 1)
                link(act.activation(np_, np_, ACT.Exp))
                act.activation(np_, np_, ACT.Ln, bias=1.0).then_inc(sem("ln_p"), 1)
                act.wait_ge(sem("arg_p"), g4 + 1)
                act.activation(wp_, zp, ACT.Exp).then_inc(sem("exp_p"), 1)
                move(("so", g4), pT[:, Q0 + g4, 0:256], lambda b: b[:, 0:256])
            def gate_sums(br, tiles):
                for dt in tiles:
                    move(("gate", br, dt), gate_at(dt), lambda b: b[:, 0:T])

            def gate_sigmoid(br):
                gone(act, ("gate", br, KT - 2))
                gone(act, ("gate", br, KT - 1))
                act.activation(gates, gates, ACT.Sigmoid).then_inc(sem("gates_ready"), 1)

            for h in range(MH):
                act.wait_ge(sem("mem_max"), h + 1)
                b = take(act, ("mz", h))
                for qt in range(2):
                    ins = act.activation(mp[:, qt, :], b[:, 256 * qt:256 * qt + 256], ACT.Exp, scale=MEM_SCALE,
                                         bias=mst[:, 2 + qt:3 + qt], accum_out=mst[:, 4 + qt:5 + qt])
                ins.then_inc(freed_by(("mz", h)), 1)
                gate_sums(0, (2 * h,))
                move(("mpT", h), mpT.rearrange("p a b -> p (a b)"), lambda b: b[:, :])
                gate_sums(0, (2 * h + 1,))
                move(("mo", h), pT[:, MQ0 + h, 0:256], lambda b: b[:, 0:256])
            move("so_s", orow[0:NB, :], lambda b: b[0:NB, :])
            move("so_sT", pT[:, Q0:Q0 + 4, NP_TOK:T], lambda b: b[:, 0:32].rearrange("p (t b) -> p t b", t=4))
            act.wait_ge(sem("mem_max_s"), 1)
            b = take(act, "mzT")
            act.activation(mps[0:32, :], b[0:32, 0:256], ACT.Exp, scale=MEM_SCALE, bias=mst[0:32, 8:9],
                           accum_out=mst[0:32, 9:10]).then_inc(freed_by("mzT"), 1)
            move("mpTs", mpTs.rearrange("p a b -> p (a b)"), lambda b: b[:, 0:64])
            move("mo_s", orow[0:NB, :], lambda b: b[0:NB, :])
            move("mo_sT", pT[:, MQ0:MQ0 + 4, NP_TOK:T], lambda b: b[:, 0:32].rearrange("p (t b) -> p t b", t=4))

            gate_sigmoid(0)
            for dt in range(4):
                move(("o", 0, dt), mergedT[:, dt, :], lambda b: b[:, 0:T])

            def beside_moves(it, place):
                for kind, br, dt in ending_at(it, place):
                    if kind == "o":
                        if dt >= 3:
                            act.wait_ge(sem("branch_summed"), KT + dt - 2)
                        move(("o", 1, dt), o_mem[dt % 3], lambda b: b[:, 0:T])
                    else:
                        act.wait_ge(sem("branch_summed"), 2 * KT)
                        gate_sums(2, (dt,))

            act.wait_ge(sem("mixed"), 1)
            act.activation(pT[0:64, 28, :], pT[0:64, 28, :], ACT.Tanh).then_inc(sem("lora_act"), 1)
            act.activation(pT[:, 29, :], pT[:, 29, :], ACT.Sigmoid).then_inc(sem("lora_act"), 1)
            for t in range(4):
                move(("dec", t), LD[:, t, :], lambda b: b[:, 0:T], ACT.Sigmoid, bias=col(DE0 + t))
            for t in range(4):
                move(("aaa", t), AA[:, t, :], lambda b: b[:, 0:T], ACT.Sigmoid, bias=col(AA0 + t))
            for t in range(4):
                move(("gr", t), GG[:, t, :], lambda b: b[:, 0:T])
            for t in range(4):
                move(("kn", t), T2[:, t, :], lambda b: b[:, 0:T], ACT.Sqrt)
            for dt in range(4, KT):
                move(("o", 0, dt), mergedT[:, dt, :], lambda b: b[:, 0:T])
            act.wait_ge(sem("branch_summed"), 8)
            gate_sums(1, range(4))
            act.wait_ge(sem("cum"), 1)
            act.activation(T2[:, :, 0:256], T2[:, :, 0:256], ACT.Exp, scale=DECAY)
            act.activation(LD[:, :, 256:T], LD[:, :, 256:T], ACT.Exp, scale=DECAY)
            act.activation(LD[:, :, 0:256], T1[:, :, 0:256], ACT.Exp, scale=DECAY).then_inc(sem("act_chain"), 1)
            link.at = link.at + 1
            act.wait_ge(sem("act_chain"), link.at)
            act.activation(T1[:, :, 0:256], T1[:, :, 0:256], ACT.Exp, scale=-DECAY).then_inc(sem("decays"), 1)
            gate_sums(1, (4, 5))
            for t in range(4):
                move(("st", t), St[:, t].rearrange("p b v -> p (b v)"), lambda b: b[:, :])
            gate_sums(1, (6, 7))
            gate_sigmoid(1)
            for j in range(8):
                move(("so_out", j), SN[0:64, 4 * (j % 2):4 * (j % 2) + 4, j // 2, :],
                     lambda b: b[0:64, :].rearrange("p (i n) -> p i n", i=4))
            act.wait_ge(sem("hats"), 1)
            for hp in range(2):
                rows = slice(64 * hp, 64 * hp + 64)
                move(("ys", hp), T1[rows, :, 256:T], lambda b: b[rows, 0:32].rearrange("p (t b) -> p t b", t=4))
            act.wait_ge(sem("arena_clear"), 2)
            for it in range(4):
                tt, hh = it // 2, it % 2
                n = (tt, hh)
                move(("tab",) + n, tokAB.rearrange("p a b -> p (a b)"), lambda b: b[:, :])
                move(("tkv",) + n, tokKV.rearrange("p a b -> p (a b)"), lambda b: b[:, :])
                beside_moves(it, "start")
                for lv in range(5):
                    move(("X", lv) + n, Xm.rearrange("p a b -> p (a b)"), lambda b: b[:, :])
                    beside_moves(it, f"X{lv}")
                move(("MV",) + n, MVs.rearrange("p a b -> p (a b)"), lambda b: b[:, 0:256])
                beside_moves(it, "MV")
                move(("Z",) + n, Zs.rearrange("p a b -> p (a b)"), lambda b: b[:, 0:256])
                move(("WT",) + n, WTs.rearrange("p a b -> p (a b)"), lambda b: b[:, 0:256])
                for place in ("WT", "U0", "U1"):
                    beside_moves(it, place)
                move(("Y",) + n, T1[:, 2 * hh:2 * hh + 2, tt * P:tt * P + P], lambda b: b[:, 0:256].rearrange("p (a b) -> p a b", a=2))
            move("wkv_out", Nm[0].rearrange("p a b -> p (a b)"), lambda b: b[:, :])
            for t in range(4):
                move(("gv", t), T2[:, t, :], lambda b: b[:, 0:T], ACT.Sqrt, bias=eps[:, 0:1])

            gate_sums(2, (7,))
            gate_sigmoid(2)

            def norm_deviation(i):
                act.wait_ge(sem("mean"), i + 1)
                tt = H1_ORDER[i % 3]
                rows = TOK[tt][1]
                src = (h1 if i < 3 else yacc)
                link(act.activation(sq[0:rows, :], src[0:rows, tt, :], ACT.Square, bias=st_[0:rows, 8 * tt + 3:8 * tt + 4],
                                    accum_out=st_[0:rows, 8 * tt + 1:8 * tt + 2]))
                act.activation(st_[0:rows, 8 * tt + 2:8 * tt + 3], st_[0:rows, 8 * tt + 1:8 * tt + 2], ACT.Sqrt,
                               scale=1.0 / D, bias=eps[0:rows, 1:2]).then_inc(sem("deviation"), 1)

            for i, tt in enumerate(H1_ORDER):
                norm_deviation(i)
                t0, rows = TOK[tt]
                for j in range(2):
                    move(("h1T", tt, j), h1T[:, 4 * j:4 * j + 4, t0:t0 + rows],
                         lambda b: b[:, :].rearrange("p (k n) -> p k n", k=4)[:, :, 0:rows])
            act.wait_ge(sem("logits"), 1)
            for tt in range(3):
                ins = act.activation(tmpE[:, tt, 0:NE], lg[:, tt, 0:NE], ACT.Exp, bias=st_[:, 8 * tt:8 * tt + 1])
            ins.then_inc(sem("exp_logits"), 1)

            def gathered_rows(n_before):
                act.wait_ge(sem("gathered"), n_before + 1)
                for i in range(2):
                    act.activation(xg[:, 4 * i:4 * i + 4, :], bank[i][:, :].rearrange("p (k n) -> p k n", k=4),
                                   ACT.Copy).then_inc(sem("xg_ready"), 1)

            def pair(it, gathers):
                def gate(u):
                    act.wait_ge(sem("g_ready"), it * 8 + (u + 1))
                    act.activation(sg[u % 2], gb[u % 2], ACT.Sigmoid, scale=SWA).then_inc(sem("sg_ready"), 1)

                def turned(u):
                    act.wait_ge(sem("h_turned"), it * 8 + (u + 1))
                    ei, j = u // 4, u % 4
                    act.activation(hT[ei][:, 2 * j:2 * j + 2, :], bank[6 + j % 2][:, 0:P].rearrange("p (a b) -> p a b", a=2),
                                   ACT.Copy).then_inc(sem("hT_ready"), 1)

                for u in (0, 4):
                    gate(u)
                    gate(u + 1)
                    turned(u)
                    gate(u + 2)
                    turned(u + 1)
                    gate(u + 3)
                    turned(u + 2)
                    if u:
                        act.wait_ge(sem("onewT_full"), it + 2)
                        act.activation(onewT, bank[2][:, 0:T], ACT.Copy).then_inc(sem("onewT_ready"), 1)
                        turned(7)
                        gathered_rows(gathers)
                    else:
                        turned(3)
                act.wait_ge(sem("down_full"), it * 4 + 4)
                act.activation(ysb[:, 0:512], bank[4][:, :], ACT.Copy)
                act.activation(ysb[0:64, 512:D], bank[5][64:128, :], ACT.Copy)
                act.activation(ysb[64:128, 512:D], bank[5][0:64, :], ACT.Copy).then_inc(sem("y_moved"), 1)

            gathered_rows(0)
            with act.Fori(0, NE // 2) as p:
                pair(p, p + 1)
            act.wait_ge(sem("flag_ready"), 1)
            over = act.value_load(flag[0:1, 0:1], min_val=0, max_val=T)
            with act.If(over > CAP):
                with act.Fori(0, ROUNDS) as r:
                    gathered_rows((r + 1) * (NE // 2 + 1))
                    with act.Fori(0, NE // 2) as p:
                        pair((r + 1) * (NE // 2) + p, (r + 1) * (NE // 2 + 1) + p + 1)
            for i in range(3, 6):
                norm_deviation(i)

        @block.vector
        def _(v):
            link = Chain(v, sem("dve_chain"))
            tt_, ts, stt = v.tensor_tensor, v.tensor_scalar, v.scalar_tensor_tensor

            def move(name, dst, src_of):
                b = take(v, name)
                v.tensor_copy(dst, src_of(b)).then_inc(freed_by(name), 1)

            for k in range(1, KT, 2):
                move(("xT", k), xT[:, k, :], lambda b: b[:, 0:T])

            for b_ in range(NB):
                q = take(v, ("qb", b_))
                for half in range(2):
                    name = ("K", 2 * b_ + half)
                    arrived(v, name)
                    k = slot(name).rearrange("p (n f) -> p n f", n=8)
                    prod_ = tt_(k, k, q[:, :].unsqueeze(1).to_broadcast([P, 8, W5]), ALU.mult)
                    if half:
                        prod_.then_inc(freed_by(("qb", b_)), 1)
                        gone(v, ("qb", b_))
                    else:
                        link(prod_)
                    v.tensor_reduce(zs[:, b_, 8 * half:8 * half + 8, :], slot(name).rearrange("p (n h d) -> p n h d", n=8, h=SBH),
                                    AX.X, ALU.add).then_inc(sem("k_used"), 1)
            for ft in range(RW0, FT):
                gone(v, ("p", ft))
            v.tensor_copy(psh[:], pT[:, RW0:FT, 255:T]).then_inc(sem("shift_cut"), 1)
            v.wait_ge(sem("k_used"), 2 * NB)
            v.wait_ge(sem("bias_in"), 16)
            z2 = zs[:].rearrange("p b n h -> p (b n) h")
            link(stt(z2, z2, SB_SCALE, sb_bias[:].unsqueeze(1).to_broadcast([P, NB * PAGES, SBH]), ALU.mult, ALU.add))
            zsf = zs[:].rearrange("p b n h -> p (b n h)")
            stt(sa_, zsf, -1.0, zsf, ALU.mult, ALU.min).then_inc(sem("negabs_s"), 1)
            v.wait_ge(sem("ln_s"), 1)
            link(stt(sb_, zsf, 0.0, sa_, ALU.max, ALU.add))
            link(v.memset(spx[:, :, PAGES - 1, :], 0.0))
            spv = sb_.rearrange("p (b n h) -> p b n h", b=NB, n=PAGES)
            for n in range(PAGES - 2, -1, -1):
                ins = tt_(spx[:, :, n, :], spx[:, :, n + 1, :], spv[:, :, n + 1, :], ALU.add)
                if n:
                    link(ins)
                else:
                    ins.then_inc(sem("sp_s"), 1)
            for i in range(2):
                b = take(v, ("cs_s", i))
                c = slice(512 * i, 512 * i + 512)
                ins = tt_(sa_[:, c], zsf[:, c], b[:, :], ALU.subtract)
                ins.then_inc(freed_by(("cs_s", i)), 1)
            for i in range(2):
                gone(v, ("cs_s", i))
            v.sem_inc(sem("arg_s"), 2)

            v.wait_ge(sem("tri_ready"), 1)
            tri2 = tri_lt[:].unsqueeze(1).to_broadcast([P, 2, P])

            def causal(buf):
                tt_(buf[:, :, 0:128], buf[:, :, 0:128], tri2, ALU.mult)
                return tt_(buf[:, :, 256:384], buf[:, :, 256:384], tri2, ALU.mult)

            def keep_own(bq):
                b = take(v, ("pv", bq))
                if bq >= 2:
                    v.wait_ge(sem("pv_summed"), bq - 1)
                tt_(pvm[bq % 2], b[:, :], m_page[:], ALU.mult).then_inc(freed_by(("pv", bq)), 1)
                gone(v, ("pv", bq))
                v.sem_inc(sem("pv_kept"), 1)

            v.wait_ge(sem("masks"), 7)
            for g4 in range(4):
                for hp in range(2):
                    gone(v, ("z", g4, hp))
                stt(np_, zp, -1.0, zp, ALU.mult, ALU.min).then_inc(sem("negabs_p"), 1)
                v.wait_ge(sem("ln_p"), g4 + 1)
                link(stt(sp_, zp, 0.0, np_, ALU.max, ALU.add))
                causal(sp_).then_inc(sem("sp_p"), 1)
                keep_own(g4)
                for hp in range(2):
                    b = take(v, ("cs", g4, hp))
                    tt_(zp[:, hp, :], zp[:, hp, :], b[:, 0:384], ALU.subtract).then_inc(freed_by(("cs", g4, hp)), 1)
                for hp in range(2):
                    gone(v, ("cs", g4, hp))
                ts(zp, zp, 0.0, None, ALU.min).then_inc(sem("arg_p"), 1)
                v.wait_ge(sem("exp_p"), g4 + 1)
                causal(wp_).then_inc(sem("w_p"), 1)

            for h in range(MH):
                b = take(v, ("mz", h))
                link(v.reduce_max(mst[:, 0:2], b[:, :].rearrange("p (a b) -> p a b", a=2), AX.X))
                ts(mst[:, 2:4], mst[:, 0:2], -MEM_SCALE, None, ALU.mult).then_inc(sem("mem_max"), 1)
                gone(v, ("mz", h))
                link(v.reciprocal(mst[:, 6:8], mst[:, 4:6]))
                for qt in range(2):
                    ins = ts(mp[:, qt, :], mp[:, qt, :], mst[:, 6 + qt:7 + qt], None, ALU.mult)
                ins.then_inc(sem("mp"), 1)
                keep_own(4 + h)
            for b_ in range(NB):
                name = ("mK", b_ // 4)
                q = take(v, ("mqb", b_))
                arrived(v, name)
                k = slot(name).rearrange("p (b m f) -> p b m f", b=4, m=2)[:, b_ % 4]
                tt_(k, k, q[:, :].unsqueeze(1).to_broadcast([P, 2, W5]), ALU.mult).then_inc(freed_by(("mqb", b_)), 1)
                gone(v, ("mqb", b_))
                ins = v.tensor_reduce(zm[:, :, MH * b_:MH * b_ + MH], k.rearrange("p m (h d) -> p m h d", h=MH), AX.X, ALU.add)
                if b_ % 4 == 3:
                    ins.then_inc(sem("mk_used"), 1)
                else:
                    link(ins)
            v.wait_ge(sem("mk_used"), 2)
            v.sem_inc(sem("zm"), 1)
            b = take(v, "mzT")
            link(v.reduce_max(mst[0:32, 10:11], b[0:32, 0:256], AX.X))
            ts(mst[0:32, 8:9], mst[0:32, 10:11], -MEM_SCALE, None, ALU.mult).then_inc(sem("mem_max_s"), 1)
            gone(v, "mzT")
            link(v.reciprocal(mst[0:32, 11:12], mst[0:32, 9:10]))
            ts(mps[0:32, :], mps[0:32, :], mst[0:32, 11:12], None, ALU.mult).then_inc(sem("mps"), 1)
            v.wait_ge(*full_of("so_s"))
            for i in range(2):
                b = take(v, ("mpv", i))
                tt_(pvm[i], b[:, :], m_mem[i], ALU.mult).then_inc(freed_by(("mpv", i)), 1)

            gone(v, "shift_in")
            v.wait_ge(*full_of("mo_sT"))
            v.wait_ge(sem("arena_clear"), 1)
            v.sem_inc(sem("rw_clear"), 1)
            for g0 in (12, 4, 0, 8):
                n = min(4, RWT - g0)
                p = pT[:, RW0 + g0:RW0 + g0 + n, :]
                d = T1[:, 0:n, :]
                tt_(d[:, :, 1:256], p[:, :, 0:255], p[:, :, 1:256], ALU.subtract)
                ts(d[:, :, 0:1], p[:, :, 0:1], -1.0, None, ALU.mult)
                link(tt_(d[:, :, 256:T], shT[:, g0:g0 + n, :], p[:, :, 256:T], ALU.subtract))
                for i in range(n):
                    ins = stt(p[:, i, :], d[:, i, :], col(MU + g0 + i), p[:, i, :], ALU.mult, ALU.add)
                link(ins)
                if g0 == 12:
                    v.sem_inc(sem("mixed"), 1)
            R, Kx, Vx = pT[:, RW0:RW0 + 4, :], pT[:, 20:24, :], pT[:, 24:28, :]

            def per_tile(dst, src, c0, op=ALU.mult, op1=None, s2=None):
                for t in range(4):
                    if op1 is None:
                        ins = ts(dst[:, t, :], src[:, t, :], col(c0 + t), None, op)
                    else:
                        ins = ts(dst[:, t, :], src[:, t, :], s2, col(c0 + t), op, op1)
                return ins

            link(per_tile(KK, Kx, KKp))
            tt_(T1, KK, KK, ALU.mult).then_inc(sem("kk_sq"), 1)
            for t in range(4):
                gone(v, ("kn", t))
            link(ts(T2, T2, 1e-12, None, ALU.max))
            link(v.reciprocal(T2, T2))
            link(tt_(KK, KK, T2, ALU.mult))
            for t in range(4):
                gone(v, ("aaa", t))
            link(per_tile(T2, AA, KAp, ALU.add, ALU.mult, -1.0))
            link(stt(KM, T2, 1.0, Kx, ALU.add, ALU.mult))
            link(tt_(T1, R, KM, ALU.mult))
            per_tile(T1, T1, RKp).then_inc(sem("rk_prod"), 1)
            for t in range(4):
                b = take(v, ("bon", t))
                tt_(BON[:, t, :], b[:, 0:T], Vx[:, t, :], ALU.mult).then_inc(freed_by(("bon", t)), 1)
            link(tt_(AA, KK, AA, ALU.mult))
            v.wait_ge(sem("masks"), 7)
            for t in range(4):
                ins = v.tensor_tensor_scan(T1[:, t, 0:256], scanm[:], LD[:, t, 0:256], 0.0, ALU.mult, ALU.add)
            link(ins)
            tt_(T2[:, :, 0:256], T1[:, :, 0:256], LD[:, :, 0:256], ALU.subtract).then_inc(sem("cum"), 1)
            v.wait_ge(sem("decays"), 1)
            pr = slice(0, 256)
            stt(KK[:, :, pr], KK[:, :, pr], -1.0, T2[:, :, pr], ALU.mult, ALU.mult)
            tt_(AA[:, :, pr], AA[:, :, pr], T1[:, :, pr], ALU.mult)
            tt_(KM[:, :, pr], KM[:, :, pr], T1[:, :, pr], ALU.mult)
            tt_(R[:, :, pr], R[:, :, pr], LD[:, :, pr], ALU.mult).then_inc(sem("hats"), 1)

            sv1 = lambda a, t: a[:, t, NP_TOK:T].unsqueeze(2).to_broadcast([P, NB, 64])
            for t in range(4):
                gone(v, ("st", t))
            for t in range(4):
                ins = tt_(S1[:, t], St[:, t], sv1(KK, t), ALU.mult)
            ins.then_inc(sem("s_kk"), 1)
            for t in range(4):
                ins = tt_(St[:, t], St[:, t], sv1(LD, t), ALU.mult)
            link(ins)
            for nm, coef, op in (("sa", AA, ALU.subtract), ("vb", KM, ALU.add)):
                for t in range(4):
                    b = take(v, (nm, t))
                    tt_(S1[:, t], b[:, :].rearrange("p (b v) -> p b v", b=NB), sv1(coef, t), ALU.mult).then_inc(freed_by((nm, t)), 1)
                for t in range(4):
                    gone(v, (nm, t))
                for t in range(4):
                    ins = tt_(St[:, t], St[:, t], S1[:, t], op)
                if nm == "sa":
                    link(ins)
                else:
                    ins.then_inc(sem("s_new"), 1)

            v.wait_ge(sem("arena_clear"), 2)
            v.memset(Sb[0], 0.0).then_inc(sem("S_zero"), 1)
            v.wait_ge(sem("S_zero"), 1)
            m2 = lambda m: m[:].unsqueeze(1).to_broadcast([P, 2, P])
            m4 = lambda m: m[:].unsqueeze(1).to_broadcast([P, 4, P])
            for it in range(4):
                tt, hh = it // 2, it % 2
                n = (tt, hh)
                part = lambda b, i: b[:, 256 * i:256 * i + 256].rearrange("p (a b) -> p a b", a=2)
                for hp in range(2):
                    u = slice(2 * hp, 2 * hp + 2)
                    b = take(v, ("g1", hp) + n)
                    tt_(Nl[:, u], part(b, 1), m2(m_lo), ALU.mult)
                    tt_(Nt[:, u], part(b, 0), m2(m_up), ALU.mult).then_inc(freed_by(("g1", hp) + n), 1)
                for hp in range(2):
                    gone(v, ("g1", hp) + n)
                tt_(Tm, Nl, m4(lev[0]), ALU.mult)
                link(tt_(Tt, Nt, m4(lev[0]), ALU.mult))
                tt_(Tm, Tm, m4(ident), ALU.add)
                tt_(Tt, Tt, m4(ident), ALU.add).then_inc(sem("T_ready"), 1)
                for hp in range(2):
                    u = slice(2 * hp, 2 * hp + 2)
                    b = take(v, ("g2", hp) + n)
                    tt_(RB[:, u], part(b, 0), m2(m_upi), ALU.mult)
                    tt_(AK[:, u], part(b, 1), m2(m_up), ALU.mult).then_inc(freed_by(("g2", hp) + n), 1)
                    b = take(v, ("g3", hp) + n)
                    tt_(RK[:, u], part(b, 0), m2(m_upi), ALU.mult).then_inc(freed_by(("g3", hp) + n), 1)
                v.wait_ge(sem("T_ready"), it + 1)
                for lv in range(5):
                    if lv < 4:
                        b = take(v, ("TX", lv) + n)
                        tt_(Tm, Tm, b[:, :].rearrange("p (a b) -> p a b", a=4), ALU.add).then_inc(freed_by(("TX", lv) + n), 1)
                        gone(v, ("TX", lv) + n)
                    b = take(v, ("XT", lv) + n)
                    tt_(Tt, Tt, b[:, :].rearrange("p (a b) -> p a b", a=4), ALU.add).then_inc(freed_by(("XT", lv) + n), 1)
                    gone(v, ("XT", lv) + n)
                gone(v, ("Z",) + n)
                for cc in range(2):
                    c = 2 * tt + cc
                    rows = slice(64 * cc, 64 * cc + 64)
                    for tl in range(2):
                        ins = ts(PM[:, tl, :], blk[:], LD[:, 2 * hh + tl, C * c + C - 1:C * c + C], None, ALU.mult)
                    link(ins)
                    b = take(v, ("U", cc) + n)
                    tt_(Us.rearrange("p a b -> p (a b)")[rows], b[rows, 0:256], Zs.rearrange("p a b -> p (a b)")[rows],
                        ALU.add).then_inc(freed_by(("U", cc) + n), 1)
                    b = take(v, ("dS", cc) + n)
                    tt_(tS, b[:, 0:256].rearrange("p (a b) -> p a b", a=2), Sb[c % 3][:, 2 * hh:2 * hh + 2, :],
                        ALU.add).then_inc(freed_by(("dS", cc) + n), 1)
                    gone(v, ("dS", cc) + n)
                    tt_(Sb[(c + 1) % 3][:, 2 * hh:2 * hh + 2, :], tS, PM, ALU.mult).then_inc(sem("S_ready"), 1)
                    v.wait_ge(sem("S_ready"), 2 * it + cc + 1)
            for t in range(4):
                b = take(v, ("gm", t))
                tt_(T1[:, t, :], T1[:, t, :], b[:, 0:T], ALU.subtract).then_inc(freed_by(("gm", t)), 1)
            for t in range(4):
                gone(v, ("gm", t))
            tt_(T2, T1, T1, ALU.mult).then_inc(sem("y_sq"), 1)
            for t in range(4):
                gone(v, ("gv", t))
            link(v.reciprocal(T2, T2))
            for t in range(4):
                ins = stt(T1[:, t, :], T1[:, t, :], col(GNG + t), T2[:, t, :], ALU.mult, ALU.mult)
            link(ins)
            for t in range(4):
                ins = stt(T1[:, t, :], T1[:, t, :], col(GNB + t), BON[:, t, :], ALU.add, ALU.add)
            link(ins)
            link(tt_(R, T1, GG, ALU.mult))
            v.sem_inc(sem("rw_done"), 2)

            v.wait_ge(sem("gates_ready"), 3)
            v.wait_ge(sem("branch_summed"), 16)
            for dt in range(KT):
                b = take(v, ("o", 2, dt))
                tt_(gate_at(dt), b[:, 0:T], gate_at(dt), ALU.mult).then_inc(freed_by(("o", 2, dt)), 1)
                gone(v, ("o", 2, dt))
                link(tt_(mergedT[:, dt, :], mergedT[:, dt, :], gate_at(dt), ALU.add))
            v.sem_inc(sem("merged"), 1)

            def norm_mean(x, tt):
                rows = TOK[tt][1]
                s = lambda j: st_[0:rows, 8 * tt + j:8 * tt + j + 1]
                link(v.reduce_sum(s(0), x[0:rows, tt, :], AX.X))
                ts(s(3), s(0), -1.0 / D, None, ALU.mult).then_inc(sem("mean"), 1)

            def norm_apply(x, tt, i, g_, b_, ready):
                rows = TOK[tt][1]
                xr_ = x[0:rows, tt, :]
                s = lambda j: st_[0:rows, 8 * tt + j:8 * tt + j + 1]
                v.wait_ge(sem("mean"), i + 1)
                v.wait_ge(sem("deviation"), i + 1)
                link(v.reciprocal(s(4), s(2)))
                link(ts(xr_, xr_, s(3), s(4), ALU.add, ALU.mult))
                link(tt_(xr_, xr_, g_[0:rows, :], ALU.mult))
                tt_(xr_, xr_, b_[0:rows, :], ALU.add).then_inc(sem(ready), 1)

            v.memset(lg, 0.0)
            link(v.memset(pos, -1.0))
            v.wait_ge(sem("ln_in"), 144)

            for i, tt in enumerate(H1_ORDER):
                rows = TOK[tt][1]
                if tt == 2:
                    b = take(v, "res_s")
                    for half in range(2):
                        c = slice(512 * half, 512 * half + 512)
                        link(stt(h1[0:rows, tt, c], xres[0:rows, tt, c], ALPHA, b[32 * half:32 * half + rows, :], ALU.mult, ALU.add))
                        ins = tt_(h1[0:rows, tt, c], h1[0:rows, tt, c], b[64 + 32 * half:64 + 32 * half + rows, :], ALU.add)
                        if half == 0:
                            link(ins)
                    ins.then_inc(freed_by("res_s"), 1)
                    gone(v, "res_s")
                else:
                    for half in range(2):
                        b = take(v, ("res", tt, half))
                        c = slice(512 * half, 512 * half + 512)
                        stt(h1[0:rows, tt, c], xres[0:rows, tt, c], ALPHA, b[0:rows, :], ALU.mult, ALU.add
                            ).then_inc(freed_by(("res", tt, half)), 1)
                    for half in range(2):
                        gone(v, ("res", tt, half))
                norm_mean(h1, tt)
                norm_apply(h1, tt, i, lng, lnb, "h1")
            for tt in H1_ORDER:
                rows = TOK[tt][1]
                b = take(v, ("logit", tt))
                tt_(lg[0:rows, tt, 0:NE], b[0:rows, 0:NE], brt[0:rows, :], ALU.add).then_inc(freed_by(("logit", tt)), 1)
                gone(v, ("logit", tt))
            L, E, S_, W_, N_ = (a[:, :, 0:NE] for a in (lg, tmpE, sel, wt, pos))
            each = lambda a: a.unsqueeze(2).to_broadcast([P, 3, NE])
            stat = lambda j: st_[:, :].rearrange("p (t j) -> p t j", j=8)[:, :, j]
            mxv = mx8.rearrange("p (t j) -> p t j", j=8)
            v.memset(wt, 0.0)
            for tt in range(3):
                ins = v.max(mxv[:, tt, :], L[:, tt, :])
            link(ins)
            ts(stat(0), mxv[:, :, 0], -1.0, None, ALU.mult).then_inc(sem("logits"), 1)
            tt_(W_, L, each(mxv[:, :, 3]), ALU.is_equal)
            link(tt_(S_, L, each(mxv[:, :, 3]), ALU.is_gt))
            link(v.reduce_sum(stat(1), S_, AX.X))
            ts(stat(2), stat(1), -1.0, 4.0, ALU.mult, ALU.add)
            for tt in range(3):
                ins = v.tensor_tensor_scan(N_[:, tt, :], ones[:, 0:NE], W_[:, tt, :], 0.0, ALU.mult, ALU.add)
            link(ins)
            link(tt_(N_, N_, each(stat(2)), ALU.is_le))
            link(tt_(W_, W_, N_, ALU.mult))
            link(tt_(S_, S_, W_, ALU.add))
            v.wait_ge(sem("exp_logits"), 1)
            link(tt_(E, E, S_, ALU.mult))
            link(v.reduce_sum(stat(3), E, AX.X))
            link(v.reciprocal(stat(4), stat(3)))
            link(tt_(W_, E, each(stat(4)), ALU.mult))
            v.sem_inc(sem("sel_ready"), 1)
            b = take(v, "rank")
            stt(pos[:, 0:2, 0:NE], b[:, 0:2 * NE].rearrange("p (t e) -> p t e", t=2), 1.0, sel[:, 0:2, 0:NE], ALU.add, ALU.mult)
            link(stt(pos[0:NB, 2, 0:NE], b[0:NB, 2 * NE:3 * NE], 1.0, sel[0:NB, 2, 0:NE], ALU.add, ALU.mult))

            def one_hot(p, n_before, first=False):
                if not first:
                    v.wait_ge(sem("gathered"), n_before)
                tt_(oneh, iota[:].unsqueeze(1).unsqueeze(1).to_broadcast([P, 3, 2, CAP]),
                    pos[:, :, bass.ds(2 * p, 2)].unsqueeze(3).to_broadcast([P, 3, 2, CAP]), ALU.is_equal
                    ).then_inc(sem("oneh_ready"), 1)

            def pair(p, it, gathers):
                v.wait_ge(sem("onewT_full"), it + 1)
                v.wait_ge(sem("oneh_ready"), gathers)
                tt_(onew, oneh, wt[:, :, bass.ds(2 * p, 2)].unsqueeze(3).to_broadcast([P, 3, 2, CAP]), ALU.mult
                    ).then_inc(sem("onew_ready"), 1)
                v.wait_ge(sem("onew_ready"), it + 1)
                one_hot(p + 1, gathers)
                for ei in range(2):
                    ins = v.tensor_copy(pick_e[ei], ident[:, bass.ds(2 * p + ei, 1)].to_broadcast([P, CAP]))
                ins.then_inc(sem("pick_ready"), 1)
                for u in range(8):
                    ei, j = u // 4, u % 4
                    g_, l_, h_, s_ = gb[u % 2], lb[u % 2], hb[u % 2], sg[u % 2]
                    v.wait_ge(sem("up_full"), it * 8 + (u + 1))
                    chunk = bank[2 + j % 2]
                    ts(g_, chunk[:, 0:256:2], LIMIT, None, ALU.min).then_inc(sem("g_ready"), 1)
                    ts(l_, chunk[:, 1:256:2], LIMIT, -LIMIT, ALU.min, ALU.max).then_inc(sem("swiglu_step"), 1)
                    v.wait_ge(sem("swiglu_step"), it * 16 + (2 * u + 1))
                    v.wait_ge(sem("g_ready"), it * 8 + (u + 1))
                    stt(l_, l_, 1.0, g_, ALU.add, ALU.mult).then_inc(sem("swiglu_step"), 1)
                    v.wait_ge(sem("swiglu_step"), it * 16 + (2 * u + 2))
                    v.wait_ge(sem("sg_ready"), it * 8 + (u + 1))
                    tt_(h_, l_, s_, ALU.mult).then_inc(sem("h_ready"), 1)
                for i in range(6):
                    tt, half = i // 2, i % 2
                    rows = TOK[tt][1]
                    c = slice(512 * half, 512 * half + 512)
                    v.wait_ge(sem("scatter_full"), it * 6 + (i + 1))
                    v.wait_ge(sem("scatter_added"), it * 6 + (i + 1))
                    tt_(yacc[0:rows, tt, c], yacc[0:rows, tt, c], bank[6 + i % 2][0:rows, :], ALU.add
                        ).then_inc(sem("scatter_added"), 1)

            v.sem_inc(sem("scatter_added"), 1)
            one_hot(0, 0, True)
            v.reduce_max(st_[:, 5:6], b[:, 96:96 + NE], AX.X).then_inc(freed_by("rank"), 1)
            gone(v, "rank")
            v.tensor_copy(flag[:], st_[:, 5:6]).then_inc(sem("flag_ready"), 1)
            v.wait_ge(sem("y_zero"), 1)
            with v.Fori(0, NE // 2) as p:
                pair(p, p, p + 1)
            v.wait_ge(sem("flag_ready"), 1)
            over = v.value_load(flag[0:1, 0:1], min_val=0, max_val=T)
            with v.If(over > CAP):
                with v.Fori(0, ROUNDS) as r:
                    ts(pos, pos, float(-CAP), None, ALU.add).then_inc(sem("pos_moved"), 1)
                    v.wait_ge(sem("pos_moved"), r + 1)
                    one_hot(0, (r + 1) * (NE // 2 + 1))
                    with v.Fori(0, NE // 2) as p:
                        pair(p, (r + 1) * (NE // 2) + p, (r + 1) * (NE // 2 + 1) + p + 1)
                v.wait_ge(sem("scatter_added"), 6 * (ROUNDS + 1) * (NE // 2) + 1)
            v.wait_ge(sem("scatter_added"), 6 * (NE // 2) + 1)
            def residual(tt):
                rows = TOK[tt][1]
                link(stt(yacc[0:rows, tt, :], h1[0:rows, tt, :], ALPHA, yacc[0:rows, tt, :], ALU.mult, ALU.add))
                norm_mean(yacc, tt)

            residual(H1_ORDER[0])
            for i, tt in enumerate(H1_ORDER):
                if i < 2:
                    residual(H1_ORDER[i + 1])
                norm_apply(yacc, tt, 3 + i, ln2g, ln2b, "y_ready")


_INS = ["x_prompt", "x_sample", "cache_sb_k", "cache_sb_v", "cache_mem_k", "cache_mem_v", "state_rw_shift",
        "state_rw_wkv", "page_table", "mem_prompt", "w_in", "sb_bias", "mu_rw", "w_decay0", "w_decay2", "w_aaa0",
        "w_aaa2", "w_gate2", "rw_k_k", "rw_k_a", "rw_r_k", "rw_gn_g", "rw_gn_b", "w_mem_kv", "w_sb_o", "w_mem_o",
        "w_rw_o", "w_out", "ln1_g", "ln1_b", "w_router", "b_router", "w_gate_up", "b_gate_up", "w_down", "b_down",
        "ln2_g", "ln2_b"]
_OUTS = {"y_prompt": (1, 256, 1024), "y_sample": (8, 1, 1024), "sb_k_prompt": (1, 1, 256, 8, 64),
         "sb_v_prompt": (1, 1, 256, 8, 64), "mem_k": (1, 1, 256, 4, 128), "mem_v": (1, 1, 256, 4, 128),
         "shift_prompt": (1, 1, 1792), "wkv_prompt": (1, 1, 8, 64, 64), "sb_k_sample": (1, 8, 1, 8, 64),
         "sb_v_sample": (1, 8, 1, 8, 64), "shift_sample": (1, 8, 1792), "wkv_sample": (1, 8, 8, 64, 64)}


def kernel(**inputs):
    import concourse.bacc as bacc
    from concourse.bass_utils import run_bass_kernel_spmd

    nc = bacc.Bacc("TRN2", target_bir_lowering=False, num_devices=1)
    arrays, ins = {}, {}
    for name in _INS:
        a = np.ascontiguousarray(inputs[name])
        arrays[f"in_{name}"] = a
        ins[name] = nc.dram_tensor(f"in_{name}", a.shape, mybir.dt.from_np(a.dtype), kind="ExternalInput").ap()
    outs = {n: nc.dram_tensor(f"out_{n}", s, F32, kind="ExternalOutput").ap() for n, s in _OUTS.items()}
    build(nc, ins, outs)
    r = run_bass_kernel_spmd(nc, [arrays], core_ids=[0])
    return tuple(r.results[0][f"out_{n}"] for n in _OUTS)
```
